# Optimizing a Trainium2 kernel written in Bass

```python
import jax, jax.numpy as jnp
from jax import lax
import numpy as np

D_MODEL = 1024
BATCH = 1
SEQ = 256
DEPTH = 1

HEAD_DIM = 64
MOBA_HEADS = 8
MOBA_BLOCK = 256
MOBA_TOPK = 3
MOBA_Q_CHUNK = 16
SWA_Q_HEADS = 8
SWA_KV_HEADS = 2
SWA_WINDOW = 128
MEM_LEN = 256
XATTN_HEADS = 4
XATTN_HEAD_DIM = 128
N_GROUPS = 4
EXPERTS_PER_GROUP = 8
EXPERT_TOPK = 2
D_EXPERT = 256

RMS_EPS = 1e-6
NEG = -1e30

MOBA_WIDTH = MOBA_HEADS * HEAD_DIM
SWA_Q_WIDTH = SWA_Q_HEADS * HEAD_DIM
SWA_KV_WIDTH = SWA_KV_HEADS * HEAD_DIM
IN_SPLITS = (MOBA_WIDTH, MOBA_WIDTH, MOBA_WIDTH,
             SWA_Q_WIDTH, SWA_KV_WIDTH, SWA_KV_WIDTH,
             D_MODEL, D_MODEL)
IN_WIDTH = sum(IN_SPLITS)

kernel_name = "hybrid_moba_swa_gated_hiermoe"

def rmsnorm(x, g):
    xf = x.astype(jnp.float32)
    y = xf * lax.rsqrt(jnp.mean(xf * xf, axis=-1, keepdims=True) + RMS_EPS)
    return (y * g.astype(jnp.float32)).astype(x.dtype)

def alibi_slopes(n_heads):
    return jnp.asarray([2.0 ** (-8.0 * (i + 1) / n_heads) for i in range(n_heads)], dtype=jnp.float32)

def moba_attention(q, k, v, slopes):
    B, T, H, hd = q.shape
    nb = -(-T // MOBA_BLOCK)
    tp = nb * MOBA_BLOCK
    pad = tp - T
    q, k, v = [jnp.pad(a, ((0, 0), (0, pad), (0, 0), (0, 0))).transpose(0, 2, 1, 3) for a in (q, k, v)]
    kb = k.reshape(B, H, nb, MOBA_BLOCK, hd)
    vb = v.reshape(B, H, nb, MOBA_BLOCK, hd)
    kmean = jnp.mean(kb.astype(jnp.float32), axis=3)
    ksel = min(MOBA_TOPK, nb)
    n_chunks = tp // MOBA_Q_CHUNK
    qc = q.reshape(B, H, n_chunks, MOBA_Q_CHUNK, hd).transpose(2, 0, 1, 3, 4)
    scale = hd ** -0.5
    bi = jnp.arange(B)[:, None, None, None]
    hi = jnp.arange(H)[None, :, None, None]
    blk_ids = jnp.arange(nb)
    offs = jnp.arange(MOBA_BLOCK)

    def chunk(args):
        q_c, c = args
        t = c * MOBA_Q_CHUNK + jnp.arange(MOBA_Q_CHUNK)
        qblk = (c * MOBA_Q_CHUNK) // MOBA_BLOCK
        gate = jnp.einsum('bhqd,bhnd->bhqn', q_c.astype(jnp.float32), kmean)
        gate = jnp.where(blk_ids < qblk, gate, NEG)
        _, idx = lax.top_k(gate, ksel)
        valid = idx < qblk
        k_sel = kb[bi, hi, idx]
        v_sel = vb[bi, hi, idx]
        s_sel = jnp.einsum('bhqd,bhqksd->bhqks', q_c, k_sel, preferred_element_type=jnp.float32) * scale
        pos_sel = idx[..., None] * MOBA_BLOCK + offs
        dist_sel = (t[:, None, None] - pos_sel).astype(jnp.float32)
        s_sel = s_sel - slopes[:, None, None, None] * dist_sel
        s_sel = jnp.where(valid[..., None], s_sel, NEG)
        k_own = lax.dynamic_slice_in_dim(k, qblk * MOBA_BLOCK, MOBA_BLOCK, axis=2)
        v_own = lax.dynamic_slice_in_dim(v, qblk * MOBA_BLOCK, MOBA_BLOCK, axis=2)
        s_own = jnp.einsum('bhqd,bhsd->bhqs', q_c, k_own, preferred_element_type=jnp.float32) * scale
        dist_own = t[:, None] - (qblk * MOBA_BLOCK + offs)[None, :]
        s_own = s_own - slopes[:, None, None] * dist_own.astype(jnp.float32)
        s_own = jnp.where(dist_own >= 0, s_own, NEG)
        s = jnp.concatenate([s_sel.reshape(B, H, MOBA_Q_CHUNK, ksel * MOBA_BLOCK), s_own], axis=-1)
        p = jax.nn.softmax(s, axis=-1).astype(v.dtype)
        p_sel = p[..., :ksel * MOBA_BLOCK].reshape(B, H, MOBA_Q_CHUNK, ksel, MOBA_BLOCK)
        p_own = p[..., ksel * MOBA_BLOCK:]
        return (jnp.einsum('bhqks,bhqksd->bhqd', p_sel, v_sel)
                + jnp.einsum('bhqs,bhsd->bhqd', p_own, v_own))

    o = lax.map(chunk, (qc, jnp.arange(n_chunks)))
    o = o.transpose(1, 0, 3, 2, 4).reshape(B, tp, H * hd)
    return o[:, :T]

def swa_attention(q, k, v, sinks, slopes):
    B, T, HQ, hd = q.shape
    HKV = k.shape[2]
    G = HQ // HKV
    W = SWA_WINDOW
    nw = T // W
    qb = q.reshape(B, nw, W, HKV, G, hd)
    kb = k.reshape(B, nw, W, HKV, hd)
    vb = v.reshape(B, nw, W, HKV, hd)
    shift = lambda a: jnp.concatenate([jnp.zeros_like(a[:, :1]), a[:, :-1]], axis=1)
    kk = jnp.concatenate([shift(kb), kb], axis=2)
    vv = jnp.concatenate([shift(vb), vb], axis=2)
    s = jnp.einsum('bnqkgd,bnskd->bnkgqs', qb, kk, preferred_element_type=jnp.float32) * (hd ** -0.5)
    qi = jnp.arange(W)
    si = jnp.arange(2 * W)
    rel = qi[:, None] - si[None, :] + W
    s_abs = jnp.arange(nw)[:, None] * W - W + si[None, :]
    valid = ((rel >= 0) & (rel < W))[None] & (s_abs >= 0)[:, None, :]
    s = s - slopes.reshape(HKV, G)[:, :, None, None] * rel.astype(jnp.float32)
    s = jnp.where(valid[None, :, None, None], s, NEG)
    sink = jnp.broadcast_to(sinks.astype(jnp.float32).reshape(1, 1, HKV, G, 1, 1), s.shape[:-1] + (1,))
    p = jax.nn.softmax(jnp.concatenate([s, sink], axis=-1), axis=-1)[..., :2 * W].astype(v.dtype)
    o = jnp.einsum('bnkgqs,bnskd->bnqkgd', p, vv)
    return o.reshape(B, T, HQ * hd)

def cross_attention(h, memn, w_q, w_kv, w_o):
    B, T, _ = h.shape
    M = memn.shape[1]
    q = (h @ w_q).reshape(B, T, XATTN_HEADS, XATTN_HEAD_DIM)
    k, v = jnp.split((memn @ w_kv).reshape(B, M, 2 * XATTN_HEADS, XATTN_HEAD_DIM), 2, axis=2)
    s = jnp.einsum('bthd,bmhd->bhtm', q, k, preferred_element_type=jnp.float32) * (XATTN_HEAD_DIM ** -0.5)
    p = jax.nn.softmax(s, axis=-1).astype(v.dtype)
    o = jnp.einsum('bhtm,bmhd->bthd', p, v).reshape(B, T, XATTN_HEADS * XATTN_HEAD_DIM)
    return o @ w_o

def hier_moe(h, w_grp, b_grp, w_exp, b_exp, w_gate, w_up, w_down):
    B, T, D = h.shape
    n = B * T
    hf = h.reshape(n, D)
    g_prob = jax.nn.softmax((hf @ w_grp).astype(jnp.float32) + b_grp.astype(jnp.float32), axis=-1)
    g_p, g_idx = lax.top_k(g_prob, 1)
    e_logits = ((hf @ w_exp).astype(jnp.float32) + b_exp.astype(jnp.float32)).reshape(n, N_GROUPS, EXPERTS_PER_GROUP)
    e_logits = jnp.take_along_axis(e_logits, g_idx[:, :, None], axis=1)[:, 0]
    e_p, e_idx = lax.top_k(jax.nn.softmax(e_logits, axis=-1), EXPERT_TOPK)
    e_w = e_p / jnp.sum(e_p, axis=-1, keepdims=True) * g_p
    w_in_group = jnp.sum(jax.nn.one_hot(e_idx, EXPERTS_PER_GROUP, dtype=jnp.float32) * e_w[..., None], axis=1)
    combine = (jax.nn.one_hot(g_idx[:, 0], N_GROUPS, dtype=jnp.float32)[:, :, None]
               * w_in_group[:, None, :]).astype(h.dtype)
    out = jnp.zeros((n, D), h.dtype)
    for g in range(N_GROUPS):
        hid = (jax.nn.silu(jnp.einsum('nd,edf->nef', hf, w_gate[g]))
               * jnp.einsum('nd,edf->nef', hf, w_up[g]) * combine[:, g, :, None])
        out = out + jnp.einsum('nef,efd->nd', hid, w_down[g])
    return out.reshape(B, T, D)

def setup_inputs(seed: int = 0) -> dict:
    key = jax.random.key(seed)
    ks = jax.random.split(key, 24)
    L, D = DEPTH, D_MODEL
    f32 = jnp.float32
    nrm = lambda k, shape, fan_in: jax.random.normal(k, shape, f32) * (fan_in ** -0.5)
    gain = lambda k, shape: 1.0 + 0.02 * jax.random.normal(k, shape, f32)
    return {
        "x": jax.random.normal(ks[0], (BATCH, SEQ, D), f32),
        "mem": jax.random.normal(ks[1], (BATCH, MEM_LEN, D), f32),
        "mix_norm_g": gain(ks[2], (L, D)),
        "w_in": nrm(ks[3], (L, D, IN_WIDTH), D),
        "moba_out_w": nrm(ks[4], (L, MOBA_WIDTH, D), MOBA_WIDTH),
        "swa_out_w": nrm(ks[5], (L, SWA_Q_WIDTH, D), SWA_Q_WIDTH),
        "swa_sinks": 0.5 * jax.random.normal(ks[6], (L, SWA_Q_HEADS), f32),
        "mix_out_w": nrm(ks[7], (L, D, D), D),
        "xattn_norm_g": gain(ks[8], (L, D)),
        "mem_norm_g": gain(ks[9], (L, D)),
        "xattn_wq": nrm(ks[10], (L, D, XATTN_HEADS * XATTN_HEAD_DIM), D),
        "xattn_wkv": nrm(ks[11], (L, D, 2 * XATTN_HEADS * XATTN_HEAD_DIM), D),
        "xattn_wo": nrm(ks[12], (L, XATTN_HEADS * XATTN_HEAD_DIM, D), XATTN_HEADS * XATTN_HEAD_DIM),
        "ffn_norm_g": gain(ks[13], (L, D)),
        "router_group_w": nrm(ks[14], (L, D, N_GROUPS), D),
        "router_group_b": 0.01 * jax.random.normal(ks[15], (L, N_GROUPS), f32),
        "router_expert_w": nrm(ks[16], (L, D, N_GROUPS * EXPERTS_PER_GROUP), D),
        "router_expert_b": 0.01 * jax.random.normal(ks[17], (L, N_GROUPS * EXPERTS_PER_GROUP), f32),
        "expert_w_gate": nrm(ks[18], (L, N_GROUPS, EXPERTS_PER_GROUP, D, D_EXPERT), D),
        "expert_w_up": nrm(ks[19], (L, N_GROUPS, EXPERTS_PER_GROUP, D, D_EXPERT), D),
        "expert_w_down": nrm(ks[20], (L, N_GROUPS, EXPERTS_PER_GROUP, D_EXPERT, D), D_EXPERT),
        "final_norm_g": gain(ks[21], (D,)),
    }

def reference(x, mem, mix_norm_g, w_in, moba_out_w, swa_out_w, swa_sinks, mix_out_w,
              xattn_norm_g, mem_norm_g, xattn_wq, xattn_wkv, xattn_wo, ffn_norm_g,
              router_group_w, router_group_b, router_expert_w, router_expert_b,
              expert_w_gate, expert_w_up, expert_w_down, final_norm_g):
    B, T, _ = x.shape
    split_at = [int(v) for v in np.cumsum(IN_SPLITS)[:-1]]
    moba_slopes = alibi_slopes(MOBA_HEADS)
    swa_slopes = alibi_slopes(SWA_Q_HEADS)
    for l in range(DEPTH):
        h = rmsnorm(x, mix_norm_g[l])
        q_a, k_a, v_a, q_b, k_b, v_b, g_a, g_b = jnp.split(h @ w_in[l], split_at, axis=-1)
        a = moba_attention(q_a.reshape(B, T, MOBA_HEADS, HEAD_DIM),
                           k_a.reshape(B, T, MOBA_HEADS, HEAD_DIM),
                           v_a.reshape(B, T, MOBA_HEADS, HEAD_DIM), moba_slopes)
        b = swa_attention(q_b.reshape(B, T, SWA_Q_HEADS, HEAD_DIM),
                          k_b.reshape(B, T, SWA_KV_HEADS, HEAD_DIM),
                          v_b.reshape(B, T, SWA_KV_HEADS, HEAD_DIM), swa_sinks[l], swa_slopes)
        merged = jax.nn.sigmoid(g_a) * (a @ moba_out_w[l]) + jax.nn.sigmoid(g_b) * (b @ swa_out_w[l])
        x = x + merged @ mix_out_w[l]
        x = x + cross_attention(rmsnorm(x, xattn_norm_g[l]), rmsnorm(mem, mem_norm_g[l]),
                                xattn_wq[l], xattn_wkv[l], xattn_wo[l])
        x = x + hier_moe(rmsnorm(x, ffn_norm_g[l]), router_group_w[l], router_group_b[l],
                         router_expert_w[l], router_expert_b[l],
                         expert_w_gate[l], expert_w_up[l], expert_w_down[l])
    return rmsnorm(x, final_norm_g)


_drawn_inputs = setup_inputs


def setup_inputs(seed=0):
    import zlib

    import numpy as np

    out = dict(_drawn_inputs(seed))
    spreads = {}
    factors = {'xattn_norm_g': 8.0,
     'mem_norm_g': 8.0,
     'router_group_b': 200.0,
     'router_expert_b': 42.488,
     'final_norm_g': 20.814,
     'ffn_norm_g': 8.0}
    for name, (base, spread) in spreads.items():
        noise = np.random.default_rng([zlib.crc32(name.encode()), seed]).standard_normal(out[name].shape)
        drawn = base * np.exp(spread * noise) if base else spread * noise
        out[name] = __import__('jax').numpy.asarray(drawn.astype(out[name].dtype))
    for name, factor in factors.items():
        out[name] = (out[name] * factor).astype(out[name].dtype)
    return out
```

```python
from contextlib import ExitStack

import concourse.bass as bass
from concourse import mybir

P = 128


def hybrid_layer(nc, x, mem, mix_norm_g, w_in, moba_out_w, swa_out_w, swa_sinks, mix_out_w, xattn_norm_g,
                 mem_norm_g, xattn_wq, xattn_wkv, xattn_wo, ffn_norm_g, router_group_w, router_group_b,
                 router_expert_w, router_expert_b, expert_w_gate, expert_w_up, expert_w_down,
                 final_norm_g, out):
    F32, F32R = mybir.dt.float32, mybir.dt.float32r
    I32, U32 = mybir.dt.int32, mybir.dt.uint32
    ALU, ACT, AX = mybir.AluOpType, mybir.ActivationFunctionType, mybir.AxisListType

    T, D = x.shape[1], x.shape[2]
    TT, KD = T // P, D // P
    HD, HEADS, WINDOW = 64, 8, 128
    PAIRS = HEADS // 2
    XH = 4
    XSCALE = float(P) ** -0.5
    NG, EPG = expert_w_gate.shape[1], expert_w_gate.shape[2]
    NE, FE = NG * EPG, expert_w_gate.shape[4]
    KF = FE // P
    WIN = 32
    QE = P // WIN
    QUADS = NE // QE
    ROUNDS = T // WIN
    EPS, NEG, BIG = 1e-6, -1e30, -3e38
    CW = 256
    HK = 4
    SK = T + WINDOW

    win = w_in[0].rearrange("(k p) n -> p k n", p=P)
    wkv = xattn_wkv[0].rearrange("(k p) n -> p k n", p=P)
    wq = xattn_wq[0].rearrange("(k p) n -> p k n", p=P)
    wmix = mix_out_w[0].rearrange("(k p) n -> p k n", p=P)
    wa = moba_out_w[0].rearrange("(k p) n -> p k n", p=P)
    wb = swa_out_w[0].rearrange("(k p) n -> p k n", p=P)
    wo = xattn_wo[0].rearrange("(k p) n -> p k n", p=P)

    def both_halves(w, col):
        return [w[:, h * HK:(h + 1) * HK, col:col + CW] for h in range(2)]

    halves, kinds = [], []
    for c in range(17):
        kinds.append(["qa", "qa", "ka", "ka", "va", "va", "qb", "qb", "kvb"][c] if c < 9 else "gate")
        halves += both_halves(win, c * CW)
    for m in range(4):
        kinds.append("merge")
        halves += [wa[:, :, m * CW:(m + 1) * CW], wb[:, :, m * CW:(m + 1) * CW]]
    for m in range(4):
        kinds.append("mix")
        halves += both_halves(wmix, m * CW)
    for name, w, col in (("kx", wkv, 0), ("kx", wkv, CW), ("qx", wq, 0), ("qx", wq, CW),
                         ("vx", wkv, 2 * CW), ("vx", wkv, 3 * CW)):
        kinds.append(name)
        halves += both_halves(w, col)
    for m in range(2):
        kinds.append("xo")
        halves += [wo[:, :, (2 * m + h) * CW:(2 * m + h + 1) * CW] for h in range(2)]
    NC, NH = len(kinds), len(halves)
    at = {k: kinds.index(k) for k in kinds}
    ON_DVE = {"merge": 1, "mix": 1, "xo": 2}

    def evac_count(c):
        if kinds[c] in ON_DVE:
            return sum(ON_DVE.get(k, 0) for k in kinds[:c + 1])
        return sum(k not in ON_DVE for k in kinds[:c + 1])

    NW, NS = 3, 2

    GU_CHUNKS, MOE_CHUNKS = KD, KD + KF * 2
    wg_v = expert_w_gate[0].rearrange("g e (k p) f -> k p (g e) f", p=P)
    wu_v = expert_w_up[0].rearrange("g e (k p) f -> k p (g e) f", p=P)
    wd_v = expert_w_down[0].rearrange("g e (k p) d -> k p (g e) d", p=P)

    ctx = ExitStack()
    with ctx:
        place = [(nc.sbuf_base + 63) // 64 * 64]

        def region(nbytes):
            place[0] += nbytes
            assert place[0] <= nc.sbuf_usable_end
            return place[0] - nbytes

        def sb(name, shape, dt, offset=None):
            n = 4
            for s in shape[1:]:
                n *= s
            offset = region((n + 31) // 32 * 32) if offset is None else offset
            return nc.alloc_sbuf_tensor_at(name, shape, dt, offset=offset)

        slot_at = [region(8192) for _ in range(MOE_CHUNKS)]
        slots = [sb(f"moe_slot{s}", [P, 2048], F32, slot_at[s]) for s in range(MOE_CHUNKS)]
        mem_raw = sb("mem_raw", [P, TT, D], F32, slot_at[9])
        mixT_hi = sb("mixT_hi", [P, 2 * PAIRS, T], F32R, slot_at[10])
        mixT_lo = sb("mixT_lo", [P, 2 * PAIRS, T], F32R, slot_at[11])
        w_at = region(NW * HK * CW * 4)
        w_raw = sb("w_raw", [P, NW, HK, CW], F32, w_at)
        fin_row = sb("fin_row", [1, D], F32, w_at)
        fin_g = sb("fin_g", [P, D], F32, w_at + 4096)
        w_hi = sb("w_hi", [P, NS, HK, CW], F32R)
        w_lo = sb("w_lo", [P, NS, HK, CW], F32R)
        xres = sb("xres", [P, TT, D], F32)
        xn = sb("xn", [P, TT, D], F32)
        r1 = region(16384)
        hT_hi = sb("hT_hi", [P, KD, T], F32R, r1)
        hT_lo = sb("hT_lo", [P, KD, T], F32R, r1 + 8192)
        mgT_hi = sb("mgT_hi", [P, KD, T], F32R, r1)
        mgT_lo = sb("mgT_lo", [P, KD, T], F32R, r1 + 8192)
        h2T_hi = sb("h2T_hi", [P, KD, T], F32R, r1)
        h2T_lo = sb("h2T_lo", [P, KD, T], F32R, r1 + 8192)
        oxT_hi = sb("oxT_hi", [P, XH, T], F32R, r1)
        oxT_lo = sb("oxT_lo", [P, XH, T], F32R, r1 + 8192)
        r2 = region(16384 + 2048 + 1024)
        qa = sb("qa", [P, PAIRS, T], F32, r2)
        ka = sb("ka", [P, PAIRS, T], F32, r2 + 4096)
        va = sb("va", [P, TT, HEADS * HD], F32, r2 + 8192)
        qb = sb("qb", [P, PAIRS, T], F32, r2 + 12288)
        kb2 = sb("kb2", [P, 2, T], F32, r2 + 16384)
        vb = sb("vb", [P, TT, P], F32, r2 + 18432)
        memT_hi = sb("memT_hi", [P, KD, T], F32R, r2)
        memT_lo = sb("memT_lo", [P, KD, T], F32R, r2 + 8192)
        h3T = sb("h3T", [P, KD, T], F32, r2)
        r3 = region(16384)
        gates = sb("gates", [P, 2 * KD, T], F32, r3)
        qx = sb("qx", [P, XH, T], F32, r3)
        kx = sb("kx", [P, XH, T], F32, r3 + 4096)
        vx = sb("vx", [P, TT, XH * P], F32, r3 + 8192)
        xpT = sb("xpT", [P, 2, 2 * T], F32, r3 + 12288)
        sc_at = region(6144 + 3072)
        scores = sb("scores", [P, 2, 2, SK], F32, sc_at)
        probT = sb("probT", [P, 2, SK], F32, sc_at + 6144)
        nt_tmp = sb("nt_tmp", [P, 2, 512], F32, sc_at)
        g_rows = sb("g_rows", [4 * KD, P], F32, sc_at + 6144)
        xprob = sb("xprob", [P, XH, TT, T], F32, sc_at)
        moe_x = sb("moe_x", [P, KD, P], F32, r1)
        sel = sb("sel", [P, TT, QE, WIN], F32, r1 + 4096)
        selw = sb("selw", [P, TT, QE, WIN], F32, r1 + 5120)
        selwT = sb("selwT", [P, T], F32, r1 + 6144)
        silu_g = sb("silu_g", [P, FE], F32, r1 + 7168)
        hid = sb("hid", [P, FE], F32, r1 + 8192)
        hidT = sb("hidT", [P, KF, P], F32, r1 + 9216)
        y_sb = sb("y_sb", [P, D], F32, r1 + 10240)
        slot_of = sb("slot_of", [P, TT, ROUNDS, NE], F32, r3)
        weight_of = sb("weight_of", [P, TT, ROUNDS, NE], F32, r3 + 2048)
        rt = r3 + 4096

        def small(name, shape, dt=F32):
            nonlocal rt
            n = 4
            for s in shape[1:]:
                n *= s
            rt += (n + 31) // 32 * 32
            return nc.alloc_sbuf_tensor_at(name, shape, dt, offset=rt - (n + 31) // 32 * 32)

        g_log = small("g_log", [P, TT, 8])
        g_top, e_top = small("g_top", [P, TT, 8]), small("e_top", [P, TT, 8])
        g_idx, e_idx = small("g_idx", [P, TT, 8], U32), small("e_idx", [P, TT, 8], U32)
        g_idf, e_idf = small("g_idf", [P, TT, 8]), small("e_idf", [P, TT, 8])
        g_exp, g_sum, g_neg = small("g_exp", [P, TT, 4]), small("g_sum", [P, TT]), small("g_neg", [P, TT])
        pen, e_log = small("pen", [P, TT, NG]), small("e_log", [P, TT, NG, EPG])
        e_neg, e2 = small("e_neg", [P, TT]), small("e2", [P, TT])
        den, ew = small("den", [P, TT]), small("ew", [P, 2, TT])
        first, both = small("first", [P, TT, NE]), small("both", [P, TT, NE])
        wfirst, wboth = small("wfirst", [P, TT, NE]), small("wboth", [P, TT, NE])
        posm = small("posm", [P, TT, NE])
        cmax, over, nover = small("cmax", [P, 1]), small("over", [P, 8]), small("nover", [P, 1])
        trips = small("trips", [P, 1], I32)
        ident = sb("ident", [P, P], F32)
        below = sb("below", [P, P], F32)
        ones = sb("ones", [P, P], F32)
        gains = sb("gains", [P, 4, KD], F32)
        dist = sb("dist", [P, 2, SK], F32)
        wr = sb("wr", [P, KD, NG + NE], F32)
        br = sb("br", [1, NG + NE], F32)
        sink_row = sb("sink_row", [1, HEADS], F32)
        sinks, nsinks = sb("sinks", [P, HEADS], F32), sb("nsinks", [P, HEADS], F32)
        iota_e = sb("iota_e", [P, NE], F32)
        iota_rw = sb("iota_rw", [P, ROUNDS], F32)
        sumsq, mean_eps, rnorm = (sb(n, [P, 4 + 1, TT], F32) for n in ("sumsq", "mean_eps", "rnorm"))
        mhalf = sb("mhalf", [P, TT], F32)
        nmax = sb("nmax", [P, 2, 2, 2], F32)
        rsum, rinv = sb("rsum", [P, 2, 4], F32), sb("rinv", [P, 2, 4], F32)
        sink_arg, sink_exp = sb("sink_arg", [P, 2, 4], F32), sb("sink_exp", [P, 2, 4], F32)
        xmax, xnmax = sb("xmax", [P, XH, TT], F32), sb("xnmax", [P, XH, TT], F32)
        xsum, xinv = sb("xsum", [P, XH, TT], F32), sb("xinv", [P, XH, TT], F32)

        PJ, SC, PT, PO = ([ctx.enter_context(nc.psum_tensor(f"{n}{i}", [P, 512], F32)) for i in range(2)]
                          for n in ("proj", "score", "probt", "attno"))

        LOGIT, LISTED, COUNTS = (PO[0], PT[0]), (PO[1], PT[1]), PJ[1]

        def sem(name):
            return ctx.enter_context(nc.semaphore(name))

        x_in, mem_in, gain_in, small_in, fin_in = (sem(n) for n in ("x_in", "mem_in", "gain_in", "small_in", "fin_in"))
        w_in_sem = [sem(f"w_loaded{i}") for i in range(NW)]
        moe_in = [sem(f"moe_loaded{i}") for i in range(MOE_CHUNKS)]
        c_ident, c_ones, c_misc, c_gain, c_sink_ps, c_sink = (
            sem(n) for n in ("c_ident", "c_ones", "c_misc", "c_gain", "c_sink_ps", "c_sink"))
        c_gain_ps = sem("c_gain_ps")
        hi_done, lo_done, half_done, ev_act, ev_dve = (
            sem(n) for n in ("hi_done", "lo_done", "half_done", "ev_act", "ev_dve"))
        sq_done, ms_done, rs_done, xn_done = (sem(n) for n in ("sq_done", "ms_done", "rs_done", "xn_done"))
        nt_ps, nt_gain, nt_hi, nt_lo = (sem(n) for n in ("nt_ps", "nt_gain", "nt_hi", "nt_lo"))
        s_ps, s_bias, s_max, s_exp, s_inv, s_norm, pt_ps, pt_sb, pv_ps, mix_hi, mix_lo = (
            sem(n) for n in ("s_ps", "s_bias", "s_max", "s_exp", "s_inv", "s_norm", "pt_ps", "pt_sb", "pv_ps",
                             "mix_hi", "mix_lo"))
        sig_done, mg_part, mg_sum, mg_hi, mg_lo = (
            sem(n) for n in ("sig_done", "mg_part", "mg_sum", "mg_hi", "mg_lo"))
        xs_ps, xs_max, xs_exp, xs_inv, xs_norm, xpt_ps, xpt_sb, xpv_ps, ox_hi, ox_lo = (
            sem(n) for n in ("xs_ps", "xs_max", "xs_exp", "xs_inv", "xs_norm", "xpt_ps", "xpt_sb", "xpv_ps",
                             "ox_hi", "ox_lo"))
        logits_ps, r_step, r_top, r_exp, r_mask, pos_ps, trips_set, fin_ps, fin_sb = (
            sem(n) for n in ("logits_ps", "r_step", "r_top", "r_exp", "r_mask", "pos_ps", "trips_set", "fin_ps",
                             "fin_sb"))
        sel_made, gather_ps, moe_x_sb, selT_ps, selT_sb, chunk_used, silu_done, hid_done = (
            sem(n) for n in ("sel_made", "gather_ps", "moe_x_sb", "selT_ps", "selT_sb", "chunk_used",
                             "silu_done", "hid_done"))
        hidT_ps, hidT_sb, y_act, y_dve, back_ps, added = (
            sem(n) for n in ("hidT_ps", "hidT_sb", "y_act", "y_dve", "back_ps", "added"))
        out_done = sem("out_done")

        block = ctx.enter_context(nc.Block())

        MEM_NORM, X2_NORM, X3_NORM = 1, 2, 3
        STEPS = HEADS + 3
        FIRST_UNDER = 6
        UNITS = 2 * PAIRS

        def s_max_count(j):
            return 2 * min(j + 1, PAIRS) + 4 * max(j + 1 - PAIRS, 0)

        def s_exp_count(j):
            return 4 * min(j + 1, PAIRS) + 5 * max(j + 1 - PAIRS, 0)

        @block.sync
        def _(sp):
            sp.dma_start(xres[:], x[0].rearrange("(t p) d -> p t d", p=P)).then_inc(x_in, 16)

            def load_half(g):
                if g >= NW:
                    sp.wait_ge(lo_done, g - NW + 1)
                sp.dma_start(w_raw[:, g % NW], halves[g]).then_inc(w_in_sem[g % NW], 16)

            def load_experts(c, quad):
                e0 = quad * QE
                if c < GU_CHUNKS:
                    dst = slots[c][:].rearrange("p (e j f) -> p e j f", e=QE, j=2)
                    sp.dma_start(dst[:, :, 0], wg_v[c, :, bass.ds(e0, QE), :]).then_inc(moe_in[c], 16)
                    sp.dma_start(dst[:, :, 1], wu_v[c, :, bass.ds(e0, QE), :]).then_inc(moe_in[c], 16)
                else:
                    kt, pair = divmod(c - GU_CHUNKS, 2)
                    dst = slots[c][:].rearrange("p (e d) -> p e d", e=2)
                    for e in range(2):
                        sp.dma_start(dst[:, e:e + 1], wd_v[kt, :, bass.ds(e0 + 2 * pair + e, 1), :])\
                            .then_inc(moe_in[c], 16)

            for g in range(NW):
                load_half(g)
            sp.dma_start(mem_raw[:], mem[0].rearrange("(t p) d -> p t d", p=P)).then_inc(mem_in, 16)
            prefetched = 0
            for g in range(NW, NH):
                load_half(g)
                if g >= 12 and g % 3 == 0 and prefetched < 9:
                    load_experts(prefetched, 0)
                    prefetched += 1
                if prefetched == 9 and g >= 2 * at["mix"] + 1 and prefetched < MOE_CHUNKS:
                    sp.wait_ge(xn_done, 2 * (MEM_NORM + 1))
                    load_experts(9, 0)
                    sp.wait_ge(half_done, 2 * at["mix"])
                    load_experts(10, 0)
                    load_experts(11, 0)
                    prefetched = MOE_CHUNKS
            assert prefetched == MOE_CHUNKS
            sp.wait_ge(lo_done, NH)
            sp.dma_start(fin_row[:], final_norm_g.rearrange("(a n) -> a n", a=1)).then_inc(fin_in, 16)
            sp.wait_ge(trips_set, 1)
            total = sp.value_load(trips[0:1, 0:1], min_val=QUADS, max_val=QUADS * ROUNDS)
            with sp.Fori(1, total) as it:
                for c in range(MOE_CHUNKS):
                    sp.wait_ge(chunk_used, (it - 1) * MOE_CHUNKS + c + 1)
                    load_experts(c, it % QUADS)
            for t in range(TT):
                sp.wait_ge(xn_done, 2 * 4 + t + 1)
                sp.dma_start(out[0, t * P:(t + 1) * P, :], xn[:, t]).then_inc(out_done, 16)
            sp.wait_ge(out_done, 16 * TT)

        @block.gpsimd
        def _(pool):
            pool.memset(ident[:], 0.0).then_inc(c_misc, 1)
            pool.memset(ones[:], 1.0).then_inc(c_ones, 1)
            pool.wait_ge(c_misc, 1)
            pool.affine_select(out=ident[:], in_=ident[:], compare_op=ALU.not_equal, fill=1.0, base=0,
                               pattern=[[-1, P]], channel_multiplier=1).then_inc(c_ident, 1)
            pool.memset(mhalf[:], -0.5).then_inc(c_misc, 1)
            for kind in range(2):
                pool.iota(dist[:, kind, 0:P], [[1, P]], base=0, channel_multiplier=-1,
                          allow_small_or_imprecise_dtypes=True).then_inc(c_misc, 1)
                pool.iota(dist[:, kind, P:SK], [[1, T]], base=-P, channel_multiplier=-1,
                          allow_small_or_imprecise_dtypes=True).then_inc(c_misc, 1)
            pool.wait_ge(c_misc, 6)
            for kind in range(2):
                pool.affine_select(out=dist[:, kind, 0:P], in_=dist[:, kind, 0:P], compare_op=ALU.is_ge,
                                   fill=NEG, base=0, pattern=[[-1, P]], channel_multiplier=1).then_inc(c_misc, 1)
                pool.affine_select(out=dist[:, kind, P:SK], in_=dist[:, kind, P:SK], compare_op=ALU.is_ge,
                                   fill=NEG, base=P, pattern=[[-1, T]], channel_multiplier=1).then_inc(c_misc, 1)
            pool.wait_ge(c_misc, 10)
            pool.affine_select(out=dist[:, 1, P:SK], in_=dist[:, 1, P:SK], compare_op=ALU.is_gt, fill=NEG,
                               base=WINDOW - P, pattern=[[1, T]], channel_multiplier=-1).then_inc(c_misc, 1)
            pool.iota(iota_e[:], [[1, NE]], base=0, channel_multiplier=0,
                      allow_small_or_imprecise_dtypes=True).then_inc(c_misc, 1)
            pool.iota(iota_rw[:], [[WIN, ROUNDS]], base=0, channel_multiplier=0,
                      allow_small_or_imprecise_dtypes=True).then_inc(c_misc, 1)
            pool.wait_ge(c_ones, 1)
            pool.affine_select(out=below[:], in_=ones[:], compare_op=ALU.is_gt, fill=0.0, base=0,
                               pattern=[[1, P]], channel_multiplier=-1).then_inc(c_misc, 1)

            def inverse_root(n):
                pool.wait_ge(ms_done, n + 1)
                pool.tensor_tensor(rnorm[:, n], mean_eps[:, n], mhalf[:], ALU.pow).then_inc(rs_done, 1)

            inverse_root(0)
            inverse_root(MEM_NORM)
            for j in range(UNITS):
                pool.wait_ge(s_inv, j + 1)
                for tt in range(TT):
                    cols = slice(0, P) if tt == 0 else slice(P, SK)
                    for hh in range(2):
                        i = 2 * tt + hh
                        pool.tensor_scalar(scores[:, j % 2, hh, cols], scores[:, j % 2, hh, cols],
                                           rinv[:, j % 2, i:i + 1], 1.0, ALU.mult, ALU.mult).then_inc(s_norm, 1)
            inverse_root(X2_NORM)
            for h in range(XH):
                pool.wait_ge(xs_inv, h + 1)
                for tt in range(TT):
                    pool.tensor_scalar(xprob[:, h, tt], xprob[:, h, tt], xinv[:, h, tt:tt + 1], 1.0,
                                       ALU.mult, ALU.mult).then_inc(xs_norm, 1)
            inverse_root(X3_NORM)
            inverse_root(4)

        @block.scalar
        def _(act):
            for i, g in enumerate((mix_norm_g, mem_norm_g, xattn_norm_g, ffn_norm_g)):
                act.dma_start(g_rows[i * KD:(i + 1) * KD, :], g[0].rearrange("(k p) -> k p", p=P)).then_inc(gain_in, 16)
            act.dma_start(sink_row[:], swa_sinks).then_inc(small_in, 16)
            act.dma_start(br[:, 0:NG], router_group_b).then_inc(small_in, 16)
            act.dma_start(br[:, NG:NG + NE], router_expert_b).then_inc(small_in, 16)
            act.dma_start(wr[:, :, 0:NG], router_group_w[0].rearrange("(k p) n -> p k n", p=P)).then_inc(small_in, 16)
            act.dma_start(wr[:, :, NG:NG + NE], router_expert_w[0].rearrange("(k p) n -> p k n", p=P))\
                .then_inc(small_in, 16)

            def squares(n, src):
                for t in range(TT):
                    act.activation(xn[:, t], src[:, t], ACT.Square, accum_out=sumsq[:, n, t:t + 1]).then_inc(sq_done, 1)

            def transposed_hi(n, hi):
                for u in range(4):
                    t, half = divmod(u, 2)
                    act.wait_ge(nt_gain, 4 * n + u + 1)
                    act.activation(hi[:, half * 4:half * 4 + 4, t * P:(t + 1) * P],
                                   nt_tmp[:, u % 2].rearrange("p (k q) -> p k q", k=4), ACT.Copy).then_inc(nt_hi, 1)

            def split_hi(g):
                if g >= NH:
                    return
                act.wait_ge(w_in_sem[g % NW], 16 * (g // NW + 1))
                if g >= NS:
                    act.wait_ge(half_done, g - NS + 1)
                act.activation(w_hi[:, g % NS], w_raw[:, g % NW], ACT.Copy).then_inc(hi_done, 1)

            def evacuate(c):
                k, i, src = kinds[c], c - at[kinds[c]], PJ[c % 2]
                two = src[:].rearrange("p (a n) -> p a n", a=2)
                act.wait_ge(half_done, 2 * c + 2)
                if k == "qa":
                    op = act.activation(qa[:, 2 * i:2 * i + 2], two, ACT.Copy, scale=float(HD) ** -0.5)
                elif k == "qb":
                    op = act.activation(qb[:, 2 * i:2 * i + 2], two, ACT.Copy, scale=float(HD) ** -0.5)
                elif k == "ka":
                    op = act.activation(ka[:, 2 * i:2 * i + 2], two, ACT.Copy)
                elif k == "va":
                    op = act.activation(va[:, :, i * CW:(i + 1) * CW], two, ACT.Copy)
                elif k == "kvb":
                    for g in range(2):
                        for half in range(2):
                            act.activation(kb2[half * HD:(half + 1) * HD, g], src[g * HD:(g + 1) * HD, 0:T], ACT.Copy)
                    op = act.activation(vb[:], src[:, T:2 * T].rearrange("p (t d) -> p t d", t=TT), ACT.Copy)
                elif k == "gate":
                    op = act.activation(gates[:, 2 * i:2 * i + 2], two, ACT.Copy)
                elif k == "kx":
                    op = act.activation(kx[:, 2 * i:2 * i + 2], two, ACT.Copy)
                elif k == "qx":
                    op = act.activation(qx[:, 2 * i:2 * i + 2], two, ACT.Copy)
                else:
                    op = act.activation(vx[:, :, i * CW:(i + 1) * CW], two, ACT.Copy)
                op.then_inc(ev_act, 1)

            def exponentials(j):
                b = j % 2
                act.wait_ge(s_max, s_max_count(j))
                for tt in range(TT):
                    cols = slice(0, P) if tt == 0 else slice(P, SK)
                    for hh in range(2):
                        i = 2 * tt + hh
                        act.activation(scores[:, b, hh, cols], scores[:, b, hh, cols], ACT.Exp,
                                       bias=nmax[:, b, tt, hh:hh + 1], accum_out=rsum[:, b, i:i + 1]).then_inc(s_exp, 1)
                if j >= PAIRS:
                    act.activation(sink_exp[:, b], sink_arg[:, b], ACT.Exp).then_inc(s_exp, 1)

            def prob_out(j):
                act.wait_ge(pt_ps, j + 1)
                if j:
                    act.wait_ge(pv_ps, j)
                for hh in range(2):
                    act.activation(probT[:, hh], PT[hh][:, 0:SK], ACT.Copy).then_inc(pt_sb, 1)

            def mix_out_hi(j):
                act.wait_ge(pv_ps, j + 1)
                act.activation(mixT_hi[:, j], PO[j % 2][:, 0:T], ACT.Copy).then_inc(mix_hi, 1)

            act.wait_ge(x_in, 16)
            squares(0, xres)
            split_hi(0)
            transposed_hi(0, hT_hi)
            split_hi(1)
            for c in range(FIRST_UNDER):
                split_hi(2 * c + 2)
                split_hi(2 * c + 3)
                evacuate(c)
                if c == 0:
                    act.wait_ge(mem_in, 16)
                    act.wait_ge(nt_ps, 4)
                    squares(MEM_NORM, mem_raw)
            for i in range(STEPS):
                c = FIRST_UNDER + i
                split_hi(2 * c + 2)
                if i < UNITS:
                    exponentials(i)
                split_hi(2 * c + 3)
                evacuate(c)
                if 1 <= i <= UNITS:
                    prob_out(i - 1)
                if 2 <= i <= UNITS + 1:
                    mix_out_hi(i - 2)
            act.wait_ge(ev_act, evac_count(at["merge"] - 1))
            for half in range(2):
                act.activation(gates[:, half * KD:(half + 1) * KD], gates[:, half * KD:(half + 1) * KD],
                               ACT.Sigmoid).then_inc(sig_done, 1)
            transposed_hi(MEM_NORM, memT_hi)
            for c in range(at["merge"], at["mix"]):
                split_hi(2 * c + 2)
                split_hi(2 * c + 3)
                m = c - at["merge"]
                act.wait_ge(mg_sum, m + 1)
                act.activation(mgT_hi[:, 2 * m:2 * m + 2], gates[:, 2 * m:2 * m + 2], ACT.Copy).then_inc(mg_hi, 1)
            for c in range(at["mix"], at["kx"]):
                split_hi(2 * c + 2)
                split_hi(2 * c + 3)
            act.wait_ge(ev_dve, evac_count(at["kx"] - 1))
            squares(X2_NORM, xres)
            for c in range(at["kx"], at["kx"] + 2):
                split_hi(2 * c + 2)
                split_hi(2 * c + 3)
                evacuate(c)
            transposed_hi(X2_NORM, h2T_hi)
            for c in range(at["qx"], at["qx"] + 2):
                split_hi(2 * c + 2)
                split_hi(2 * c + 3)
                evacuate(c)

            def xexponentials(h):
                act.wait_ge(xs_max, 2 * h + 2)
                for tt in range(TT):
                    act.activation(xprob[:, h, tt], SC[h % 2][:, tt * T:(tt + 1) * T], ACT.Exp, scale=XSCALE,
                                   bias=xnmax[:, h, tt:tt + 1], accum_out=xsum[:, h, tt:tt + 1]).then_inc(xs_exp, 1)

            for i in range(2):
                xexponentials(2 * i)
                xexponentials(2 * i + 1)
                c = at["vx"] + i
                split_hi(2 * c + 2)
                split_hi(2 * c + 3)
                evacuate(c)
            for h in range(XH):
                act.wait_ge(xpt_ps, h + 1)
                if h >= 2:
                    act.wait_ge(xpv_ps, h - 1)
                act.activation(xpT[:, h % 2], PT[h % 2][:], ACT.Copy).then_inc(xpt_sb, 1)
                if h:
                    act.wait_ge(xpv_ps, h)
                    act.activation(oxT_hi[:, h - 1], PO[(h - 1) % 2][:, 0:T], ACT.Copy).then_inc(ox_hi, 1)
            act.wait_ge(xpv_ps, XH)
            act.activation(oxT_hi[:, XH - 1], PO[(XH - 1) % 2][:, 0:T], ACT.Copy).then_inc(ox_hi, 1)
            split_hi(2 * at["xo"] + 2)
            split_hi(2 * at["xo"] + 3)
            act.wait_ge(ev_dve, evac_count(NC - 1))
            squares(X3_NORM, xres)

            for t in range(TT):
                act.wait_ge(r_top, 2 * t + 1)
                act.activation(g_exp[:, t], g_log[:, t, 0:NG], ACT.Exp, bias=g_neg[:, t:t + 1],
                               accum_out=g_sum[:, t:t + 1]).then_inc(r_exp, 1)
                act.wait_ge(r_top, 2 * t + 2)
                act.activation(e2[:, t:t + 1], e_top[:, t, 1:2], ACT.Exp, bias=e_neg[:, t:t + 1]).then_inc(r_exp, 1)
            act.wait_ge(fin_ps, 1)
            for half in range(2):
                act.activation(fin_g[:, half * 512:(half + 1) * 512], SC[half][:], ACT.Copy).then_inc(fin_sb, 1)

            act.wait_ge(trips_set, 1)
            total = act.value_load(trips[0:1, 0:1], min_val=QUADS, max_val=QUADS * ROUNDS)
            with act.Fori(0, total) as it:
                act.wait_ge(selT_ps, it + 1)
                act.activation(selwT[:], PT[1][:, 0:T], ACT.Copy).then_inc(selT_sb, 1)
                act.wait_ge(chunk_used, it * MOE_CHUNKS + GU_CHUNKS)
                act.activation(silu_g[:], PJ[0][:, 0:FE], ACT.Silu).then_inc(silu_done, 1)
                act.wait_ge(hidT_ps, it + 1)
                act.activation(hidT[:], PT[0][:, 0:KF * P].rearrange("p (k s) -> p k s", k=KF), ACT.Copy)\
                    .then_inc(hidT_sb, 1)
                act.wait_ge(chunk_used, it * MOE_CHUNKS + MOE_CHUNKS)
                act.activation(y_sb[:, 0:512], SC[0][:], ACT.Copy).then_inc(y_act, 1)
            act.wait_ge(added, total * 4)
            squares(4, xres)

        @block.vector
        def _(dve):
            def normalise(n, src):
                dve.wait_ge(sq_done, 2 * n + 2)
                dve.tensor_scalar(mean_eps[:, n], sumsq[:, n], 1.0 / D, EPS, ALU.mult, ALU.add).then_inc(ms_done, 1)
                dve.wait_ge(rs_done, n + 1)
                for t in range(TT):
                    dve.tensor_scalar(xn[:, t], src[:, t], rnorm[:, n, t:t + 1], None, ALU.mult).then_inc(xn_done, 1)

            def transposed_lo(n, hi, lo):
                for u in range(5):
                    if u < 4:
                        t, half = divmod(u, 2)
                        dve.wait_ge(nt_ps, 4 * n + u + 1)
                        if u >= 2:
                            dve.wait_ge(nt_lo, 4 * n + u - 1)
                        dve.tensor_tensor(nt_tmp[:, u % 2].rearrange("p (k q) -> p k q", k=4),
                                          SC[u % 2][:].rearrange("p (k q) -> p k q", k=4),
                                          gains[:, n, half * 4:half * 4 + 4].unsqueeze(2).broadcast_to([P, 4, P]),
                                          ALU.mult).then_inc(nt_gain, 1)
                    if u >= 1:
                        v = u - 1
                        t, half = divmod(v, 2)
                        dst = (slice(None), slice(half * 4, half * 4 + 4), slice(t * P, (t + 1) * P))
                        dve.wait_ge(nt_hi, 4 * n + v + 1)
                        dve.tensor_tensor(lo[dst], nt_tmp[:, v % 2].rearrange("p (k q) -> p k q", k=4),
                                          hi[dst].bitcast(F32), ALU.subtract).then_inc(nt_lo, 1)

            def split_lo(g):
                if g >= NH:
                    return
                dve.wait_ge(hi_done, g + 1)
                dve.tensor_tensor(w_lo[:, g % NS], w_raw[:, g % NW], w_hi[:, g % NS].bitcast(F32), ALU.subtract)\
                    .then_inc(lo_done, 1)

            def bias_and_max(j):
                b, swa = j % 2, j >= PAIRS
                dve.wait_ge(s_ps, j + 1)
                if j >= 2:
                    dve.wait_ge(pt_ps, j - 1)
                for hh in range(2):
                    h = 2 * (j % PAIRS) + hh
                    dve.scalar_tensor_tensor(out=scores[:, b, hh], in0=dist[:, int(swa)], scalar=2.0 ** -(h + 1),
                                             in1=SC[hh][:, 0:SK], op0=ALU.mult, op1=ALU.add).then_inc(s_bias, 1)
                dve.wait_ge(s_bias, 2 * j + 2)
                for tt in range(TT):
                    cols = slice(0, P) if tt == 0 else slice(P, SK)
                    dve.tensor_reduce(nmax[:, b, tt], scores[:, b, :, cols], axis=AX.X, op=ALU.max,
                                      negate=True).then_inc(s_max, 1)
                if swa:
                    h = 2 * (j % PAIRS)
                    count = s_max_count(j)
                    dve.wait_ge(s_max, count - 2)
                    dve.tensor_tensor(nmax[:, b], nmax[:, b], nsinks[:, h:h + 2].unsqueeze(1).broadcast_to([P, 2, 2]),
                                      ALU.min).then_inc(s_max, 1)
                    dve.wait_ge(s_max, count - 1)
                    dve.tensor_tensor(sink_arg[:, b].rearrange("p (t h) -> p t h", t=2), nmax[:, b],
                                      sinks[:, h:h + 2].unsqueeze(1).broadcast_to([P, 2, 2]), ALU.add)\
                        .then_inc(s_max, 1)

            sunk = [0]

            def inverse_sums(j):
                b = j % 2
                dve.wait_ge(s_exp, s_exp_count(j))
                if j >= PAIRS:
                    dve.tensor_tensor(rsum[:, b], rsum[:, b], sink_exp[:, b], ALU.add).then_inc(c_sink, 1)
                    sunk[0] += 1
                    dve.wait_ge(c_sink, 1 + sunk[0])
                dve.reciprocal(rinv[:, b], rsum[:, b]).then_inc(s_inv, 1)

            def mix_out_lo(j):
                dve.wait_ge(mix_hi, j + 1)
                dve.tensor_tensor(mixT_lo[:, j], PO[j % 2][:, 0:T], mixT_hi[:, j].bitcast(F32), ALU.subtract)\
                    .then_inc(mix_lo, 1)

            dve.wait_ge(c_gain_ps, 1)
            dve.tensor_copy(gains[:], PO[0][:, 0:4 * KD].rearrange("p (n k) -> p n k", n=4)).then_inc(c_gain, 1)
            normalise(0, xres)
            dve.wait_ge(c_gain, 1)
            transposed_lo(0, hT_hi, hT_lo)
            split_lo(0)
            split_lo(1)
            dve.wait_ge(c_sink_ps, 1)
            dve.tensor_copy(sinks[:], PO[1][:, 0:HEADS]).then_inc(c_sink, 1)
            dve.tensor_scalar(nsinks[:], PO[1][:, 0:HEADS], -1.0, None, ALU.mult).then_inc(c_gain, 1)
            dve.wait_ge(c_sink, 1)
            dve.wait_ge(c_gain, 2)
            for c in range(FIRST_UNDER):
                split_lo(2 * c + 2)
                split_lo(2 * c + 3)
                if c == 1:
                    normalise(MEM_NORM, mem_raw)
            dve.wait_ge(c_misc, 14)
            for i in range(STEPS):
                c = FIRST_UNDER + i
                if i < UNITS:
                    bias_and_max(i)
                split_lo(2 * c + 2)
                if i < UNITS:
                    inverse_sums(i)
                split_lo(2 * c + 3)
                if 2 <= i <= UNITS + 1:
                    mix_out_lo(i - 2)
            transposed_lo(MEM_NORM, memT_hi, memT_lo)
            dve.wait_ge(sig_done, 2)
            for c in range(at["merge"], at["mix"]):
                m = c - at["merge"]
                split_lo(2 * c + 2)
                split_lo(2 * c + 3)
                dve.wait_ge(half_done, 2 * c + 2)
                ga, gb = gates[:, 2 * m:2 * m + 2], gates[:, KD + 2 * m:KD + 2 * m + 2]
                dve.tensor_tensor(ga, ga, PJ[c % 2][:].rearrange("p (a n) -> p a n", a=2), ALU.mult)\
                    .then_inc(mg_part, 1)
                dve.tensor_tensor(gb, gb, PT[c % 2][:].rearrange("p (a n) -> p a n", a=2), ALU.mult)\
                    .then_inc(ev_dve, 1)
                dve.wait_ge(mg_part, m + 1)
                dve.wait_ge(ev_dve, evac_count(c))
                dve.tensor_tensor(ga, ga, gb, ALU.add).then_inc(mg_sum, 1)
                dve.wait_ge(mg_hi, m + 1)
                dve.tensor_tensor(mgT_lo[:, 2 * m:2 * m + 2], ga, mgT_hi[:, 2 * m:2 * m + 2].bitcast(F32),
                                  ALU.subtract).then_inc(mg_lo, 1)

            def add_residual(src, col):
                dst = xres[:, :, col:col + CW]
                dve.tensor_tensor(dst, dst, src[:].rearrange("p (t n) -> p t n", t=TT), ALU.add).then_inc(ev_dve, 1)

            for c in range(at["mix"], at["kx"]):
                split_lo(2 * c + 2)
                split_lo(2 * c + 3)
                dve.wait_ge(half_done, 2 * c + 2)
                add_residual(PJ[c % 2], (c - at["mix"]) * CW)
            normalise(X2_NORM, xres)
            for c in range(at["kx"], at["kx"] + 2):
                split_lo(2 * c + 2)
                split_lo(2 * c + 3)
            transposed_lo(X2_NORM, h2T_hi, h2T_lo)
            for c in range(at["qx"], at["qx"] + 2):
                split_lo(2 * c + 2)
                split_lo(2 * c + 3)
            for i in range(2):
                for h in (2 * i, 2 * i + 1):
                    dve.wait_ge(xs_ps, h + 1)
                    dve.tensor_reduce(xmax[:, h], SC[h % 2][:].rearrange("p (t m) -> p t m", t=TT), axis=AX.X,
                                      op=ALU.max).then_inc(xs_max, 1)
                    dve.wait_ge(xs_max, 2 * h + 1)
                    dve.tensor_scalar(xnmax[:, h], xmax[:, h], -XSCALE, None, ALU.mult).then_inc(xs_max, 1)
                for h in (2 * i, 2 * i + 1):
                    dve.wait_ge(xs_exp, 2 * h + 2)
                    dve.reciprocal(xinv[:, h], xsum[:, h]).then_inc(xs_inv, 1)
                c = at["vx"] + i
                split_lo(2 * c + 2)
                split_lo(2 * c + 3)
            for h in range(XH):
                dve.wait_ge(ox_hi, h + 1)
                dve.tensor_tensor(oxT_lo[:, h], PO[h % 2][:, 0:T], oxT_hi[:, h].bitcast(F32), ALU.subtract)\
                    .then_inc(ox_lo, 1)
            split_lo(2 * at["xo"] + 2)
            split_lo(2 * at["xo"] + 3)
            for c in range(at["xo"], NC):
                dve.wait_ge(half_done, 2 * c + 2)
                add_residual(PJ[c % 2], (2 * (c - at["xo"])) * CW)
                add_residual(PT[c % 2], (2 * (c - at["xo"]) + 1) * CW)
            normalise(X3_NORM, xres)
            for u in range(4):
                t, half = divmod(u, 2)
                dve.wait_ge(nt_ps, 4 * X3_NORM + u + 1)
                dve.tensor_tensor(h3T[:, half * 4:half * 4 + 4, t * P:(t + 1) * P],
                                  SC[u % 2][:].rearrange("p (k q) -> p k q", k=4),
                                  gains[:, X3_NORM, half * 4:half * 4 + 4].unsqueeze(2).broadcast_to([P, 4, P]),
                                  ALU.mult).then_inc(nt_gain, 1)

            steps = [0]

            def then(op):
                op.then_inc(r_step, 1)
                steps[0] += 1
                dve.wait_ge(r_step, steps[0])

            then(dve.memset(g_log[:], BIG))
            for t in range(TT):
                logit = LOGIT[t][:, 0:NG + NE]
                dve.wait_ge(logits_ps, t + 1)
                then(dve.tensor_copy(g_log[:, t, 0:NG], logit[:, 0:NG]))
                then(dve.max(g_top[:, t], g_log[:, t]))
                dve.tensor_scalar(g_neg[:, t:t + 1], g_top[:, t, 0:1], -1.0, None, ALU.mult).then_inc(r_top, 1)
                then(dve.max_index(g_idx[:, t], g_top[:, t], g_log[:, t]))
                then(dve.tensor_copy(g_idf[:, t], g_idx[:, t]))
                then(dve.tensor_scalar(pen[:, t], iota_e[:, 0:NG], g_idf[:, t, 0:1], BIG, ALU.not_equal, ALU.mult))
                then(dve.tensor_tensor(e_log[:, t], logit[:, NG:NG + NE].rearrange("p (g e) -> p g e", g=NG),
                                       pen[:, t].unsqueeze(2).broadcast_to([P, NG, EPG]), ALU.add))
                flat = e_log[:, t].rearrange("p g e -> p (g e)")
                then(dve.max(e_top[:, t], flat))
                dve.tensor_scalar(e_neg[:, t:t + 1], e_top[:, t, 0:1], -1.0, None, ALU.mult).then_inc(r_top, 1)
                then(dve.max_index(e_idx[:, t], e_top[:, t], flat))
                then(dve.tensor_copy(e_idf[:, t], e_idx[:, t]))
                then(dve.tensor_scalar(first[:, t], iota_e[:], e_idf[:, t, 0:1], None, ALU.is_equal))
                dve.scalar_tensor_tensor(out=both[:, t], in0=iota_e[:], scalar=e_idf[:, t, 1:2], in1=first[:, t],
                                         op0=ALU.is_equal, op1=ALU.add).then_inc(r_mask, 1)
            for t in range(TT):
                dve.wait_ge(pos_ps, t + 1)
                then(dve.scalar_tensor_tensor(out=posm[:, t], in0=LISTED[t][:, 0:NE], scalar=1000.0,
                                              in1=both[:, t], op0=ALU.add, op1=ALU.mult))
                then(dve.tensor_scalar(posm[:, t], posm[:, t], -1000.0, None, ALU.add))
                then(dve.tensor_tensor(slot_of[:, t], posm[:, t].unsqueeze(1).broadcast_to([P, ROUNDS, NE]),
                                       iota_rw[:].unsqueeze(2).broadcast_to([P, ROUNDS, NE]), ALU.subtract))
            for t in range(TT):
                one = slice(t, t + 1)
                dve.wait_ge(r_exp, 2 * t + 2)
                then(dve.scalar_tensor_tensor(out=den[:, one], in0=e2[:, one], scalar=1.0, in1=g_sum[:, one],
                                              op0=ALU.add, op1=ALU.mult))
                then(dve.reciprocal(ew[:, 0, one], den[:, one]))
                then(dve.tensor_tensor(ew[:, 1, one], ew[:, 0, one], e2[:, one], ALU.mult))
                then(dve.tensor_scalar(wfirst[:, t], iota_e[:], e_idf[:, t, 0:1], ew[:, 0, one], ALU.is_equal, ALU.mult))
                then(dve.tensor_scalar(wboth[:, t], iota_e[:], e_idf[:, t, 1:2], ew[:, 1, one], ALU.is_equal, ALU.mult))
                then(dve.tensor_tensor(wboth[:, t], wboth[:, t], wfirst[:, t], ALU.add))
                then(dve.tensor_copy(weight_of[:, t], wboth[:, t].unsqueeze(1).broadcast_to([P, ROUNDS, NE])))
            dve.wait_ge(pos_ps, TT + 1)
            then(dve.tensor_reduce(cmax[:], COUNTS[:, 0:NE], axis=AX.X, op=ALU.max))
            then(dve.tensor_scalar(over[:, 0:ROUNDS - 1], iota_rw[:, 1:ROUNDS], cmax[:], None, ALU.is_lt))
            then(dve.tensor_reduce(nover[:], over[:, 0:ROUNDS - 1], axis=AX.X, op=ALU.add))
            dve.tensor_scalar(trips[:], nover[:], float(QUADS), float(QUADS), ALU.mult, ALU.add).then_inc(trips_set, 1)

            dve.wait_ge(trips_set, 1)
            total = dve.value_load(trips[0:1, 0:1], min_val=QUADS, max_val=QUADS * ROUNDS)
            slots_flat = slot_of[:].rearrange("p t r e -> p t (r e)")
            weight_flat = weight_of[:].rearrange("p t r e -> p t (r e)")
            iota_s = iota_e[:, 0:WIN].unsqueeze(1).broadcast_to([P, QE, WIN])
            with dve.Fori(0, total) as it:
                for t in range(TT):
                    dve.tensor_tensor(sel[:, t], slots_flat[:, t, bass.ds(it * QE, QE)].unsqueeze(2)
                                      .broadcast_to([P, QE, WIN]), iota_s, ALU.is_equal).then_inc(sel_made, 1)
                dve.wait_ge(sel_made, it * 4 + 2)
                for t in range(TT):
                    dve.tensor_tensor(selw[:, t], sel[:, t], weight_flat[:, t, bass.ds(it * QE, QE)].unsqueeze(2)
                                      .broadcast_to([P, QE, WIN]), ALU.mult).then_inc(sel_made, 1)
                for half in range(2):
                    dve.wait_ge(gather_ps, it * 2 + half + 1)
                    dve.tensor_tensor(moe_x[:, half * 4:half * 4 + 4], SC[half][:].rearrange("p (k s) -> p k s", k=4),
                                      gains[:, X3_NORM, half * 4:half * 4 + 4].unsqueeze(2).broadcast_to([P, 4, P]),
                                      ALU.mult).then_inc(moe_x_sb, 1)
                dve.wait_ge(silu_done, it + 1)
                dve.tensor_tensor(hid[:], silu_g[:], PJ[0][:, FE:2 * FE], ALU.mult).then_inc(hid_done, 1)
                dve.wait_ge(chunk_used, it * MOE_CHUNKS + MOE_CHUNKS)
                dve.tensor_copy(y_sb[:, 512:1024], SC[1][:]).then_inc(y_dve, 1)
                for s in range(4):
                    t, half = divmod(s, 2)
                    cols = slice(half * 512, (half + 1) * 512)
                    dve.wait_ge(back_ps, it * 4 + s + 1)
                    dve.tensor_tensor(xres[:, t, cols], xres[:, t, cols], PO[s % 2][:], ALU.add).then_inc(added, 1)

            dve.wait_ge(sq_done, 10)
            dve.tensor_scalar(mean_eps[:, 4], sumsq[:, 4], 1.0 / D, EPS, ALU.mult, ALU.add).then_inc(ms_done, 1)
            dve.wait_ge(rs_done, 5)
            dve.wait_ge(fin_sb, 2)
            for t in range(TT):
                dve.scalar_tensor_tensor(out=xn[:, t], in0=xres[:, t], scalar=rnorm[:, 4, t:t + 1], in1=fin_g[:],
                                         op0=ALU.mult, op1=ALU.mult).then_inc(xn_done, 1)

        @block.tensor
        def _(pe):
            def transpose_rows(n):
                for u in range(4):
                    t, half = divmod(u, 2)
                    pe.wait_ge(xn_done, 2 * n + t + 1)
                    if u >= 2:
                        pe.wait_ge(nt_gain, 4 * n + u - 1)
                    for k in range(4):
                        col = (half * 4 + k) * P
                        op = pe.transpose(SC[u % 2][:, k * P:(k + 1) * P], xn[:, t, col:col + P], ident[:])
                    op.then_inc(nt_ps, 1)

            def product(ps, a, b, start, stop):
                pe.matmul(ps, a[0], b[0], start=start, stop=False, skip_group_check=True)
                pe.matmul(ps, a[0], b[1], start=False, stop=False, skip_group_check=True)
                return pe.matmul(ps, a[1], b[0], start=False, stop=stop, skip_group_check=True)

            def half_chunk(g, hi, lo):
                c, h = divmod(g, 2)
                kind, b = kinds[c], g % NS
                own = kind in ("merge", "xo")
                ps = PT[c % 2] if own and h else PJ[c % 2]
                if h == 0 and c >= 2:
                    pe.wait_ge(ev_dve if kinds[c - 2] in ON_DVE else ev_act, evac_count(c - 2))
                pe.wait_ge(lo_done, g + 1)
                k0 = {"merge": h * HK, "xo": 0}.get(kind, h * HK)
                opens, closes = own or h == 0, own or h == 1
                for k in range(HK):
                    for j in range(2):
                        W = (w_hi[:, b, k], w_lo[:, b, k])
                        wcol = [w[:, j * P:(j + 1) * P] for w in W]
                        X = (hi[:, k0 + k], lo[:, k0 + k])
                        xcol = [v[:, j * P:(j + 1) * P] for v in X]
                        start, stop = opens and k == 0 and j == 0, closes and k == HK - 1
                        if kind in ("va", "vx", "mix", "xo"):
                            op = product(ps[:, j * T:(j + 1) * T], xcol, W, start, stop)
                        elif kind == "kvb" and j == 1:
                            for t in range(TT):
                                op = product(ps[:, T + t * P:T + (t + 1) * P], [v[:, t * P:(t + 1) * P] for v in X],
                                             wcol, start, stop)
                        else:
                            op = product(ps[:, j * T:(j + 1) * T], wcol, X, start, stop)
                op.then_inc(half_done, 1)

            def pair_scores(j):
                swa, i = divmod(j, PAIRS)
                need = "kvb" if swa else ("ka" if i < 2 else "ka")
                pe.wait_ge(ev_act, evac_count(at["kvb"] if swa else at["ka"] + i // 2))
                if j:
                    pe.wait_ge(s_bias, 2 * j)
                q = qb if swa else qa
                for tt in range(TT):
                    for hh in range(2):
                        rows = slice(hh * HD, (hh + 1) * HD)
                        keys = kb2[rows, (2 * i + hh) // 4] if swa else ka[rows, i]
                        if tt == 0:
                            op = pe.matmul(SC[hh][:, 0:P], q[rows, i, 0:P], keys[:, 0:P], start=True, stop=True)
                        else:
                            op = pe.matmul(SC[hh][:, P:SK], q[rows, i, P:T], keys, start=True, stop=True)
                op.then_inc(s_ps, 1)

            def pair_transposes(j):
                pe.wait_ge(s_norm, 4 * (j + 1))
                if j:
                    pe.wait_ge(pt_sb, 2 * j)
                for hh in range(2):
                    for i in range(3):
                        cols = slice(i * P, (i + 1) * P)
                        op = pe.transpose(PT[hh][:, cols], scores[:, j % 2, hh, cols], ident[:])
                op.then_inc(pt_ps, 1)

            def pair_values(j):
                swa, i = divmod(j, PAIRS)
                pe.wait_ge(ev_act, evac_count(at["kvb"] if swa else at["va"] + i // 2))
                pe.wait_ge(pt_sb, 2 * j + 2)
                if j >= 2:
                    pe.wait_ge(mix_lo, j - 1)
                for tt, kt, cols in ((0, 0, slice(0, P)), (1, 0, slice(P, 2 * P)), (1, 1, slice(2 * P, SK))):
                    for hh in range(2):
                        h = 2 * i + hh
                        v = vb[:, kt, (h // 4) * HD:(h // 4 + 1) * HD] if swa else va[:, kt, h * HD:(h + 1) * HD]
                        op = pe.matmul(PO[j % 2][hh * HD:(hh + 1) * HD, tt * P:(tt + 1) * P], v, probT[:, hh, cols],
                                       start=kt == 0, stop=kt == tt)
                op.then_inc(pv_ps, 1)

            pe.wait_ge(c_ident, 1)
            pe.wait_ge(gain_in, 64)
            pe.transpose(PO[0][:, 0:4 * KD], g_rows[:], ident[0:4 * KD, 0:4 * KD]).then_inc(c_gain_ps, 1)
            pe.wait_ge(c_ones, 1)
            pe.wait_ge(small_in, 80)
            pe.matmul(PO[1][:, 0:HEADS], ones[0:1, :], sink_row[:], start=True, stop=True).then_inc(c_sink_ps, 1)
            transpose_rows(0)
            pe.wait_ge(nt_lo, 4)
            for c in range(FIRST_UNDER):
                half_chunk(2 * c, hT_hi, hT_lo)
                half_chunk(2 * c + 1, hT_hi, hT_lo)
            pe.wait_ge(c_gain, 2)
            pe.wait_ge(c_sink, 1)
            for i in range(STEPS):
                c = FIRST_UNDER + i
                if i < UNITS:
                    pair_scores(i)
                half_chunk(2 * c, hT_hi, hT_lo)
                half_chunk(2 * c + 1, hT_hi, hT_lo)
                if 1 <= i <= UNITS:
                    pair_transposes(i - 1)
                if 2 <= i <= UNITS + 1:
                    pair_values(i - 2)
            transpose_rows(MEM_NORM)
            pe.wait_ge(mix_lo, UNITS)
            for g in range(2 * at["merge"], 2 * at["mix"]):
                half_chunk(g, mixT_hi, mixT_lo)
            pe.wait_ge(mg_lo, 4)
            for g in range(2 * at["mix"], 2 * at["kx"]):
                half_chunk(g, mgT_hi, mgT_lo)
            pe.wait_ge(nt_lo, 4 * (MEM_NORM + 1))
            for g in range(2 * at["kx"], 2 * at["qx"]):
                half_chunk(g, memT_hi, memT_lo)
            transpose_rows(X2_NORM)
            pe.wait_ge(nt_lo, 4 * (X2_NORM + 1))
            for g in range(2 * at["qx"], 2 * at["vx"]):
                half_chunk(g, h2T_hi, h2T_lo)
            pe.wait_ge(ev_act, evac_count(at["vx"] - 1))
            for i in range(2):
                for h in (2 * i, 2 * i + 1):
                    if h >= 2:
                        pe.wait_ge(xs_exp, 2 * (h - 1))
                    for tt in range(TT):
                        op = pe.matmul(SC[h % 2][:, tt * T:(tt + 1) * T], qx[:, h, tt * P:(tt + 1) * P], kx[:, h],
                                       start=True, stop=True)
                    op.then_inc(xs_ps, 1)
                for g in range(2 * (at["vx"] + i), 2 * (at["vx"] + i) + 2):
                    half_chunk(g, memT_hi, memT_lo)

            def x_transposes(h):
                pe.wait_ge(xs_norm, 2 * h + 2)
                if h >= 2:
                    pe.wait_ge(xpt_sb, h - 1)
                for mt in range(2):
                    for tt in range(TT):
                        op = pe.transpose(PT[h % 2][:, mt * T + tt * P:mt * T + (tt + 1) * P],
                                          xprob[:, h, tt, mt * P:(mt + 1) * P], ident[:])
                op.then_inc(xpt_ps, 1)

            def x_values(h):
                pe.wait_ge(xpt_sb, h + 1)
                if h >= 2:
                    pe.wait_ge(ox_lo, h - 1)
                for mt in range(2):
                    op = pe.matmul(PO[h % 2][:, 0:T], vx[:, mt, h * P:(h + 1) * P], xpT[:, h % 2, mt * T:(mt + 1) * T],
                                   start=mt == 0, stop=mt == 1)
                op.then_inc(xpv_ps, 1)

            x_transposes(0)
            pe.wait_ge(ev_act, evac_count(at["xo"] - 1))
            for h in range(XH):
                if h + 1 < XH:
                    x_transposes(h + 1)
                x_values(h)
            pe.wait_ge(ox_lo, XH)
            for g in range(2 * at["xo"], NH):
                half_chunk(g, oxT_hi, oxT_lo)
            pe.wait_ge(fin_in, 16)
            transpose_rows(X3_NORM)

            for t in range(TT):
                ps = LOGIT[t][:, 0:NG + NE]
                pe.wait_ge(nt_gain, 4 * X3_NORM + 2 * t + 2)
                for k in range(KD):
                    pe.matmul(ps, h3T[:, k, t * P:(t + 1) * P], wr[:, k], start=k == 0, stop=False)
                pe.matmul(ps, ones[0:1, :], br[:], start=False, stop=True).then_inc(logits_ps, 1)
            pe.wait_ge(nt_gain, 4 * X3_NORM + 4)
            for half in range(2):
                op = pe.matmul(SC[half][:], ones[0:1, :], fin_row[:, half * 512:(half + 1) * 512], start=True, stop=True)
            op.then_inc(fin_ps, 1)
            pe.wait_ge(c_misc, 14)
            pe.wait_ge(r_mask, 1)
            pe.matmul(LISTED[0][:, 0:NE], below[:], both[:, 0], start=True, stop=True).then_inc(pos_ps, 1)
            pe.wait_ge(r_mask, 2)
            pe.matmul(LISTED[1][:, 0:NE], ones[:], both[:, 0], start=True, stop=False)
            pe.matmul(LISTED[1][:, 0:NE], below[:], both[:, 1], start=False, stop=True).then_inc(pos_ps, 1)
            pe.matmul(COUNTS[:, 0:NE], ones[:], both[:, 0], start=True, stop=False)
            pe.matmul(COUNTS[:, 0:NE], ones[:], both[:, 1], start=False, stop=True).then_inc(pos_ps, 1)

            pe.wait_ge(trips_set, 1)
            pe.wait_ge(fin_sb, 2)
            total = pe.value_load(trips[0:1, 0:1], min_val=QUADS, max_val=QUADS * ROUNDS)
            with pe.Fori(0, total) as it:
                pe.wait_ge(sel_made, it * 4 + 2)
                for k in range(KD):
                    for t in range(TT):
                        op = pe.matmul(SC[k // 4][:, (k % 4) * P:(k % 4 + 1) * P], xn[:, t, k * P:(k + 1) * P],
                                       sel[:, t].rearrange("p e s -> p (e s)"), start=t == 0, stop=t == TT - 1)
                    if k % 4 == 3:
                        op.then_inc(gather_ps, 1)
                pe.wait_ge(sel_made, it * 4 + 4)
                for t in range(TT):
                    op = pe.transpose(PT[1][:, t * P:(t + 1) * P], selw[:, t].rearrange("p e s -> p (e s)"), ident[:])
                op.then_inc(selT_ps, 1)
                for k in range(KD):
                    if k % 4 == 0:
                        pe.wait_ge(moe_x_sb, it * 2 + k // 4 + 1)
                    pe.wait_ge(moe_in[k], it * 32 + 32)
                    for e in range(QE):
                        op = pe.matmul(PJ[0][e * WIN:(e + 1) * WIN, :], moe_x[:, k, e * WIN:(e + 1) * WIN],
                                       slots[k][:, e * 512:(e + 1) * 512], start=k == 0, stop=k == KD - 1)
                    op.then_inc(chunk_used, 1)
                pe.wait_ge(hid_done, it + 1)
                for k in range(KF):
                    op = pe.transpose(PT[0][:, k * P:(k + 1) * P], hid[:, k * P:(k + 1) * P], ident[:])
                op.then_inc(hidT_ps, 1)
                pe.wait_ge(hidT_sb, it + 1)
                for kt in range(KF):
                    for pair in range(2):
                        pe.wait_ge(moe_in[GU_CHUNKS + 2 * kt + pair], it * 32 + 32)
                    for half in range(2):
                        for e in range(QE):
                            w = slots[GU_CHUNKS + 2 * kt + e // 2]
                            col = (e % 2) * D + half * 512
                            op = pe.matmul(SC[half][e * WIN:(e + 1) * WIN, :], hidT[:, kt, e * WIN:(e + 1) * WIN],
                                           w[:, col:col + 512], start=kt == 0, stop=kt == KF - 1)
                    op.then_inc(chunk_used, 2)
                pe.wait_ge(selT_sb, it + 1)
                pe.wait_ge(y_act, it + 1)
                pe.wait_ge(y_dve, it + 1)
                for s in range(4):
                    t, half = divmod(s, 2)
                    if s >= 2:
                        pe.wait_ge(added, it * 4 + s - 1)
                    pe.matmul(PO[s % 2][:], selwT[:, t * P:(t + 1) * P], y_sb[:, half * 512:(half + 1) * 512],
                              start=True, stop=True).then_inc(back_ps, 1)


_INS = ["x", "mem", "mix_norm_g", "w_in", "moba_out_w", "swa_out_w", "swa_sinks", "mix_out_w", "xattn_norm_g",
        "mem_norm_g", "xattn_wq", "xattn_wkv", "xattn_wo", "ffn_norm_g", "router_group_w", "router_group_b",
        "router_expert_w", "router_expert_b", "expert_w_gate", "expert_w_up", "expert_w_down", "final_norm_g"]
_OUTS = [((1, 256, 1024), "float32")]


def kernel(**inputs):
    import numpy as _np
    import concourse.bacc as _bacc
    from concourse import mybir as _mybir
    from concourse.bass_utils import run_bass_kernel_spmd as _run

    nc = _bacc.Bacc("TRN2", target_bir_lowering=False, num_devices=1)
    arrays, args = {}, []
    for name in _INS:
        a = _np.ascontiguousarray(inputs[name])
        arrays[f"in_{name}_dram"] = a
        args.append(nc.dram_tensor(f"in_{name}_dram", a.shape, _mybir.dt.from_np(a.dtype), kind="ExternalInput").ap())
    for i, (shape, dtype) in enumerate(_OUTS):
        dt = _mybir.dt.from_np(_np.dtype(dtype))
        args.append(nc.dram_tensor(f"out_{i}_dram", shape, dt, kind="ExternalOutput").ap())
    hybrid_layer(nc, *args)
    r = _run(nc, [arrays], core_ids=[0])
    got = tuple(r.results[0][f"out_{i}_dram"] for i in range(len(_OUTS)))
    return got[0]
```

```python
from contextlib import ExitStack

import concourse.bass as bass
from concourse import mybir

P = 128


def hybrid_layer(nc, x, mem, mix_norm_g, w_in, moba_out_w, swa_out_w, swa_sinks, mix_out_w, xattn_norm_g,
                 mem_norm_g, xattn_wq, xattn_wkv, xattn_wo, ffn_norm_g, router_group_w, router_group_b,
                 router_expert_w, router_expert_b, expert_w_gate, expert_w_up, expert_w_down,
                 final_norm_g, out):
    F32, F32R = mybir.dt.float32, mybir.dt.float32r
    I32, U32 = mybir.dt.int32, mybir.dt.uint32
    ALU, ACT, AX = mybir.AluOpType, mybir.ActivationFunctionType, mybir.AxisListType

    T, D = x.shape[1], x.shape[2]
    TT, KD = T // P, D // P
    HD, HEADS, WINDOW = 64, 8, 128
    PAIRS = HEADS // 2
    XH = 4
    XSCALE = float(P) ** -0.5
    NG, EPG = expert_w_gate.shape[1], expert_w_gate.shape[2]
    NE, FE = NG * EPG, expert_w_gate.shape[4]
    KF = FE // P
    WIN = 32
    QE = P // WIN
    QUADS = NE // QE
    ROUNDS = T // WIN
    EPS, NEG, BIG = 1e-6, -1e30, -3e38
    UNLISTED = 1000
    CW = 256
    HK = 4
    SK = T + WINDOW

    win = w_in[0].rearrange("(k p) n -> p k n", p=P)
    wkv = xattn_wkv[0].rearrange("(k p) n -> p k n", p=P)
    wq = xattn_wq[0].rearrange("(k p) n -> p k n", p=P)
    wmix = mix_out_w[0].rearrange("(k p) n -> p k n", p=P)
    wa = moba_out_w[0].rearrange("(k p) n -> p k n", p=P)
    wb = swa_out_w[0].rearrange("(k p) n -> p k n", p=P)
    wo = xattn_wo[0].rearrange("(k p) n -> p k n", p=P)

    def both_halves(w, col):
        return [w[:, h * HK:(h + 1) * HK, col:col + CW] for h in range(2)]

    halves, kinds = [], []
    for c in range(17):
        kinds.append(["qa", "qa", "ka", "ka", "va", "va", "qb", "qb", "kvb"][c] if c < 9 else "gate")
        halves += both_halves(win, c * CW)
    for m in range(4):
        kinds.append("merge")
        halves += [wa[:, :, m * CW:(m + 1) * CW], wb[:, :, m * CW:(m + 1) * CW]]
    for name, w, col in (("kx", wkv, 0), *(("mix", wmix, m * CW) for m in range(4)), ("kx", wkv, CW),
                         ("vx", wkv, 2 * CW), ("qx", wq, 0), ("qx", wq, CW), ("vx", wkv, 3 * CW)):
        kinds.append(name)
        halves += both_halves(w, col)
    for m in range(2):
        kinds.append("xo")
        halves += [wo[:, :, (2 * m + h) * CW:(2 * m + h + 1) * CW] for h in range(2)]
    NC, NH = len(kinds), len(halves)
    at = {k: kinds.index(k) for k in kinds}
    last = {k: NC - 1 - kinds[::-1].index(k) for k in kinds}
    ON_DVE = {"merge": 1, "mix": 1, "xo": 2}

    def evac_count(c):
        if kinds[c] in ON_DVE:
            return sum(ON_DVE.get(k, 0) for k in kinds[:c + 1])
        return sum(k not in ON_DVE for k in kinds[:c + 1])

    NW, NS = 3, 3

    GU_CHUNKS, MOE_CHUNKS = KD, KD + KF * 2
    BODY_QUADS = 4
    BODIES, BODY_CHUNKS = QUADS // BODY_QUADS, BODY_QUADS * MOE_CHUNKS
    SLOTS = 20

    def slot_of_chunk(i):
        return i % SLOTS

    def loads_of_slot(s):
        return sum(slot_of_chunk(i) == s for i in range(BODY_CHUNKS))

    def landed(i, body):
        s = slot_of_chunk(i)
        nth = sum(slot_of_chunk(n) == s for n in range(i))
        return body * (32 * loads_of_slot(s)) + 32 * (nth + 1)

    def previous_user(i):
        users = [n for n in range(BODY_CHUNKS) if slot_of_chunk(n) == slot_of_chunk(i)]
        return users[users.index(i) - 1] if users.index(i) else users[-1] - BODY_CHUNKS
    wg_v = expert_w_gate[0].rearrange("g e (k p) f -> k p (g e) f", p=P)
    wu_v = expert_w_up[0].rearrange("g e (k p) f -> k p (g e) f", p=P)
    wd_v = expert_w_down[0].rearrange("g e (k p) d -> k p (g e) d", p=P)

    ctx = ExitStack()
    with ctx:
        place = [(nc.sbuf_base + 63) // 64 * 64]

        def region(nbytes):
            place[0] += nbytes
            assert place[0] <= nc.sbuf_usable_end
            return place[0] - nbytes

        def sb(name, shape, dt, offset=None):
            n = 4
            for s in shape[1:]:
                n *= s
            offset = region((n + 31) // 32 * 32) if offset is None else offset
            return nc.alloc_sbuf_tensor_at(name, shape, dt, offset=offset)

        slot_at = [region(8192) for _ in range(11)]
        mem_raw = sb("mem_raw", [P, TT, D], F32, slot_at[8])
        mixT_hi = sb("mixT_hi", [P, 2 * PAIRS, T], F32R, slot_at[9])
        mixT_lo = sb("mixT_lo", [P, 2 * PAIRS, T], F32R, slot_at[10])
        w_at = region(NW * HK * CW * 4)
        w_raw = sb("w_raw", [P, NW, HK, CW], F32, w_at)
        w_hi = sb("w_hi", [P, NS, HK, CW], F32R)
        w_lo = sb("w_lo", [P, NS, HK, CW], F32R)
        fin_g = sb("fin_g", [P, D], F32, w_at + 4 * 8192)
        xres = sb("xres", [P, TT, D], F32)
        xn = sb("xn", [P, TT, D], F32)
        r1 = region(16384)
        hT_hi = sb("hT_hi", [P, KD, T], F32R, r1)
        hT_lo = sb("hT_lo", [P, KD, T], F32R, r1 + 8192)
        mgT_hi = sb("mgT_hi", [P, KD, T], F32R, r1)
        mgT_lo = sb("mgT_lo", [P, KD, T], F32R, r1 + 8192)
        h2T_hi = sb("h2T_hi", [P, KD, T], F32R, slot_at[9])
        h2T_lo = sb("h2T_lo", [P, KD, T], F32R, slot_at[10])
        oxT_hi = sb("oxT_hi", [P, XH, T], F32R, r1)
        oxT_lo = sb("oxT_lo", [P, XH, T], F32R, r1 + 8192)
        r2 = region(16384 + 2048 + 1024)
        r3 = region(16384)
        slot_at += [r2, r2 + 8192, r3]
        slot_at += [w_at + n * 8192 for n in range(4)] + [r1]
        qa = sb("qa", [P, PAIRS, T], F32, r2)
        ka = sb("ka", [P, PAIRS, T], F32, r2 + 4096)
        va = sb("va", [P, TT, HEADS * HD], F32, r2 + 8192)
        qb = sb("qb", [P, PAIRS, T], F32, r2 + 12288)
        kb2 = sb("kb2", [P, 2, T], F32, r2 + 16384)
        vb = sb("vb", [P, TT, P], F32, r2 + 18432)
        memT_hi = sb("memT_hi", [P, KD, T], F32R, r2)
        memT_lo = sb("memT_lo", [P, KD, T], F32R, r2 + 8192)
        gates = sb("gates", [P, 2 * KD, T], F32, r3)
        qx = sb("qx", [P, XH, T], F32, r3)
        kx = sb("kx", [P, XH, T], F32, r3 + 4096)
        vx = sb("vx", [P, TT, XH * P], F32, r3 + 8192)
        xpT = sb("xpT", [P, 2, 2 * T], F32, r3 + 12288)
        sc_at = region(6144 + 3072)
        scores = sb("scores", [P, 2, 2, SK], F32, sc_at)
        probT = sb("probT", [P, 2, SK], F32, sc_at + 6144)
        g_rows = sb("g_rows", [4 * KD, P], F32, sc_at)
        xprob = sb("xprob", [P, XH, TT, T], F32, sc_at)
        h3T = sb("h3T", [P, KD, T], F32, sc_at)
        ones_r = sb("ones_r", [P, P], F32R, sc_at + 8192)
        below_r = sb("below_r", [P, P], F32R, sc_at + 8192 + 512)
        slot_at += [sc_at]
        slots = [sb(f"moe_slot{s}", [P, 2048], F32, a) for s, a in enumerate(slot_at)]
        assert len(slots) == SLOTS
        moe_x = sb("moe_x", [P, KD, P], F32, r1 + 8192)
        fin_row = sb("fin_row", [1, D], F32, r1 + 8192)
        sel = sb("sel", [P, TT, QE, WIN], F32, r1 + 12288)
        selw = sb("selw", [P, TT, QE, WIN], F32, r1 + 13312)
        selwT = sb("selwT", [P, T], F32, r1 + 14336)
        silu_g = sb("silu_g", [P, FE], F32, r1 + 15360)
        hid = sb("hid", [P, FE], F32, r2 + 16384)
        hidT = sb("hidT", [P, KF, P], F32, r2 + 17408)
        slot_of = sb("slot_of", [P, TT, ROUNDS, NE], F32, r3 + 8192)
        weight_of = sb("weight_of", [P, TT, ROUNDS, NE], F32, r3 + 10240)
        rt = r3 + 12288

        def small(name, shape, dt=F32):
            nonlocal rt
            n = 4
            for s in shape[1:]:
                n *= s
            rt += (n + 31) // 32 * 32
            assert rt <= r3 + 16384
            return nc.alloc_sbuf_tensor_at(name, shape, dt, offset=rt - (n + 31) // 32 * 32)

        logit = small("logit", [P, TT, NE])
        g_log = small("g_log", [P, TT, 8])
        g_top, e_top = small("g_top", [P, TT, 8]), small("e_top", [P, TT, 8])
        g_idx, e_idx = small("g_idx", [P, TT, 8], U32), small("e_idx", [P, TT, 8], U32)
        g_idf, e_idf = small("g_idf", [P, TT, 8]), small("e_idf", [P, TT, 8])
        g_exp, g_sum, g_neg = small("g_exp", [P, TT, 4]), small("g_sum", [P, TT]), small("g_neg", [P, TT])
        pen, e_log = small("pen", [P, TT, NG]), small("e_log", [P, TT, NG, EPG])
        e_neg, e2 = small("e_neg", [P, TT]), small("e2", [P, TT])
        den, ew = small("den", [P, TT]), small("ew", [P, 2, TT])
        first, both = small("first", [P, TT, NE]), small("both", [P, TT, NE], F32R)
        wfirst, wboth = small("wfirst", [P, TT, NE]), small("wboth", [P, TT, NE])
        posm = small("posm", [P, TT, NE])
        cmax, over, nover = small("cmax", [P, 1]), small("over", [P, 8]), small("nover", [P, 1])
        trips = small("trips", [P, 1], I32)
        ident = sb("ident", [P, P], F32)
        below = sb("below", [P, P], F32)
        ones = sb("ones", [P, P], F32)
        gains = sb("gains", [P, 4, KD], F32)
        dist_at = region(2 * SK * 4 + KD * (NG + NE) * 4)
        dist = sb("dist", [P, 2, SK], F32, dist_at)
        wr = sb("wr", [P, KD, NG + NE], F32, r3)
        wrg = sb("wrg", [P, KD, NG + NE], F32, dist_at + 2 * SK * 4)
        y_sb = sb("y_sb", [P, D], F32, dist_at)
        br, br_all = sb("br", [1, NG + NE], F32), sb("br_all", [P, NG + NE], F32)
        sink_row = sb("sink_row", [1, HEADS], F32)
        sinks, nsinks = sb("sinks", [P, HEADS], F32), sb("nsinks", [P, HEADS], F32)
        iota_e = sb("iota_e", [P, NE], F32)
        iota_rw = sb("iota_rw", [P, ROUNDS], F32)
        mean_sq = sb("mean_sq", [P, 4 + 1, TT, 2], F32)
        mean_eps, rnorm = (sb(n, [P, 4 + 1, TT], F32) for n in ("mean_eps", "rnorm"))
        xscale = sb("xscale", [P, TT], F32)
        mhalf = sb("mhalf", [P, TT], F32)
        nmax = sb("nmax", [P, 2, 2, 2], F32)
        rsum, rinv = sb("rsum", [P, 2, 4], F32), sb("rinv", [P, 2, 4], F32)
        sink_arg, sink_exp = sb("sink_arg", [P, 2, 4], F32), sb("sink_exp", [P, 2, 4], F32)
        xmax, xnmax = sb("xmax", [P, XH, TT], F32), sb("xnmax", [P, XH, TT], F32)
        xsum, xinv = sb("xsum", [P, XH, TT], F32), sb("xinv", [P, XH, TT], F32)

        PJ, SC, PT, PO = ([ctx.enter_context(nc.psum_tensor(f"{n}{i}", [P, 512], F32)) for i in range(2)]
                          for n in ("proj", "score", "probt", "attno"))

        LOGIT, LISTED, COUNTS = PO[0], PO[1], PJ[1]
        FIN_BANKS = (PJ[0], PT[1])
        NT_BANKS = (SC[0], SC[1], PT[0], PT[1])
        NT_BANKS3 = (SC[0], SC[1], PT[1], PO[1])

        def sem(name):
            return ctx.enter_context(nc.semaphore(name))

        x_in = [sem(f"x_in{t}") for t in range(TT)]
        mem_in, gain_in, small_in, fin_in = (sem(n) for n in ("mem_in", "gain_in", "small_in", "fin_in"))
        w_in_sem = [sem(f"w_loaded{i}") for i in range(NW)]
        moe_in = [sem(f"moe_loaded{i}") for i in range(SLOTS)]
        c_ident, c_ones, c_misc, c_gain, c_sink_ps, c_sink = (
            sem(n) for n in ("c_ident", "c_ones", "c_misc", "c_gain", "c_sink_ps", "c_sink"))
        c_gain_ps = sem("c_gain_ps")
        hi_done, lo_done, half_done, ev_act, ev_dve = (
            sem(n) for n in ("hi_done", "lo_done", "half_done", "ev_act", "ev_dve"))
        sq_done, ms_done, rs_done, xn_done = (sem(n) for n in ("sq_done", "ms_done", "rs_done", "xn_done"))
        nt_ps, nt_hi, nt_lo = (sem(n) for n in ("nt_ps", "nt_hi", "nt_lo"))
        s_ps, s_bias, s_max, s_exp, s_inv, s_norm, pt_ps, pt_sb, pv_ps, mix_hi, mix_lo = (
            sem(n) for n in ("s_ps", "s_bias", "s_max", "s_exp", "s_inv", "s_norm", "pt_ps", "pt_sb", "pv_ps",
                             "mix_hi", "mix_lo"))
        sig_done, mg_part, mg_sum, mg_hi, mg_lo = (
            sem(n) for n in ("sig_done", "mg_part", "mg_sum", "mg_hi", "mg_lo"))
        xscale_set = sem("xscale_set")
        xs_ps, xs_max, xs_exp, xs_inv, xs_norm, xpt_ps, xpt_act, xpt_dve, xpv_ps, ox_hi, ox_lo = (
            sem(n) for n in ("xs_ps", "xs_max", "xs_exp", "xs_inv", "xs_norm", "xpt_ps", "xpt_act", "xpt_dve",
                             "xpv_ps", "ox_hi", "ox_lo"))
        h3_act, h3_dve, r_ew, r_weight, r_posm, r_rest, w_step, logits_ps = (
            sem(n) for n in ("h3_act", "h3_dve", "r_ew", "r_weight", "r_posm", "r_rest", "w_step", "logits_ps"))
        r_step, r_top, r_exp, r_mask, pos_ps, trips_set, fin_ps, fin_sb = (
            sem(n) for n in ("r_step", "r_top", "r_exp", "r_mask", "pos_ps", "trips_set", "fin_ps", "fin_sb"))
        sel_made, gather_ps, moe_x_sb, selT_ps, selT_sb, chunk_used, silu_done, hid_done = (
            sem(n) for n in ("sel_made", "gather_ps", "moe_x_sb", "selT_ps", "selT_sb", "chunk_used",
                             "silu_done", "hid_done"))
        hidT_ps, hidT_sb, y_act, y_dve, back_ps = (
            sem(n) for n in ("hidT_ps", "hidT_sb", "y_act", "y_dve", "back_ps"))
        added = [[sem(f"added{t}{half}") for half in range(2)] for t in range(TT)]
        fin_xg, fin_act, fin_dve, out_done = (sem(n) for n in ("fin_xg", "fin_act", "fin_dve", "out_done"))

        block = ctx.enter_context(nc.Block())

        MEM_NORM, X2_NORM, X3_NORM = 1, 2, 3
        V1 = last["vx"]

        def sq_count(n, t):
            return 4 * n + (2 * t + 2 if n in (0, MEM_NORM) else t + 3)

        STEPS = HEADS + 3
        FIRST_UNDER = 6
        XS_BANKS = (SC[0], SC[1], PO[0], PO[1])
        UNITS = 2 * PAIRS

        def s_max_count(j):
            return 2 * min(j + 1, PAIRS) + 4 * max(j + 1 - PAIRS, 0)

        def s_exp_count(j):
            return 4 * min(j + 1, PAIRS) + 5 * max(j + 1 - PAIRS, 0)

        @block.sync
        def _(sp):
            for t in range(TT):
                sp.dma_start(xres[:, t], x[0, t * P:(t + 1) * P, :]).then_inc(x_in[t], 16)
            for i, g in enumerate((mix_norm_g, mem_norm_g, xattn_norm_g, ffn_norm_g)):
                sp.dma_start(g_rows[i * KD:(i + 1) * KD, :], g[0].rearrange("(k p) -> k p", p=P)).then_inc(gain_in, 16)

            def load_half(g):
                if g >= NW:
                    sp.wait_ge(lo_done, g - NW + 1)
                sp.dma_start(w_raw[:, g % NW], halves[g]).then_inc(w_in_sem[g % NW], 16)

            def load_experts(i, body):
                q, c = divmod(i, MOE_CHUNKS)
                s, e0 = slot_of_chunk(i), (body * BODY_QUADS + q) * QE
                if c < GU_CHUNKS:
                    dst = slots[s][:].rearrange("p (e j f) -> p e j f", e=QE, j=2)
                    sp.dma_start(dst[:, :, 0], wg_v[c, :, bass.ds(e0, QE), :]).then_inc(moe_in[s], 16)
                    sp.dma_start(dst[:, :, 1], wu_v[c, :, bass.ds(e0, QE), :]).then_inc(moe_in[s], 16)
                else:
                    half, kt = divmod(c - GU_CHUNKS, 2)
                    dst = slots[s][:].rearrange("p (e d) -> p e d", e=QE)
                    for e in range(0, QE, 2):
                        sp.dma_start(dst[:, e:e + 2], wd_v[kt, :, bass.ds(e0 + e, 2), half * 512:(half + 1) * 512])\
                            .then_inc(moe_in[s], 16)

            for g in range(NW):
                load_half(g)
            sp.dma_start(mem_raw[:], mem[0].rearrange("(t p) d -> p t d", p=P)).then_inc(mem_in, 16)
            prefetched = 0
            for g in range(NW, NH):
                load_half(g)
                if g >= 12 and g % 3 == 0 and prefetched < 8:
                    load_experts(prefetched, 0)
                    prefetched += 1
                if prefetched == 8 and g > 2 * at["kx"] + 1:
                    sp.wait_ge(xn_done, 2 * (MEM_NORM + 1))
                    load_experts(8, 0)
                    prefetched = 9
                if g in (2 * V1 + 3, 2 * V1 + 4):
                    sp.wait_ge(half_done, 2 * last["qx"] + 2)
                    load_experts(prefetched, 0)
                    prefetched += 1
            assert prefetched == 11
            sp.wait_ge(half_done, 2 * V1 + 2)
            load_experts(11, 0)
            load_experts(12, 0)
            sp.wait_ge(xs_ps, XH)
            load_experts(13, 0)
            sp.wait_ge(lo_done, NH - 1)
            load_experts(14, 0)
            sp.wait_ge(half_done, NH)
            sp.dma_start(fin_row[:], final_norm_g.rearrange("(a n) -> a n", a=1)).then_inc(fin_in, 16)
            for i in range(15, 19):
                load_experts(i, 0)
            sp.wait_ge(logits_ps, 1)
            load_experts(19, 0)
            for i in range(SLOTS, BODY_CHUNKS):
                sp.wait_ge(chunk_used, previous_user(i) + 1)
                load_experts(i, 0)
            sp.wait_ge(trips_set, 1)
            total = sp.value_load(trips[0:1, 0:1], min_val=BODIES, max_val=BODIES * ROUNDS)
            with sp.Fori(1, total) as body:
                for i in range(BODY_CHUNKS):
                    sp.wait_ge(chunk_used, body * BODY_CHUNKS + previous_user(i) + 1)
                    load_experts(i, body % BODIES)
            for t in range(TT):
                for half, scaled in ((1, fin_dve), (0, fin_act)):
                    cols = slice(half * 512, (half + 1) * 512)
                    sp.wait_ge(scaled, t + 1)
                    sp.dma_start(out[0, t * P:(t + 1) * P, cols], xn[:, t, cols]).then_inc(out_done, 16)
            sp.wait_ge(out_done, 16 * 2 * TT)

        @block.gpsimd
        def _(pool):
            pool.memset(ident[:], 0.0).then_inc(c_misc, 1)
            pool.memset(ones[:], 1.0).then_inc(c_ones, 1)
            pool.wait_ge(c_misc, 1)
            pool.affine_select(out=ident[:], in_=ident[:], compare_op=ALU.not_equal, fill=1.0, base=0,
                               pattern=[[-1, P]], channel_multiplier=1).then_inc(c_ident, 1)
            pool.memset(mhalf[:], -0.5).then_inc(c_misc, 1)
            for kind in range(2):
                pool.iota(dist[:, kind, 0:P], [[1, P]], base=0, channel_multiplier=-1,
                          allow_small_or_imprecise_dtypes=True).then_inc(c_misc, 1)
                pool.iota(dist[:, kind, P:SK], [[1, T]], base=-P, channel_multiplier=-1,
                          allow_small_or_imprecise_dtypes=True).then_inc(c_misc, 1)
            pool.wait_ge(c_misc, 6)
            for kind in range(2):
                pool.affine_select(out=dist[:, kind, 0:P], in_=dist[:, kind, 0:P], compare_op=ALU.is_ge,
                                   fill=NEG, base=0, pattern=[[-1, P]], channel_multiplier=1).then_inc(c_misc, 1)
                pool.affine_select(out=dist[:, kind, P:SK], in_=dist[:, kind, P:SK], compare_op=ALU.is_ge,
                                   fill=NEG, base=P, pattern=[[-1, T]], channel_multiplier=1).then_inc(c_misc, 1)
            pool.wait_ge(c_misc, 10)
            pool.affine_select(out=dist[:, 1, P:SK], in_=dist[:, 1, P:SK], compare_op=ALU.is_gt, fill=NEG,
                               base=WINDOW - P, pattern=[[1, T]], channel_multiplier=-1).then_inc(c_misc, 1)
            pool.iota(iota_e[:], [[1, NE]], base=0, channel_multiplier=0,
                      allow_small_or_imprecise_dtypes=True).then_inc(c_misc, 1)
            pool.iota(iota_rw[:], [[WIN, ROUNDS]], base=UNLISTED, channel_multiplier=0,
                      allow_small_or_imprecise_dtypes=True).then_inc(c_misc, 1)
            pool.wait_ge(c_ones, 1)
            pool.affine_select(out=below[:], in_=ones[:], compare_op=ALU.is_gt, fill=0.0, base=0,
                               pattern=[[1, P]], channel_multiplier=-1).then_inc(c_misc, 1)

            def inverse_root(n):
                for t in range(TT):
                    pool.wait_ge(ms_done, 2 * n + t + 1)
                    pool.tensor_tensor(rnorm[:, n, t:t + 1], mean_eps[:, n, t:t + 1], mhalf[:, 0:1], ALU.pow)\
                        .then_inc(rs_done, 1)

            inverse_root(0)
            pool.wait_ge(c_gain, 1)
            pool.wait_ge(small_in, 80)
            pool.tensor_tensor(wrg[:], wr[:], gains[:, X3_NORM].unsqueeze(2).broadcast_to([P, KD, NG + NE]),
                               ALU.mult).then_inc(c_misc, 1)
            inverse_root(MEM_NORM)
            for j in range(UNITS):
                pool.wait_ge(s_inv, j + 1)
                for tt in range(TT):
                    cols = slice(0, P) if tt == 0 else slice(P, SK)
                    for hh in range(2):
                        i = 2 * tt + hh
                        pool.tensor_scalar(scores[:, j % 2, hh, cols], scores[:, j % 2, hh, cols],
                                           rinv[:, j % 2, i:i + 1], 1.0, ALU.mult, ALU.mult).then_inc(s_norm, 1)
            inverse_root(X2_NORM)
            for h in range(XH):
                pool.wait_ge(xs_inv, h + 1)
                for tt in range(TT):
                    pool.tensor_scalar(xprob[:, h, tt], xprob[:, h, tt], xinv[:, h, tt:tt + 1], 1.0,
                                       ALU.mult, ALU.mult).then_inc(xs_norm, 1)
            pool.tensor_copy(ones_r[:], ones[:]).then_inc(c_misc, 1)
            pool.tensor_copy(below_r[:], below[:]).then_inc(c_misc, 1)
            inverse_root(X3_NORM)
            written = 0

            def then(op):
                nonlocal written
                op.then_inc(w_step, 1)
                written += 1
                pool.wait_ge(w_step, written)

            pool.wait_ge(r_ew, 1)
            for t in range(TT):
                pool.tensor_scalar(wfirst[:, t], iota_e[:], e_idf[:, t, 0:1], ew[:, 0, t:t + 1], ALU.is_equal,
                                   ALU.mult).then_inc(w_step, 1)
                written += 1
                then(pool.tensor_scalar(wboth[:, t], iota_e[:], e_idf[:, t, 1:2], ew[:, 1, t:t + 1], ALU.is_equal,
                                        ALU.mult))
                then(pool.tensor_tensor(wboth[:, t], wboth[:, t], wfirst[:, t], ALU.add))
                pool.tensor_copy(weight_of[:, t], wboth[:, t].unsqueeze(1).broadcast_to([P, ROUNDS, NE]))\
                    .then_inc(r_weight, 1)
            pool.wait_ge(r_posm, 1)
            for t in range(TT):
                pool.tensor_tensor(slot_of[:, t, 1:], posm[:, t].unsqueeze(1).broadcast_to([P, ROUNDS - 1, NE]),
                                   iota_rw[:, 1:].unsqueeze(2).broadcast_to([P, ROUNDS - 1, NE]), ALU.subtract)\
                    .then_inc(r_rest, 1)
            pool.wait_ge(trips_set, 1)
            total = pool.value_load(trips[0:1, 0:1], min_val=BODIES, max_val=BODIES * ROUNDS)
            pool.wait_ge(fin_sb, 2)
            for t in range(TT):
                pool.wait_ge(added[t][0], total * BODY_QUADS)
                pool.tensor_tensor(xn[:, t, 0:512], xres[:, t, 0:512], fin_g[:, 0:512], ALU.mult).then_inc(fin_xg, 1)
            inverse_root(4)

        @block.scalar
        def _(act):
            act.wait_ge(c_misc, 2)
            act.activation(xscale[:, 0:1], mhalf[:, 0:1], ACT.Square)
            act.dma_start(sink_row[:], swa_sinks).then_inc(small_in, 16)
            act.dma_start(br[:, 0:NG], router_group_b).then_inc(small_in, 16)
            act.dma_start(br[:, NG:NG + NE], router_expert_b).then_inc(small_in, 16)
            act.dma_start(wr[:, :, 0:NG], router_group_w[0].rearrange("(k p) n -> p k n", p=P)).then_inc(small_in, 16)
            act.dma_start(wr[:, :, NG:NG + NE], router_expert_w[0].rearrange("(k p) n -> p k n", p=P))\
                .then_inc(small_in, 16)

            def squares(n, src, t, half, junk=None):
                cols = slice(half * 512, (half + 1) * 512)
                act.activation(xn[:, t, cols] if junk is None else junk, src[:, t, cols], ACT.Square,
                               scale=float(D) ** -0.5, accum_out=mean_sq[:, n, t, half:half + 1]).then_inc(sq_done, 1)

            def unit_hi(n, hi, u):
                act.wait_ge(nt_ps, 4 * n + u + 1)
                for i in range(2):
                    k = 2 * u + i
                    op = act.activation(hi[:, k], NT_BANKS[u][:, i * T:(i + 1) * T], ACT.Copy,
                                        scale=gains[:, n, k:k + 1])
                op.then_inc(nt_hi, 1)

            def split_hi(g):
                if g >= NH:
                    return
                act.wait_ge(w_in_sem[g % NW], 16 * (g // NW + 1))
                if g >= NS:
                    act.wait_ge(half_done, g - NS + 1)
                act.activation(w_hi[:, g % NS], w_raw[:, g % NW], ACT.Copy).then_inc(hi_done, 1)

            def evacuate(c):
                k, i, src = kinds[c], kinds[:c].count(kinds[c]), PJ[c % 2]
                two = src[:].rearrange("p (a n) -> p a n", a=2)
                act.wait_ge(half_done, 2 * c + 2)
                if k == "qa":
                    op = act.activation(qa[:, 2 * i:2 * i + 2], two, ACT.Copy, scale=float(HD) ** -0.5)
                elif k == "qb":
                    op = act.activation(qb[:, 2 * i:2 * i + 2], two, ACT.Copy, scale=float(HD) ** -0.5)
                elif k == "ka":
                    op = act.activation(ka[:, 2 * i:2 * i + 2], two, ACT.Copy)
                elif k == "va":
                    op = act.activation(va[:, :, i * CW:(i + 1) * CW], two, ACT.Copy)
                elif k == "kvb":
                    for g in range(2):
                        for half in range(2):
                            act.activation(kb2[half * HD:(half + 1) * HD, g], src[g * HD:(g + 1) * HD, 0:T], ACT.Copy)
                    op = act.activation(vb[:], src[:, T:2 * T].rearrange("p (t d) -> p t d", t=TT), ACT.Copy)
                elif k == "gate":
                    if i == 0:
                        act.wait_ge(c_misc, 15)
                    op = act.activation(gates[:, 2 * i:2 * i + 2], two, ACT.Copy)
                elif k == "kx":
                    op = act.activation(kx[:, 2 * i:2 * i + 2], two, ACT.Copy)
                elif k == "qx":
                    op = act.activation(qx[:, 2 * i:2 * i + 2], two, ACT.Copy)
                else:
                    op = act.activation(vx[:, :, i * CW:(i + 1) * CW], two, ACT.Copy)
                op.then_inc(ev_act, 1)

            def exponentials(j):
                b = j % 2
                act.wait_ge(s_max, s_max_count(j))
                for tt in range(TT):
                    cols = slice(0, P) if tt == 0 else slice(P, SK)
                    for hh in range(2):
                        i = 2 * tt + hh
                        act.activation(scores[:, b, hh, cols], scores[:, b, hh, cols], ACT.Exp,
                                       bias=nmax[:, b, tt, hh:hh + 1], accum_out=rsum[:, b, i:i + 1]).then_inc(s_exp, 1)
                if j >= PAIRS:
                    act.activation(sink_exp[:, b], sink_arg[:, b], ACT.Exp).then_inc(s_exp, 1)

            def prob_out(j):
                act.wait_ge(pt_ps, j + 1)
                if j:
                    act.wait_ge(pv_ps, j)
                for hh in range(2):
                    act.activation(probT[:, hh], PT[hh][:, 0:SK], ACT.Copy).then_inc(pt_sb, 1)

            def mix_out_hi(j):
                act.wait_ge(pv_ps, j + 1)
                act.activation(mixT_hi[:, j], PO[j % 2][:, 0:T], ACT.Copy).then_inc(mix_hi, 1)

            for t in range(TT):
                act.wait_ge(x_in[t], 16)
                squares(0, xres, t, 0)
                squares(0, xres, t, 1)
            split_hi(0)
            act.wait_ge(c_gain, 1)
            unit_hi(0, hT_hi, 0)
            unit_hi(0, hT_hi, 1)
            split_hi(1)
            unit_hi(0, hT_hi, 2)
            unit_hi(0, hT_hi, 3)
            for c in range(FIRST_UNDER):
                split_hi(2 * c + 2)
                split_hi(2 * c + 3)
                evacuate(c)
                if c == 0:
                    act.wait_ge(mem_in, 16)
                    for t in range(TT):
                        squares(MEM_NORM, mem_raw, t, 0)
                        squares(MEM_NORM, mem_raw, t, 1)
            for i in range(STEPS):
                c = FIRST_UNDER + i
                split_hi(2 * c + 2)
                if i < UNITS:
                    exponentials(i)
                split_hi(2 * c + 3)
                evacuate(c)
                if 1 <= i <= UNITS:
                    prob_out(i - 1)
                if 2 <= i <= UNITS + 1:
                    mix_out_hi(i - 2)
            def sigmoids(m):
                for g in (0, KD):
                    act.activation(gates[:, g + 2 * m:g + 2 * m + 2], gates[:, g + 2 * m:g + 2 * m + 2],
                                   ACT.Sigmoid).then_inc(sig_done, 1)

            for u in range(4):
                unit_hi(MEM_NORM, memT_hi, u)
            act.wait_ge(ev_act, evac_count(last["gate"]))
            sigmoids(0)
            for m in range(4):
                c = at["merge"] + m
                split_hi(2 * c + 2)
                if m < 3:
                    sigmoids(m + 1)
                split_hi(2 * c + 3)
                act.wait_ge(mg_sum, m + 1)
                act.activation(mgT_hi[:, 2 * m:2 * m + 2], gates[:, 2 * m:2 * m + 2], ACT.Copy).then_inc(mg_hi, 1)

            def step(c):
                split_hi(2 * c + 2)
                split_hi(2 * c + 3)
                if kinds[c] not in ON_DVE:
                    evacuate(c)

            step(at["kx"])
            for m in range(4):
                step(at["mix"] + m)
                if m:
                    unit_hi(X2_NORM, h2T_hi, m - 1)
            step(last["kx"])
            unit_hi(X2_NORM, h2T_hi, 3)
            act.wait_ge(ev_dve, evac_count(last["mix"]))
            for half in range(2):
                for t in range(TT):
                    squares(X2_NORM, xres, t, half)
            step(at["vx"])
            step(at["qx"])
            step(last["qx"])

            def xexponentials(h):
                act.wait_ge(xs_max, 2 * h + 2)
                for tt in range(TT):
                    act.activation(xprob[:, h, tt], XS_BANKS[h][:, tt * T:(tt + 1) * T], ACT.Exp,
                                   scale=xscale[:, tt:tt + 1], bias=xnmax[:, h, tt:tt + 1],
                                   accum_out=xsum[:, h, tt:tt + 1]).then_inc(xs_exp, 1)

            xexponentials(0)
            split_hi(2 * V1 + 2)
            xexponentials(1)
            xexponentials(2)
            split_hi(2 * V1 + 3)
            xexponentials(3)
            evacuate(V1)

            def ox_out_hi(h):
                act.wait_ge(xpv_ps, h + 1)
                act.activation(oxT_hi[:, h], PO[h % 2][:, 0:T], ACT.Copy).then_inc(ox_hi, 1)

            for h in range(XH):
                if h % 2 == 0:
                    act.wait_ge(xpt_ps, h + 1)
                    if h:
                        act.wait_ge(xpv_ps, h - 1)
                    act.activation(xpT[:, 0], PT[0][:], ACT.Copy).then_inc(xpt_act, 1)
                if h:
                    ox_out_hi(h - 1)
            ox_out_hi(XH - 1)
            split_hi(2 * V1 + 4)
            split_hi(2 * V1 + 5)

            def h3_out(u):
                act.wait_ge(nt_ps, 4 * X3_NORM + u + 1)
                act.activation(h3T[:, 2 * u:2 * u + 2], NT_BANKS3[u][:].rearrange("p (k q) -> p k q", k=2),
                               ACT.Copy).then_inc(h3_act, 1)

            h3_out(0)
            act.wait_ge(ev_dve, evac_count(NC - 1) - 2)
            for t in range(TT):
                squares(X3_NORM, xres, t, 0)
            h3_out(2)
            act.wait_ge(ev_dve, evac_count(NC - 1))
            for t in range(TT):
                squares(X3_NORM, xres, t, 1)

            for t in range(TT):
                act.wait_ge(r_top, t + 1)
                act.activation(g_exp[:, t], g_log[:, t, 0:NG], ACT.Exp, bias=g_neg[:, t:t + 1],
                               accum_out=g_sum[:, t:t + 1]).then_inc(r_exp, 1)
            for t in range(TT):
                act.wait_ge(r_top, TT + t + 1)
                act.activation(e2[:, t:t + 1], e_top[:, t, 1:2], ACT.Exp, bias=e_neg[:, t:t + 1]).then_inc(r_exp, 1)
            act.wait_ge(fin_ps, 1)
            for half in range(2):
                act.activation(fin_g[:, half * 512:(half + 1) * 512], FIN_BANKS[half][:], ACT.Copy).then_inc(fin_sb, 1)

            act.wait_ge(trips_set, 1)
            total = act.value_load(trips[0:1, 0:1], min_val=BODIES, max_val=BODIES * ROUNDS)
            with act.Fori(0, total) as body:
                for q in range(BODY_QUADS):
                    n = body * BODY_QUADS + q
                    act.wait_ge(chunk_used, n * MOE_CHUNKS + GU_CHUNKS)
                    act.activation(silu_g[:], PJ[0][:, 0:FE], ACT.Silu).then_inc(silu_done, 1)
                    act.wait_ge(hidT_ps, n + 1)
                    act.activation(hidT[:], PT[0][:, 0:KF * P].rearrange("p (k s) -> p k s", k=KF), ACT.Copy)\
                        .then_inc(hidT_sb, 1)
                    act.wait_ge(chunk_used, n * MOE_CHUNKS + GU_CHUNKS + KF)
                    act.activation(y_sb[:, 0:512], SC[0][:], ACT.Copy).then_inc(y_act, 1)
            for half in range(2):
                for t in range(TT):
                    act.wait_ge(added[t][half], total * BODY_QUADS)
                    squares(4, xres, t, half, None if half else moe_x[:, 4 * t:4 * t + 4].rearrange("p k s -> p (k s)"))
            for t in range(TT):
                act.wait_ge(fin_xg, t + 1)
                act.wait_ge(rs_done, 2 * 4 + t + 1)
                act.activation(xn[:, t, 0:512], xn[:, t, 0:512], ACT.Copy, scale=rnorm[:, 4, t:t + 1])\
                    .then_inc(fin_act, 1)

        @block.vector
        def _(dve):
            def means(n, t):
                dve.wait_ge(sq_done, sq_count(n, t))
                dve.tensor_scalar(mean_eps[:, n, t:t + 1], mean_sq[:, n, t, 0:1], mean_sq[:, n, t, 1:2], EPS,
                                  ALU.add, ALU.add).then_inc(ms_done, 1)

            def normalise(n, src):
                for t in range(TT):
                    means(n, t)
                for t in range(TT):
                    dve.wait_ge(rs_done, 2 * n + t + 1)
                    dve.tensor_scalar(xn[:, t], src[:, t], rnorm[:, n, t:t + 1], None, ALU.mult).then_inc(xn_done, 1)

            def unit_lo(n, hi, lo, u):
                dve.wait_ge(nt_hi, 4 * n + u + 1)
                for i in range(2):
                    k = 2 * u + i
                    op = dve.scalar_tensor_tensor(out=lo[:, k], in0=NT_BANKS[u][:, i * T:(i + 1) * T],
                                                  scalar=gains[:, n, k:k + 1], in1=hi[:, k].bitcast(F32),
                                                  op0=ALU.mult, op1=ALU.subtract)
                op.then_inc(nt_lo, 1)

            def split_lo(g):
                if g >= NH:
                    return
                dve.wait_ge(hi_done, g + 1)
                dve.tensor_tensor(w_lo[:, g % NS], w_raw[:, g % NW], w_hi[:, g % NS].bitcast(F32), ALU.subtract)\
                    .then_inc(lo_done, 1)

            def bias_and_max(j):
                b, swa = j % 2, j >= PAIRS
                dve.wait_ge(s_ps, j + 1)
                if j >= 2:
                    dve.wait_ge(pt_ps, j - 1)
                for hh in range(2):
                    h = 2 * (j % PAIRS) + hh
                    dve.scalar_tensor_tensor(out=scores[:, b, hh], in0=dist[:, int(swa)], scalar=2.0 ** -(h + 1),
                                             in1=SC[hh][:, 0:SK], op0=ALU.mult, op1=ALU.add).then_inc(s_bias, 1)
                dve.wait_ge(s_bias, 2 * j + 2)
                for tt in range(TT):
                    cols = slice(0, P) if tt == 0 else slice(P, SK)
                    dve.tensor_reduce(nmax[:, b, tt], scores[:, b, :, cols], axis=AX.X, op=ALU.max,
                                      negate=True).then_inc(s_max, 1)
                if swa:
                    h = 2 * (j % PAIRS)
                    count = s_max_count(j)
                    dve.wait_ge(s_max, count - 2)
                    dve.tensor_tensor(nmax[:, b], nmax[:, b], nsinks[:, h:h + 2].unsqueeze(1).broadcast_to([P, 2, 2]),
                                      ALU.min).then_inc(s_max, 1)
                    dve.wait_ge(s_max, count - 1)
                    dve.tensor_tensor(sink_arg[:, b].rearrange("p (t h) -> p t h", t=2), nmax[:, b],
                                      sinks[:, h:h + 2].unsqueeze(1).broadcast_to([P, 2, 2]), ALU.add)\
                        .then_inc(s_max, 1)

            sunk = [0]

            def inverse_sums(j):
                b = j % 2
                dve.wait_ge(s_exp, s_exp_count(j))
                if j >= PAIRS:
                    dve.tensor_tensor(rsum[:, b], rsum[:, b], sink_exp[:, b], ALU.add).then_inc(c_sink, 1)
                    sunk[0] += 1
                    dve.wait_ge(c_sink, 1 + sunk[0])
                dve.reciprocal(rinv[:, b], rsum[:, b]).then_inc(s_inv, 1)

            def mix_out_lo(j):
                dve.wait_ge(mix_hi, j + 1)
                dve.tensor_tensor(mixT_lo[:, j], PO[j % 2][:, 0:T], mixT_hi[:, j].bitcast(F32), ALU.subtract)\
                    .then_inc(mix_lo, 1)

            normalise(0, xres)
            dve.wait_ge(c_gain_ps, 1)
            dve.tensor_copy(gains[:], PO[0][:, 0:4 * KD].rearrange("p (n k) -> p n k", n=4)).then_inc(c_gain, 1)
            split_lo(0)
            dve.wait_ge(c_gain, 1)
            unit_lo(0, hT_hi, hT_lo, 0)
            unit_lo(0, hT_hi, hT_lo, 1)
            split_lo(1)
            unit_lo(0, hT_hi, hT_lo, 2)
            unit_lo(0, hT_hi, hT_lo, 3)
            dve.wait_ge(c_sink_ps, 1)
            dve.tensor_copy(sinks[:], PO[1][:, 0:HEADS]).then_inc(c_sink, 1)
            dve.tensor_scalar(nsinks[:], PO[1][:, 0:HEADS], -1.0, None, ALU.mult).then_inc(c_gain, 1)
            dve.tensor_copy(br_all[:], PO[1][:, HEADS:HEADS + NG + NE]).then_inc(c_gain, 1)
            dve.wait_ge(c_sink, 1)
            dve.wait_ge(c_gain, 3)
            for c in range(FIRST_UNDER):
                split_lo(2 * c + 2)
                split_lo(2 * c + 3)
                if c == 1:
                    normalise(MEM_NORM, mem_raw)
            dve.wait_ge(c_misc, 15)
            for i in range(STEPS):
                c = FIRST_UNDER + i
                if i < UNITS:
                    bias_and_max(i)
                split_lo(2 * c + 2)
                if i < UNITS:
                    inverse_sums(i)
                split_lo(2 * c + 3)
                if 2 <= i <= UNITS + 1:
                    mix_out_lo(i - 2)
            for u in range(4):
                unit_lo(MEM_NORM, memT_hi, memT_lo, u)
            def merged_lo(m):
                dve.wait_ge(mg_hi, m + 1)
                dve.tensor_tensor(mgT_lo[:, 2 * m:2 * m + 2], gates[:, 2 * m:2 * m + 2],
                                  mgT_hi[:, 2 * m:2 * m + 2].bitcast(F32), ALU.subtract).then_inc(mg_lo, 1)

            for m in range(4):
                c = at["merge"] + m
                split_lo(2 * c + 2)
                ga, gb = gates[:, 2 * m:2 * m + 2], gates[:, KD + 2 * m:KD + 2 * m + 2]
                dve.wait_ge(half_done, 2 * c + 1)
                dve.wait_ge(sig_done, 2 * m + 2)
                dve.tensor_tensor(ga, ga, PJ[c % 2][:].rearrange("p (a n) -> p a n", a=2), ALU.mult)\
                    .then_inc(mg_part, 1)
                if m:
                    merged_lo(m - 1)
                split_lo(2 * c + 3)
                dve.wait_ge(half_done, 2 * c + 2)
                dve.tensor_tensor(gb, gb, PT[c % 2][:].rearrange("p (a n) -> p a n", a=2), ALU.mult)\
                    .then_inc(ev_dve, 1)
                dve.wait_ge(mg_part, m + 1)
                dve.wait_ge(ev_dve, evac_count(c))
                dve.tensor_tensor(ga, ga, gb, ALU.add).then_inc(mg_sum, 1)
            merged_lo(3)

            def add_residual(src, col):
                dst = xres[:, :, col:col + CW]
                dve.tensor_tensor(dst, dst, src[:].rearrange("p (t n) -> p t n", t=TT), ALU.add).then_inc(ev_dve, 1)

            def step(c):
                split_lo(2 * c + 2)
                split_lo(2 * c + 3)

            step(at["kx"])
            for c in range(at["mix"], last["mix"] + 1):
                step(c)
                dve.wait_ge(half_done, 2 * c + 2)
                add_residual(PJ[c % 2], (c - at["mix"]) * CW)
                if c > at["mix"]:
                    unit_lo(X2_NORM, h2T_hi, h2T_lo, c - at["mix"] - 1)
            step(last["kx"])
            unit_lo(X2_NORM, h2T_hi, h2T_lo, 3)
            step(at["vx"])
            for t in range(TT):
                means(X2_NORM, t)
            step(at["qx"])
            dve.wait_ge(rs_done, 2 * (X2_NORM + 1))
            dve.tensor_scalar(xscale[:], rnorm[:, X2_NORM], XSCALE, None, ALU.mult).then_inc(xscale_set, 1)
            step(last["qx"])
            dve.wait_ge(xscale_set, 1)

            def x_maxima(h):
                dve.wait_ge(xs_ps, h + 1)
                dve.tensor_reduce(xmax[:, h], XS_BANKS[h][:].rearrange("p (t m) -> p t m", t=TT), axis=AX.X,
                                  op=ALU.max).then_inc(xs_max, 1)
                dve.wait_ge(xs_max, 2 * h + 1)
                dve.scalar_tensor_tensor(out=xnmax[:, h], in0=xmax[:, h], scalar=-1.0, in1=xscale[:], op0=ALU.mult,
                                         op1=ALU.mult).then_inc(xs_max, 1)

            def x_inverse_sums(h):
                dve.wait_ge(xs_exp, 2 * h + 2)
                dve.reciprocal(xinv[:, h], xsum[:, h]).then_inc(xs_inv, 1)

            x_maxima(0)
            x_maxima(1)
            split_lo(2 * V1 + 2)
            x_maxima(2)
            x_inverse_sums(0)
            x_maxima(3)
            x_inverse_sums(1)
            x_inverse_sums(2)
            split_lo(2 * V1 + 3)
            x_inverse_sums(3)

            def ox_out_lo(h):
                dve.wait_ge(ox_hi, h + 1)
                dve.tensor_tensor(oxT_lo[:, h], PO[h % 2][:, 0:T], oxT_hi[:, h].bitcast(F32), ALU.subtract)\
                    .then_inc(ox_lo, 1)

            for h in range(XH):
                if h % 2:
                    dve.wait_ge(xpt_ps, h + 1)
                    if h > 1:
                        dve.wait_ge(xpv_ps, h - 1)
                    dve.tensor_copy(xpT[:, 1], PT[1][:]).then_inc(xpt_dve, 1)
                    ox_out_lo(h - 1)
                elif h:
                    ox_out_lo(h - 1)
            ox_out_lo(XH - 1)
            split_lo(2 * V1 + 4)
            split_lo(2 * V1 + 5)

            def h3_out(u):
                dve.wait_ge(nt_ps, 4 * X3_NORM + u + 1)
                dve.tensor_copy(h3T[:, 2 * u:2 * u + 2], NT_BANKS3[u][:].rearrange("p (k q) -> p k q", k=2))\
                    .then_inc(h3_dve, 1)

            for m in range(4):
                c, half = at["xo"] + m // 2, m % 2
                dve.wait_ge(half_done, 2 * c + half + 1)
                add_residual((PT if half else PJ)[c % 2], m * CW)
                if m == 2:
                    h3_out(1)
            h3_out(3)
            for t in range(TT):
                means(X3_NORM, t)

            steps, done = [0], [0] * TT

            def mark(ts, op):
                op.then_inc(r_step, 1)
                steps[0] += 1
                for t in ts:
                    done[t] = steps[0]

            def after(ts):
                dve.wait_ge(r_step, max(done[t] for t in ts))

            both_tiles = range(TT)
            mark(both_tiles, dve.memset(g_log[:], BIG))
            after(both_tiles)
            dve.wait_ge(rs_done, 2 * (X3_NORM + 1))
            dve.wait_ge(logits_ps, 1)
            for t in range(TT):
                mark([t], dve.scalar_tensor_tensor(out=g_log[:, t, 0:NG], in0=LOGIT[:, t * 64:t * 64 + NG],
                                                   scalar=rnorm[:, X3_NORM, t:t + 1], in1=br_all[:, 0:NG],
                                                   op0=ALU.mult, op1=ALU.add))
            for t in range(TT):
                after([t])
                mark([t], dve.max(g_top[:, t], g_log[:, t]))
            for t in range(TT):
                dve.scalar_tensor_tensor(out=logit[:, t], in0=LOGIT[:, t * 64 + NG:t * 64 + NG + NE],
                                         scalar=rnorm[:, X3_NORM, t:t + 1], in1=br_all[:, NG:NG + NE],
                                         op0=ALU.mult, op1=ALU.add)
            for t in range(TT):
                after([t])
                mark([t], dve.max_index(g_idx[:, t], g_top[:, t], g_log[:, t]))
            for t in range(TT):
                dve.tensor_scalar(g_neg[:, t:t + 1], g_top[:, t, 0:1], -1.0, None, ALU.mult).then_inc(r_top, 1)
            after(both_tiles)
            mark(both_tiles, dve.tensor_copy(g_idf[:], g_idx[:]))
            after(both_tiles)
            for t in range(TT):
                mark(both_tiles, dve.tensor_scalar(pen[:, t], iota_e[:, 0:NG], g_idf[:, t, 0:1], BIG,
                                                   ALU.not_equal, ALU.mult))
            after(both_tiles)
            mark(both_tiles, dve.tensor_tensor(e_log[:], logit[:].rearrange("p t (g e) -> p t g e", g=NG),
                                               pen[:].unsqueeze(3).broadcast_to([P, TT, NG, EPG]), ALU.add))
            after(both_tiles)
            for t in range(TT):
                mark([t], dve.max(e_top[:, t], e_log[:, t].rearrange("p g e -> p (g e)")))
            for t in range(TT):
                after([t])
                mark([t], dve.max_index(e_idx[:, t], e_top[:, t], e_log[:, t].rearrange("p g e -> p (g e)")))
            for t in range(TT):
                dve.tensor_scalar(e_neg[:, t:t + 1], e_top[:, t, 0:1], -1.0, None, ALU.mult).then_inc(r_top, 1)
            after(both_tiles)
            mark(both_tiles, dve.tensor_copy(e_idf[:], e_idx[:]))
            after(both_tiles)
            for t in range(TT):
                mark([t], dve.tensor_scalar(first[:, t], iota_e[:], e_idf[:, t, 0:1], None, ALU.is_equal))
            for t in range(TT):
                after([t])
                dve.scalar_tensor_tensor(out=both[:, t], in0=iota_e[:], scalar=e_idf[:, t, 1:2], in1=first[:, t],
                                         op0=ALU.is_equal, op1=ALU.add).then_inc(r_mask, 1)
            dve.wait_ge(r_exp, 2 * TT)
            mark(both_tiles, dve.scalar_tensor_tensor(out=den[:], in0=e2[:], scalar=1.0, in1=g_sum[:], op0=ALU.add,
                                                      op1=ALU.mult))
            after(both_tiles)
            mark(both_tiles, dve.reciprocal(ew[:, 0], den[:]))
            after(both_tiles)
            dve.tensor_tensor(ew[:, 1], ew[:, 0], e2[:], ALU.mult).then_inc(r_ew, 1)
            dve.tensor_scalar(xn[:, 0], xres[:, 0], rnorm[:, X3_NORM, 0:1], None, ALU.mult).then_inc(xn_done, 1)
            dve.wait_ge(pos_ps, 1)
            dve.scalar_tensor_tensor(out=posm[:], in0=LISTED[:, 0:TT * NE].rearrange("p (t e) -> p t e", t=TT),
                                     scalar=float(UNLISTED), in1=both[:].bitcast(F32), op0=ALU.add, op1=ALU.mult)\
                .then_inc(r_posm, 1)
            dve.wait_ge(pos_ps, 2)
            mark(both_tiles, dve.tensor_reduce(cmax[:], COUNTS[:, 0:NE], axis=AX.X, op=ALU.max))
            dve.wait_ge(r_posm, 1)
            dve.tensor_scalar(slot_of[:, :, 0], posm[:], -float(UNLISTED), None, ALU.add).then_inc(r_rest, 1)
            after(both_tiles)
            mark(both_tiles, dve.tensor_scalar(over[:, 0:ROUNDS - 1], iota_rw[:, 1:ROUNDS], cmax[:], float(UNLISTED),
                                               ALU.subtract, ALU.is_lt))
            after(both_tiles)
            mark(both_tiles, dve.tensor_reduce(nover[:], over[:, 0:ROUNDS - 1], axis=AX.X, op=ALU.add))
            after(both_tiles)
            dve.tensor_scalar(trips[:], nover[:], float(BODIES), float(BODIES), ALU.mult, ALU.add).then_inc(trips_set, 1)
            dve.tensor_scalar(xn[:, 1], xres[:, 1], rnorm[:, X3_NORM, 1:2], None, ALU.mult).then_inc(xn_done, 1)
            dve.wait_ge(r_rest, 1)

            dve.wait_ge(trips_set, 1)
            total = dve.value_load(trips[0:1, 0:1], min_val=BODIES, max_val=BODIES * ROUNDS)
            slots_flat = slot_of[:].rearrange("p t r e -> p t (r e)")
            weight_flat = weight_of[:].rearrange("p t r e -> p t (r e)")
            iota_s = iota_e[:, 0:WIN].unsqueeze(1).unsqueeze(1).broadcast_to([P, TT, QE, WIN])
            dve.wait_ge(c_gain, 3)
            with dve.Fori(0, total) as body:
                for q in range(BODY_QUADS):
                    n = body * BODY_QUADS + q
                    dve.tensor_tensor(sel[:], slots_flat[:, :, bass.ds(n * QE, QE)].unsqueeze(3)
                                      .broadcast_to([P, TT, QE, WIN]), iota_s, ALU.is_equal).then_inc(sel_made, 1)
                    for half in range(2):
                        dve.wait_ge(gather_ps, n * 2 + half + 1)
                        dve.tensor_tensor(moe_x[:, half * 4:half * 4 + 4],
                                          SC[half][:].rearrange("p (k s) -> p k s", k=4),
                                          gains[:, X3_NORM, half * 4:half * 4 + 4].unsqueeze(2)
                                          .broadcast_to([P, 4, P]), ALU.mult).then_inc(moe_x_sb, 1)
                    dve.wait_ge(sel_made, n * 2 + 1)
                    dve.wait_ge(r_weight, TT)
                    dve.wait_ge(r_rest, 1 + TT)
                    dve.tensor_tensor(selw[:], sel[:], weight_flat[:, :, bass.ds(n * QE, QE)].unsqueeze(3)
                                      .broadcast_to([P, TT, QE, WIN]), ALU.mult).then_inc(sel_made, 1)
                    dve.wait_ge(silu_done, n + 1)
                    dve.tensor_tensor(hid[:], silu_g[:], PJ[0][:, FE:2 * FE], ALU.mult).then_inc(hid_done, 1)
                    dve.wait_ge(selT_ps, n + 1)
                    dve.tensor_copy(selwT[:], PT[1][:, 0:T]).then_inc(selT_sb, 1)
                    for half in range(2):
                        cols = slice(half * 512, (half + 1) * 512)
                        if half:
                            dve.wait_ge(chunk_used, n * MOE_CHUNKS + MOE_CHUNKS)
                            dve.tensor_copy(y_sb[:, cols], SC[1][:]).then_inc(y_dve, 1)
                        for t in range(TT):
                            dve.wait_ge(back_ps, n * 4 + 2 * half + t + 1)
                            dve.tensor_tensor(xres[:, t, cols], xres[:, t, cols], PO[t][:], ALU.add)\
                                .then_inc(added[t][half], 1)

            dve.wait_ge(fin_sb, 2)
            for t in range(TT):
                means(4, t)
            for t in range(TT):
                dve.wait_ge(rs_done, 2 * 4 + t + 1)
                dve.scalar_tensor_tensor(out=xn[:, t, 512:], in0=xres[:, t, 512:], scalar=rnorm[:, 4, t:t + 1],
                                         in1=fin_g[:, 512:], op0=ALU.mult, op1=ALU.mult).then_inc(fin_dve, 1)

        @block.tensor
        def _(pe):
            def transpose_unit(banks, src, u, t):
                for i in range(2):
                    k = 2 * u + i
                    op = pe.transpose(banks[u][:, i * T + t * P:i * T + (t + 1) * P], src[:, t, k * P:(k + 1) * P],
                                      ident[:])
                return op

            def transpose_normalised(order):
                for t in range(TT):
                    pe.wait_ge(xn_done, 2 * order + t + 1)
                    for u in range(4):
                        op = transpose_unit(NT_BANKS, xn, u, t)
                        if t == TT - 1:
                            op.then_inc(nt_ps, 1)

            def transpose_residual(banks, u, added_count):
                pe.wait_ge(ev_dve, added_count)
                for t in range(TT):
                    op = transpose_unit(banks, xres, u, t)
                op.then_inc(nt_ps, 1)

            def product(ps, a, b, start, stop):
                pe.matmul(ps, a[0], b[0], start=start, stop=False, skip_group_check=True)
                pe.matmul(ps, a[0], b[1], start=False, stop=False, skip_group_check=True)
                return pe.matmul(ps, a[1], b[0], start=False, stop=stop, skip_group_check=True)

            def half_chunk(g, hi, lo, ready=None, before=0, tiles=1):
                c, h = divmod(g, 2)
                kind, b = kinds[c], g % NS
                own = kind in ("merge", "xo")
                ps = PT[c % 2] if own and h else PJ[c % 2]
                if h == 0 and c >= 2:
                    pe.wait_ge(ev_dve if kinds[c - 2] in ON_DVE else ev_act, evac_count(c - 2))
                if g == 2 * at["merge"] + 1:
                    pe.wait_ge(nt_lo, 4 * (MEM_NORM + 1))
                pe.wait_ge(lo_done, g + 1)
                k0 = {"merge": h * HK, "xo": 0}.get(kind, h * HK)
                opens, closes = own or h == 0, own or h == 1
                for k in range(HK):
                    if ready is not None and k % tiles == 0:
                        pe.wait_ge(ready, before + (k0 + k) // tiles + 1)
                    for j in range(2):
                        W = (w_hi[:, b, k], w_lo[:, b, k])
                        wcol = [w[:, j * P:(j + 1) * P] for w in W]
                        X = (hi[:, k0 + k], lo[:, k0 + k])
                        xcol = [v[:, j * P:(j + 1) * P] for v in X]
                        start, stop = opens and k == 0 and j == 0, closes and k == HK - 1
                        if kind in ("va", "vx", "mix", "xo"):
                            op = product(ps[:, j * T:(j + 1) * T], xcol, W, start, stop)
                        elif kind == "kvb" and j == 1:
                            for t in range(TT):
                                op = product(ps[:, T + t * P:T + (t + 1) * P], [v[:, t * P:(t + 1) * P] for v in X],
                                             wcol, start, stop)
                        else:
                            op = product(ps[:, j * T:(j + 1) * T], wcol, X, start, stop)
                op.then_inc(half_done, 1)

            def pair_scores(j):
                swa, i = divmod(j, PAIRS)
                pe.wait_ge(ev_act, evac_count(at["kvb"] if swa else at["ka"] + i // 2))
                if j:
                    pe.wait_ge(s_bias, 2 * j)
                q = qb if swa else qa
                for tt in range(TT):
                    for hh in range(2):
                        rows = slice(hh * HD, (hh + 1) * HD)
                        keys = kb2[rows, (2 * i + hh) // 4] if swa else ka[rows, i]
                        if tt == 0:
                            op = pe.matmul(SC[hh][:, 0:P], q[rows, i, 0:P], keys[:, 0:P], start=True, stop=True)
                        else:
                            op = pe.matmul(SC[hh][:, P:SK], q[rows, i, P:T], keys, start=True, stop=True)
                op.then_inc(s_ps, 1)

            def pair_transposes(j):
                pe.wait_ge(s_norm, 4 * (j + 1))
                if j:
                    pe.wait_ge(pt_sb, 2 * j)
                for hh in range(2):
                    for i in range(3):
                        cols = slice(i * P, (i + 1) * P)
                        op = pe.transpose(PT[hh][:, cols], scores[:, j % 2, hh, cols], ident[:])
                op.then_inc(pt_ps, 1)

            def pair_values(j):
                swa, i = divmod(j, PAIRS)
                pe.wait_ge(ev_act, evac_count(at["kvb"] if swa else at["va"] + i // 2))
                pe.wait_ge(pt_sb, 2 * j + 2)
                if j >= 2:
                    pe.wait_ge(mix_lo, j - 1)
                for tt, kt, cols in ((0, 0, slice(0, P)), (1, 0, slice(P, 2 * P)), (1, 1, slice(2 * P, SK))):
                    for hh in range(2):
                        h = 2 * i + hh
                        v = vb[:, kt, (h // 4) * HD:(h // 4 + 1) * HD] if swa else va[:, kt, h * HD:(h + 1) * HD]
                        op = pe.matmul(PO[j % 2][hh * HD:(hh + 1) * HD, tt * P:(tt + 1) * P], v, probT[:, hh, cols],
                                       start=kt == 0, stop=kt == tt)
                op.then_inc(pv_ps, 1)

            pe.wait_ge(c_ident, 1)
            pe.wait_ge(gain_in, 64)
            pe.transpose(PO[0][:, 0:4 * KD], g_rows[:], ident[0:4 * KD, 0:4 * KD]).then_inc(c_gain_ps, 1)
            transpose_normalised(0)
            pe.wait_ge(c_ones, 1)
            pe.wait_ge(small_in, 80)
            pe.matmul(PO[1][:, 0:HEADS], ones[0:1, :], sink_row[:], start=True, stop=True)
            pe.matmul(PO[1][:, HEADS:HEADS + NG + NE], ones[0:1, :], br[:], start=True, stop=True)\
                .then_inc(c_sink_ps, 1)
            for g in range(2 * FIRST_UNDER):
                if g < 2:
                    half_chunk(g, hT_hi, hT_lo, nt_lo, 0, 2)
                else:
                    half_chunk(g, hT_hi, hT_lo)
            pe.wait_ge(c_gain, 3)
            pe.wait_ge(c_sink, 1)
            for i in range(STEPS):
                c = FIRST_UNDER + i
                if i < UNITS:
                    pair_scores(i)
                half_chunk(2 * c, hT_hi, hT_lo)
                half_chunk(2 * c + 1, hT_hi, hT_lo)
                if 1 <= i <= UNITS:
                    pair_transposes(i - 1)
                if 2 <= i <= UNITS + 1:
                    pair_values(i - 2)
            transpose_normalised(MEM_NORM)

            def chunk(c, hi, lo, *ready):
                half_chunk(2 * c, hi, lo, *ready)
                half_chunk(2 * c + 1, hi, lo, *ready)

            chunk(at["merge"], mixT_hi, mixT_lo, mix_lo, 0, 1)
            for c in range(at["merge"] + 1, last["merge"] + 1):
                chunk(c, mixT_hi, mixT_lo)
            chunk(at["kx"], memT_hi, memT_lo)
            for m in range(4):
                chunk(at["mix"] + m, mgT_hi, mgT_lo, mg_lo, 0, 2)
                if m:
                    transpose_residual(NT_BANKS, m - 1, evac_count(at["mix"] + m - 1))
            chunk(last["kx"], memT_hi, memT_lo)
            transpose_residual(NT_BANKS, 3, evac_count(last["mix"]))
            chunk(at["vx"], memT_hi, memT_lo)
            chunk(at["qx"], h2T_hi, h2T_lo, nt_lo, 4 * X2_NORM, 2)
            chunk(last["qx"], h2T_hi, h2T_lo)

            def x_scores(h):
                pe.wait_ge(ev_act, evac_count((at["qx"], last["qx"])[h // 2]))
                for tt in range(TT):
                    op = pe.matmul(XS_BANKS[h][:, tt * T:(tt + 1) * T], qx[:, h, tt * P:(tt + 1) * P], kx[:, h],
                                   start=True, stop=True)
                op.then_inc(xs_ps, 1)

            x_scores(0)
            x_scores(1)
            half_chunk(2 * V1, memT_hi, memT_lo)
            x_scores(2)
            x_scores(3)
            half_chunk(2 * V1 + 1, memT_hi, memT_lo)

            def x_transposes(h):
                pe.wait_ge(xs_norm, 2 * h + 2)
                for mt in range(2):
                    for tt in range(TT):
                        op = pe.transpose(PT[h % 2][:, mt * T + tt * P:mt * T + (tt + 1) * P],
                                          xprob[:, h, tt, mt * P:(mt + 1) * P], ident[:])
                op.then_inc(xpt_ps, 1)

            def x_values(h):
                pe.wait_ge((xpt_act, xpt_dve)[h % 2], h // 2 + 1)
                if h >= 2:
                    pe.wait_ge(ox_lo, h - 1)
                for mt in range(2):
                    op = pe.matmul(PO[h % 2][:, 0:T], vx[:, mt, h * P:(h + 1) * P], xpT[:, h % 2, mt * T:(mt + 1) * T],
                                   start=mt == 0, stop=mt == 1)
                op.then_inc(xpv_ps, 1)

            x_transposes(0)
            pe.wait_ge(ev_act, evac_count(last["vx"]))
            for h in range(XH):
                if h + 1 < XH:
                    x_transposes(h + 1)
                x_values(h)
            X = 2 * at["xo"]
            half_chunk(X, oxT_hi, oxT_lo, ox_lo, 0, 1)
            half_chunk(X + 1, oxT_hi, oxT_lo)
            half_chunk(X + 2, oxT_hi, oxT_lo)
            transpose_residual(NT_BANKS3, 0, evac_count(NC - 1) - 3)
            transpose_residual(NT_BANKS3, 1, evac_count(NC - 1) - 2)
            half_chunk(X + 3, oxT_hi, oxT_lo)
            transpose_residual(NT_BANKS3, 2, evac_count(NC - 1) - 1)

            def logits(ks):
                for k in ks:
                    for t in range(TT):
                        op = pe.matmul(LOGIT[:, t * 64:t * 64 + NG + NE], h3T[:, k, t * P:(t + 1) * P], wrg[:, k],
                                       start=k == 0 and t == 0, stop=k == KD - 1, skip_group_check=True)
                return op

            pe.wait_ge(h3_act, 1)
            logits((0, 1))
            pe.wait_ge(h3_dve, 1)
            logits((2, 3))
            transpose_residual(NT_BANKS3, 3, evac_count(NC - 1))
            pe.wait_ge(h3_act, 2)
            logits((4, 5))
            pe.wait_ge(h3_dve, 2)
            logits((6, 7)).then_inc(logits_ps, 1)
            pe.wait_ge(fin_in, 16)
            for half in range(2):
                op = pe.matmul(FIN_BANKS[half][:], ones[0:1, :], fin_row[:, half * 512:(half + 1) * 512],
                               start=True, stop=True)
            op.then_inc(fin_ps, 1)
            pe.wait_ge(c_misc, 17)
            pe.wait_ge(r_mask, 2)
            flat = both[:].rearrange("p t e -> p (t e)")
            pe.matmul(LISTED[:, 0:2 * NE], below_r[:], flat, start=True, stop=False, skip_group_check=True)
            pe.matmul(LISTED[:, NE:2 * NE], ones_r[:], both[:, 0], start=False, stop=True, skip_group_check=True)\
                .then_inc(pos_ps, 1)
            pe.matmul(COUNTS[:, 0:NE], ones_r[:], both[:, 0], start=True, stop=False)
            pe.matmul(COUNTS[:, 0:NE], ones_r[:], both[:, 1], start=False, stop=True).then_inc(pos_ps, 1)

            pe.wait_ge(fin_sb, 2)
            pe.wait_ge(trips_set, 1)
            total = pe.value_load(trips[0:1, 0:1], min_val=BODIES, max_val=BODIES * ROUNDS)
            with pe.Fori(0, total) as body:
                for q in range(BODY_QUADS):
                    n = body * BODY_QUADS + q
                    pe.wait_ge(sel_made, n * 2 + 1)
                    pe.wait_ge(xn_done, 6)
                    for k in range(KD):
                        for t in range(TT):
                            op = pe.matmul(SC[k // 4][:, (k % 4) * P:(k % 4 + 1) * P], xn[:, t, k * P:(k + 1) * P],
                                           sel[:, t].rearrange("p e s -> p (e s)"), start=t == 0, stop=t == TT - 1)
                        if k % 4 == 3:
                            op.then_inc(gather_ps, 1)
                    for k in range(KD):
                        i = q * MOE_CHUNKS + k
                        if k % 4 == 0:
                            pe.wait_ge(moe_x_sb, n * 2 + k // 4 + 1)
                        pe.wait_ge(moe_in[slot_of_chunk(i)], landed(i, body))
                        for e in range(QE):
                            op = pe.matmul(PJ[0][e * WIN:(e + 1) * WIN, :], moe_x[:, k, e * WIN:(e + 1) * WIN],
                                           slots[slot_of_chunk(i)][:, e * 512:(e + 1) * 512],
                                           start=k == 0, stop=k == KD - 1)
                        op.then_inc(chunk_used, 1)
                    pe.wait_ge(sel_made, n * 2 + 2)
                    for t in range(TT):
                        op = pe.transpose(PT[1][:, t * P:(t + 1) * P], selw[:, t].rearrange("p e s -> p (e s)"),
                                          ident[:])
                    op.then_inc(selT_ps, 1)
                    pe.wait_ge(hid_done, n + 1)
                    for k in range(KF):
                        op = pe.transpose(PT[0][:, k * P:(k + 1) * P], hid[:, k * P:(k + 1) * P], ident[:])
                    op.then_inc(hidT_ps, 1)

                    def down(half, kt):
                        i = q * MOE_CHUNKS + GU_CHUNKS + 2 * half + kt
                        pe.wait_ge(moe_in[slot_of_chunk(i)], landed(i, body))
                        for e in range(QE):
                            op = pe.matmul(SC[half][e * WIN:(e + 1) * WIN, :], hidT[:, kt, e * WIN:(e + 1) * WIN],
                                           slots[slot_of_chunk(i)][:, e * 512:(e + 1) * 512],
                                           start=kt == 0, stop=kt == KF - 1)
                        op.then_inc(chunk_used, 1)

                    def back_to_tokens(half):
                        for t in range(TT):
                            if half:
                                pe.wait_ge(added[t][0], n + 1)
                            pe.matmul(PO[t][:], selwT[:, t * P:(t + 1) * P], y_sb[:, half * 512:(half + 1) * 512],
                                      start=True, stop=True).then_inc(back_ps, 1)

                    pe.wait_ge(hidT_sb, n + 1)
                    down(0, 0)
                    down(0, 1)
                    down(1, 0)
                    pe.wait_ge(selT_sb, n + 1)
                    pe.wait_ge(y_act, n + 1)
                    back_to_tokens(0)
                    down(1, 1)
                    pe.wait_ge(y_dve, n + 1)
                    back_to_tokens(1)


_INS = ["x", "mem", "mix_norm_g", "w_in", "moba_out_w", "swa_out_w", "swa_sinks", "mix_out_w", "xattn_norm_g",
        "mem_norm_g", "xattn_wq", "xattn_wkv", "xattn_wo", "ffn_norm_g", "router_group_w", "router_group_b",
        "router_expert_w", "router_expert_b", "expert_w_gate", "expert_w_up", "expert_w_down", "final_norm_g"]
_OUTS = [((1, 256, 1024), "float32")]


def kernel(**inputs):
    import numpy as _np
    import concourse.bacc as _bacc
    from concourse import mybir as _mybir
    from concourse.bass_utils import run_bass_kernel_spmd as _run

    nc = _bacc.Bacc("TRN2", target_bir_lowering=False, num_devices=1)
    arrays, args = {}, []
    for name in _INS:
        a = _np.ascontiguousarray(inputs[name])
        arrays[f"in_{name}_dram"] = a
        args.append(nc.dram_tensor(f"in_{name}_dram", a.shape, _mybir.dt.from_np(a.dtype), kind="ExternalInput").ap())
    for i, (shape, dtype) in enumerate(_OUTS):
        dt = _mybir.dt.from_np(_np.dtype(dtype))
        args.append(nc.dram_tensor(f"out_{i}_dram", shape, dt, kind="ExternalOutput").ap())
    hybrid_layer(nc, *args)
    r = _run(nc, [arrays], core_ids=[0])
    got = tuple(r.results[0][f"out_{i}_dram"] for i in range(len(_OUTS)))
    return got[0]
```

```python
from contextlib import ExitStack

import concourse.bass as bass
from concourse import mybir

P = 128


def hybrid_layer(nc, x, mem, mix_norm_g, w_in, moba_out_w, swa_out_w, swa_sinks, mix_out_w, xattn_norm_g,
                 mem_norm_g, xattn_wq, xattn_wkv, xattn_wo, ffn_norm_g, router_group_w, router_group_b,
                 router_expert_w, router_expert_b, expert_w_gate, expert_w_up, expert_w_down,
                 final_norm_g, out):
    F32, F32R = mybir.dt.float32, mybir.dt.float32r
    I32, U32 = mybir.dt.int32, mybir.dt.uint32
    ALU, ACT, AX = mybir.AluOpType, mybir.ActivationFunctionType, mybir.AxisListType

    T, D = x.shape[1], x.shape[2]
    TT, KD = T // P, D // P
    HD, HEADS, WINDOW = 64, 8, 128
    PAIRS = HEADS // 2
    XH = 4
    XSCALE = float(P) ** -0.5
    NG, EPG = expert_w_gate.shape[1], expert_w_gate.shape[2]
    NE, FE = NG * EPG, expert_w_gate.shape[4]
    KF = FE // P
    WIN = 32
    QE = P // WIN
    QUADS = NE // QE
    ROUNDS = T // WIN
    EPS, NEG, BIG = 1e-6, -1e30, -3e38
    UNLISTED = 1000
    CW = 256
    HK = 4
    SK = T + WINDOW

    win = w_in[0].rearrange("(k p) n -> p k n", p=P)
    wkv = xattn_wkv[0].rearrange("(k p) n -> p k n", p=P)
    wq = xattn_wq[0].rearrange("(k p) n -> p k n", p=P)
    wmix = mix_out_w[0].rearrange("(k p) n -> p k n", p=P)
    wa = moba_out_w[0].rearrange("(k p) n -> p k n", p=P)
    wb = swa_out_w[0].rearrange("(k p) n -> p k n", p=P)
    wo = xattn_wo[0].rearrange("(k p) n -> p k n", p=P)

    def both_halves(w, col):
        return [w[:, h * HK:(h + 1) * HK, col:col + CW] for h in range(2)]

    halves, kinds = [], []
    for c in range(17):
        kinds.append(["qa", "qa", "ka", "ka", "va", "va", "qb", "qb", "kvb"][c] if c < 9 else "gate")
        halves += both_halves(win, c * CW)
    for m in range(4):
        kinds.append("merge")
        halves += [wa[:, :, m * CW:(m + 1) * CW], wb[:, :, m * CW:(m + 1) * CW]]
    for name, w, col in (("kx", wkv, 0), *(("mix", wmix, m * CW) for m in range(4)), ("kx", wkv, CW),
                         ("vx", wkv, 2 * CW), ("qx", wq, 0), ("qx", wq, CW), ("vx", wkv, 3 * CW)):
        kinds.append(name)
        halves += both_halves(w, col)
    for m in range(2):
        kinds.append("xo")
        halves += [wo[:, :, (2 * m + h) * CW:(2 * m + h + 1) * CW] for h in range(2)]
    NC, NH = len(kinds), len(halves)
    at = {k: kinds.index(k) for k in kinds}
    last = {k: NC - 1 - kinds[::-1].index(k) for k in kinds}
    ON_DVE = {"merge": 1, "mix": 1, "xo": 2}

    def evac_count(c):
        if kinds[c] in ON_DVE:
            return sum(ON_DVE.get(k, 0) for k in kinds[:c + 1])
        return sum(k not in ON_DVE for k in kinds[:c + 1])

    NW, NS = 3, 3

    GU_CHUNKS, MOE_CHUNKS = KD, KD + KF * 2
    BODY_QUADS = 4
    BODIES, BODY_CHUNKS = QUADS // BODY_QUADS, BODY_QUADS * MOE_CHUNKS
    SLOTS = 22

    def slot_of_chunk(i):
        return i % SLOTS

    def loads_of_slot(s):
        return sum(slot_of_chunk(i) == s for i in range(BODY_CHUNKS))

    def landed(i, body):
        s = slot_of_chunk(i)
        nth = sum(slot_of_chunk(n) == s for n in range(i))
        return body * (32 * loads_of_slot(s)) + 32 * (nth + 1)

    def previous_user(i):
        users = [n for n in range(BODY_CHUNKS) if slot_of_chunk(n) == slot_of_chunk(i)]
        return users[users.index(i) - 1] if users.index(i) else users[-1] - BODY_CHUNKS

    wg_v = expert_w_gate[0].rearrange("g e (k p) f -> k p (g e) f", p=P)
    wu_v = expert_w_up[0].rearrange("g e (k p) f -> k p (g e) f", p=P)
    wd_v = expert_w_down[0].rearrange("g e (k p) d -> k p (g e) d", p=P)

    ctx = ExitStack()
    with ctx:
        place = [(nc.sbuf_base + 63) // 64 * 64]

        def region(nbytes):
            place[0] += nbytes
            assert place[0] <= nc.sbuf_usable_end
            return place[0] - nbytes

        def sb(name, shape, dt, offset=None):
            n = 4
            for s in shape[1:]:
                n *= s
            offset = region((n + 31) // 32 * 32) if offset is None else offset
            return nc.alloc_sbuf_tensor_at(name, shape, dt, offset=offset)

        slot_at = [region(8192) for _ in range(11)]
        mem_raw = sb("mem_raw", [P, TT, D], F32, slot_at[8])
        mixT_hi = sb("mixT_hi", [P, 2 * PAIRS, T], F32R, slot_at[9])
        mixT_lo = sb("mixT_lo", [P, 2 * PAIRS, T], F32R, slot_at[10])
        w_at = region(NW * HK * CW * 4)
        w_raw = sb("w_raw", [P, NW, HK, CW], F32, w_at)
        w_hi = sb("w_hi", [P, NS, HK, CW], F32R)
        w_lo = sb("w_lo", [P, NS, HK, CW], F32R)
        xres = sb("xres", [P, TT, D], F32)
        xn_at = region(8192)
        xn = sb("xn", [P, TT, D], F32, xn_at)
        r1 = region(16384)
        hT_hi = sb("hT_hi", [P, KD, T], F32R, r1)
        hT_lo = sb("hT_lo", [P, KD, T], F32R, r1 + 8192)
        mgT_hi = sb("mgT_hi", [P, KD, T], F32R, r1)
        mgT_lo = sb("mgT_lo", [P, KD, T], F32R, r1 + 8192)
        h2T_hi = sb("h2T_hi", [P, KD, T], F32R, slot_at[9])
        h2T_lo = sb("h2T_lo", [P, KD, T], F32R, slot_at[10])
        oxT_hi = sb("oxT_hi", [P, XH, T], F32R, r1)
        oxT_lo = sb("oxT_lo", [P, XH, T], F32R, r1 + 8192)
        r2 = region(16384 + 2048 + 1024)
        r3 = region(16384)
        slot_at += [r2, r2 + 8192, r3, r3 + 8192]
        slot_at += [w_at + 4096 + n * 8192 for n in range(4)] + [r1]
        qa = sb("qa", [P, PAIRS, T], F32, r2)
        ka = sb("ka", [P, PAIRS, T], F32, r2 + 4096)
        va = sb("va", [P, TT, HEADS * HD], F32, r2 + 8192)
        qb = sb("qb", [P, PAIRS, T], F32, r2 + 12288)
        kb2 = sb("kb2", [P, 2, T], F32, r2 + 16384)
        vb = sb("vb", [P, TT, P], F32, r2 + 18432)
        memT_hi = sb("memT_hi", [P, KD, T], F32R, r2)
        memT_lo = sb("memT_lo", [P, KD, T], F32R, r2 + 8192)
        gates = sb("gates", [P, 2 * KD, T], F32, r3)
        qx = sb("qx", [P, XH, T], F32, r3)
        kx = sb("kx", [P, XH, T], F32, r3 + 4096)
        vx = sb("vx", [P, TT, XH * P], F32, r3 + 8192)
        xpT = sb("xpT", [P, 2, 2 * T], F32, r3 + 12288)
        sc_at = region(6144 + 3072)
        scores = sb("scores", [P, 2, 2, SK], F32, sc_at)
        probT = sb("probT", [P, 2, SK], F32, sc_at + 6144)
        g_rows = sb("g_rows", [4 * KD, P], F32, sc_at)
        xprob = sb("xprob", [P, XH, TT, T], F32, sc_at)
        h3T = sb("h3T", [P, KD, T], F32, sc_at)
        ones_r = sb("ones_r", [P, P], F32R, sc_at + 8192)
        below_r = sb("below_r", [P, P], F32R, sc_at + 8192 + 512)
        slot_at += [xn_at, sc_at]
        slots = [sb(f"moe_slot{s}", [P, 2048], F32, a) for s, a in enumerate(slot_at)]
        assert len(slots) == SLOTS
        moe_x = sb("moe_x", [P, KD, P], F32, r1 + 8192)
        sel = sb("sel", [P, TT, QE, WIN], F32, r1 + 12288)
        sel_norm = sb("sel_norm", [P, TT, QE, WIN], F32, sc_at + 8192)
        selw = sb("selw", [P, TT, QE, WIN], F32, r1 + 13312)
        selwT = sb("selwT", [P, T], F32, r1 + 14336)
        silu_g = sb("silu_g", [P, FE], F32, r1 + 15360)
        hid = sb("hid", [P, FE], F32, r2 + 16384)
        hidT = sb("hidT", [P, KF, P], F32, r2 + 17408)
        fin_g = sb("fin_g", [P, D], F32, slot_at[10])
        rt = w_at

        def small(name, shape, dt=F32):
            nonlocal rt
            n = 4
            for s in shape[1:]:
                n *= s
            rt += (n + 31) // 32 * 32
            assert rt <= w_at + HK * CW * 4
            return nc.alloc_sbuf_tensor_at(name, shape, dt, offset=rt - (n + 31) // 32 * 32)

        logit = small("logit", [P, TT, NE])
        g_log = small("g_log", [P, TT, 8])
        g_top, e_top = small("g_top", [P, TT, 8]), small("e_top", [P, TT, 8])
        g_idx, e_idx = small("g_idx", [P, TT, 8], U32), small("e_idx", [P, TT, 8], U32)
        g_idf, e_idf = small("g_idf", [P, TT, 8]), small("e_idf", [P, TT, 8])
        g_exp, g_sum, g_neg = small("g_exp", [P, TT, 4]), small("g_sum", [P, TT]), small("g_neg", [P, TT])
        pen, e_log = small("pen", [P, TT, NG]), small("e_log", [P, TT, NG, EPG])
        e_neg, e2 = small("e_neg", [P, TT]), small("e2", [P, TT])
        den, ew = small("den", [P, TT]), small("ew", [P, 2, TT])
        first, both = small("first", [P, TT, NE]), small("both", [P, TT, NE], F32R)
        wfirst, wboth = small("wfirst", [P, TT, NE]), small("wboth", [P, TT, NE])
        slot_of = small("slot_of", [P, TT, NE])
        posm = small("posm", [P, TT, NE])
        cmax, over, nover = small("cmax", [P, 1]), small("over", [P, 8]), small("nover", [P, 1])
        trips = small("trips", [P, 1], I32)
        ident = sb("ident", [P, P], F32)
        below = sb("below", [P, P], F32)
        ones = sb("ones", [P, P], F32)
        gains = sb("gains", [P, 4, KD], F32)
        dist_at = region(2 * SK * 4 + KD * (NG + NE) * 4)
        dist = sb("dist", [P, 2, SK], F32, dist_at)
        wr = sb("wr", [P, KD, NG + NE], F32, r3)
        wrg = sb("wrg", [P, KD, NG + NE], F32, dist_at + 2 * SK * 4)
        y_sb = sb("y_sb", [P, D], F32, dist_at)
        br, br_all = sb("br", [1, NG + NE], F32), sb("br_all", [P, NG + NE], F32)
        sink_row = sb("sink_row", [1, HEADS], F32)
        sinks, nsinks = sb("sinks", [P, HEADS], F32), sb("nsinks", [P, HEADS], F32)
        iota_e = sb("iota_e", [P, NE], F32)
        iota_rw = sb("iota_rw", [P, ROUNDS], F32)
        mean_sq = sb("mean_sq", [P, 4 + 1, TT, 2], F32)
        mean_eps, rnorm = (sb(n, [P, 4 + 1, TT], F32) for n in ("mean_eps", "rnorm"))
        xscale = sb("xscale", [P, TT], F32)
        mhalf = sb("mhalf", [P, TT], F32)
        nmax = sb("nmax", [P, 2, 2, 2], F32)
        rsum, rinv = sb("rsum", [P, 2, 4], F32), sb("rinv", [P, 2, 4], F32)
        sink_arg, sink_exp = sb("sink_arg", [P, 2, 4], F32), sb("sink_exp", [P, 2, 4], F32)
        xmax, xnmax = sb("xmax", [P, XH, TT], F32), sb("xnmax", [P, XH, TT], F32)
        xsum, xinv = sb("xsum", [P, XH, TT], F32), sb("xinv", [P, XH, TT], F32)

        PJ, SC, PT, PO = ([ctx.enter_context(nc.psum_tensor(f"{n}{i}", [P, 512], F32)) for i in range(2)]
                          for n in ("proj", "score", "probt", "attno"))

        LOGIT, LISTED, COUNTS = SC[0], SC[1], SC[0]
        ACC = ((PO[0], PJ[1]), (PO[1], PT[1]))
        HID_T, SEL_T = PT[0][:, 0:KF * P], SC[1][:, 0:T]
        NT_BANKS = (PT[0], PT[1], SC[0], SC[1])
        NT_BANKS3 = (SC[0], SC[1], PT[1], PO[1])

        def sem(name):
            return ctx.enter_context(nc.semaphore(name))

        x_in = [sem(f"x_in{t}") for t in range(TT)]
        mem_in, gain_in, small_in, wr_in, fin_in = (
            sem(n) for n in ("mem_in", "gain_in", "small_in", "wr_in", "fin_in"))
        w_in_sem = [sem(f"w_loaded{i}") for i in range(NW)]
        moe_in = [sem(f"moe_loaded{i}") for i in range(SLOTS)]
        c_ident, c_ones, c_misc, c_gain, c_sink_ps, c_sink = (
            sem(n) for n in ("c_ident", "c_ones", "c_misc", "c_gain", "c_sink_ps", "c_sink"))
        c_gain_ps = sem("c_gain_ps")
        hi_done, lo_done, half_done, ev_act, ev_dve = (
            sem(n) for n in ("hi_done", "lo_done", "half_done", "ev_act", "ev_dve"))
        sq_done, ms_done, rs_done, xn_done, x0n_done = (
            sem(n) for n in ("sq_done", "ms_done", "rs_done", "xn_done", "x0n_done"))
        nt_ps, nt_hi, nt_lo = (sem(n) for n in ("nt_ps", "nt_hi", "nt_lo"))
        s_ps, s_bias, s_max, s_exp, s_inv, s_norm, pt_ps, pt_sb, pv_ps, mix_hi, mix_lo = (
            sem(n) for n in ("s_ps", "s_bias", "s_max", "s_exp", "s_inv", "s_norm", "pt_ps", "pt_sb", "pv_ps",
                             "mix_hi", "mix_lo"))
        sig_done, mg_part, mg_sum, mg_hi, mg_lo = (
            sem(n) for n in ("sig_done", "mg_part", "mg_sum", "mg_hi", "mg_lo"))
        xscale_set = sem("xscale_set")
        xs_ps, xs_max, xs_exp, xs_inv, xs_norm, xpt_ps, xpt_act, xpt_dve, xpv_ps, ox_hi, ox_lo = (
            sem(n) for n in ("xs_ps", "xs_max", "xs_exp", "xs_inv", "xs_norm", "xpt_ps", "xpt_act", "xpt_dve",
                             "xpv_ps", "ox_hi", "ox_lo"))
        h3_act, h3_dve, r_ew, r_weight, r_posm, r_slots, w_step, logits_ps = (
            sem(n) for n in ("h3_act", "h3_dve", "r_ew", "r_weight", "r_posm", "r_slots", "w_step", "logits_ps"))
        r_step, r_top, r_exp, r_mask, pos_ps, trips_set = (
            sem(n) for n in ("r_step", "r_top", "r_exp", "r_mask", "pos_ps", "trips_set"))
        sel_made, gather_ps, moe_x_sb, selT_ps, selT_sb, chunk_used, silu_done, hid_done = (
            sem(n) for n in ("sel_made", "gather_ps", "moe_x_sb", "selT_ps", "selT_sb", "chunk_used",
                             "silu_done", "hid_done"))
        hidT_ps, hidT_sb, y_act, y_dve = (
            sem(n) for n in ("hidT_ps", "hidT_sb", "y_act", "y_dve"))
        slots_moved = sem("slots_moved")
        back_ps = [[sem(f"back_ps{t}{half}") for half in range(2)] for t in range(TT)]
        fin_xg, fin_act, fin_dve, out_done = (sem(n) for n in ("fin_xg", "fin_act", "fin_dve", "out_done"))

        block = ctx.enter_context(nc.Block())

        MEM_NORM, X2_NORM, X3_NORM = 1, 2, 3
        V1 = last["vx"]

        def sq_count(n, t):
            return 2 * n + t + 1 if n in (0, MEM_NORM) else 4 + 4 * (n - X2_NORM) + 3 + t

        STEPS = HEADS + 3
        FIRST_UNDER = 6
        XS_BANKS = (SC[0], SC[1], PO[0], PO[1])
        UNITS = 2 * PAIRS

        def s_max_count(j):
            return 2 * min(j + 1, PAIRS) + 4 * max(j + 1 - PAIRS, 0)

        def s_exp_count(j):
            return 4 * min(j + 1, PAIRS) + 5 * max(j + 1 - PAIRS, 0)

        @block.sync
        def _(sp):
            for t in range(TT):
                sp.dma_start(xres[:, t], x[0, t * P:(t + 1) * P, :]).then_inc(x_in[t], 16)
            for i, g in enumerate((mix_norm_g, mem_norm_g, xattn_norm_g, ffn_norm_g)):
                sp.dma_start(g_rows[i * KD:(i + 1) * KD, :], g[0].rearrange("(k p) -> k p", p=P)).then_inc(gain_in, 16)

            def load_half(g):
                if g >= NW:
                    sp.wait_ge(lo_done, g - NW + 1)
                sp.dma_start(w_raw[:, g % NW], halves[g]).then_inc(w_in_sem[g % NW], 16)

            def load_experts(i, body):
                q, c = divmod(i, MOE_CHUNKS)
                s, e0 = slot_of_chunk(i), (body * BODY_QUADS + q) * QE
                if c < GU_CHUNKS:
                    dst = slots[s][:].rearrange("p (e j f) -> p e j f", e=QE, j=2)
                    sp.dma_start(dst[:, :, 0], wg_v[c, :, bass.ds(e0, QE), :]).then_inc(moe_in[s], 16)
                    sp.dma_start(dst[:, :, 1], wu_v[c, :, bass.ds(e0, QE), :]).then_inc(moe_in[s], 16)
                else:
                    half, kt = divmod(c - GU_CHUNKS, 2)
                    dst = slots[s][:].rearrange("p (e d) -> p e d", e=QE)
                    for e in range(0, QE, 2):
                        sp.dma_start(dst[:, e:e + 2], wd_v[kt, :, bass.ds(e0 + e, 2), half * 512:(half + 1) * 512])\
                            .then_inc(moe_in[s], 16)

            for g in range(NW):
                load_half(g)
            sp.dma_start(mem_raw[:], mem[0].rearrange("(t p) d -> p t d", p=P)).then_inc(mem_in, 16)
            sp.dma_start(wr[:, :, 0:NG], router_group_w[0].rearrange("(k p) n -> p k n", p=P)).then_inc(wr_in, 16)
            sp.dma_start(wr[:, :, NG:NG + NE], router_expert_w[0].rearrange("(k p) n -> p k n", p=P))\
                .then_inc(wr_in, 16)
            prefetched = 0
            for g in range(NW, NH):
                load_half(g)
                if g >= 12 and g % 3 == 0 and prefetched < 8:
                    load_experts(prefetched, 0)
                    prefetched += 1
                if prefetched == 8 and g > 2 * at["kx"] + 1:
                    sp.wait_ge(xn_done, 1 + TT)
                    load_experts(8, 0)
                    prefetched = 9
                if g in (2 * V1 + 3, 2 * V1 + 4):
                    sp.wait_ge(half_done, 2 * last["qx"] + 2)
                    load_experts(prefetched, 0)
                    prefetched += 1
            assert prefetched == 11
            sp.wait_ge(half_done, 2 * V1 + 2)
            load_experts(11, 0)
            load_experts(12, 0)
            sp.wait_ge(xs_ps, XH)
            load_experts(13, 0)
            sp.wait_ge(xpv_ps, XH)
            load_experts(14, 0)
            sp.wait_ge(lo_done, NH)
            load_experts(15, 0)
            sp.wait_ge(half_done, NH - 1)
            load_experts(16, 0)
            sp.wait_ge(half_done, NH)
            for i in range(17, 20):
                load_experts(i, 0)
            sp.wait_ge(sq_done, sq_count(X3_NORM, TT - 1))
            load_experts(20, 0)
            sp.wait_ge(logits_ps, 1)
            load_experts(21, 0)
            for i in range(SLOTS, BODY_CHUNKS):
                sp.wait_ge(chunk_used, previous_user(i) + 1)
                load_experts(i, 0)
            sp.wait_ge(trips_set, 1)
            total = sp.value_load(trips[0:1, 0:1], min_val=BODIES, max_val=BODIES * ROUNDS)
            with sp.Fori(1, total) as body:
                for i in range(BODY_CHUNKS):
                    sp.wait_ge(chunk_used, body * BODY_CHUNKS + previous_user(i) + 1)
                    load_experts(i, body % BODIES)
            sp.wait_ge(sel_made, total * (3 * BODY_QUADS))
            sp.dma_start(fin_g[:], final_norm_g.rearrange("(a n) -> a n", a=1).broadcast_to([P, D]))\
                .then_inc(fin_in, 16)
            for t in range(TT):
                for half, scaled in ((1, fin_dve), (0, fin_act)):
                    cols = slice(half * 512, (half + 1) * 512)
                    sp.wait_ge(scaled, t + 1)
                    sp.dma_start(out[0, t * P:(t + 1) * P, cols], xres[:, t, cols]).then_inc(out_done, 16)
            sp.wait_ge(out_done, 16 * 2 * TT)

        @block.gpsimd
        def _(pool):
            pool.memset(ident[:], 0.0).then_inc(c_misc, 1)
            pool.memset(mean_sq[:], 0.0)
            pool.memset(ones[:], 1.0).then_inc(c_ones, 1)
            pool.wait_ge(c_misc, 1)
            pool.affine_select(out=ident[:], in_=ident[:], compare_op=ALU.not_equal, fill=1.0, base=0,
                               pattern=[[-1, P]], channel_multiplier=1).then_inc(c_ident, 1)
            pool.memset(mhalf[:], -0.5).then_inc(c_misc, 1)
            for kind in range(2):
                pool.iota(dist[:, kind, 0:P], [[1, P]], base=0, channel_multiplier=-1,
                          allow_small_or_imprecise_dtypes=True).then_inc(c_misc, 1)
                pool.iota(dist[:, kind, P:SK], [[1, T]], base=-P, channel_multiplier=-1,
                          allow_small_or_imprecise_dtypes=True).then_inc(c_misc, 1)
            pool.wait_ge(c_misc, 6)
            for kind in range(2):
                pool.affine_select(out=dist[:, kind, 0:P], in_=dist[:, kind, 0:P], compare_op=ALU.is_ge,
                                   fill=NEG, base=0, pattern=[[-1, P]], channel_multiplier=1).then_inc(c_misc, 1)
                pool.affine_select(out=dist[:, kind, P:SK], in_=dist[:, kind, P:SK], compare_op=ALU.is_ge,
                                   fill=NEG, base=P, pattern=[[-1, T]], channel_multiplier=1).then_inc(c_misc, 1)
            pool.wait_ge(c_misc, 10)
            pool.affine_select(out=dist[:, 1, P:SK], in_=dist[:, 1, P:SK], compare_op=ALU.is_gt, fill=NEG,
                               base=WINDOW - P, pattern=[[1, T]], channel_multiplier=-1).then_inc(c_misc, 1)
            pool.iota(iota_e[:], [[1, NE]], base=0, channel_multiplier=0,
                      allow_small_or_imprecise_dtypes=True).then_inc(c_misc, 1)
            pool.iota(iota_rw[:], [[WIN, ROUNDS]], base=UNLISTED, channel_multiplier=0,
                      allow_small_or_imprecise_dtypes=True).then_inc(c_misc, 1)
            pool.wait_ge(c_ones, 1)
            pool.affine_select(out=below[:], in_=ones[:], compare_op=ALU.is_gt, fill=0.0, base=0,
                               pattern=[[1, P]], channel_multiplier=-1).then_inc(c_misc, 1)

            def inverse_root(n):
                for t in range(TT):
                    pool.wait_ge(ms_done, 2 * n + t + 1)
                    pool.tensor_tensor(rnorm[:, n, t:t + 1], mean_eps[:, n, t:t + 1], mhalf[:, 0:1], ALU.pow)\
                        .then_inc(rs_done, 1)

            inverse_root(0)
            pool.wait_ge(c_gain, 1)
            pool.wait_ge(wr_in, 32)
            pool.tensor_tensor(wrg[:], wr[:], gains[:, X3_NORM].unsqueeze(2).broadcast_to([P, KD, NG + NE]),
                               ALU.mult).then_inc(c_misc, 1)
            inverse_root(MEM_NORM)
            for j in range(UNITS):
                pool.wait_ge(s_inv, j + 1)
                for tt in range(TT):
                    cols = slice(0, P) if tt == 0 else slice(P, SK)
                    for hh in range(2):
                        i = 2 * tt + hh
                        pool.tensor_scalar(scores[:, j % 2, hh, cols], scores[:, j % 2, hh, cols],
                                           rinv[:, j % 2, i:i + 1], 1.0, ALU.mult, ALU.mult).then_inc(s_norm, 1)
            inverse_root(X2_NORM)
            for h in range(XH):
                pool.wait_ge(xs_inv, h + 1)
                for tt in range(TT):
                    pool.tensor_scalar(xprob[:, h, tt], xprob[:, h, tt], xinv[:, h, tt:tt + 1], 1.0,
                                       ALU.mult, ALU.mult).then_inc(xs_norm, 1)
            pool.tensor_copy(ones_r[:], ones[:]).then_inc(c_misc, 1)
            pool.tensor_copy(below_r[:], below[:]).then_inc(c_misc, 1)
            inverse_root(X3_NORM)
            written = 0

            def then(op):
                nonlocal written
                op.then_inc(w_step, 1)
                written += 1
                pool.wait_ge(w_step, written)

            pool.wait_ge(r_ew, 1)
            for t in range(TT):
                pool.tensor_scalar(wfirst[:, t], iota_e[:], e_idf[:, t, 0:1], ew[:, 0, t:t + 1], ALU.is_equal,
                                   ALU.mult).then_inc(w_step, 1)
                written += 1
                then(pool.tensor_scalar(wboth[:, t], iota_e[:], e_idf[:, t, 1:2], ew[:, 1, t:t + 1], ALU.is_equal,
                                        ALU.mult))
                pool.tensor_tensor(wboth[:, t], wboth[:, t], wfirst[:, t], ALU.add).then_inc(r_weight, 1)
            inverse_root(4)

        @block.scalar
        def _(act):
            act.wait_ge(c_misc, 2)
            act.wait_ge(c_ones, 1)
            act.activation(xscale[:, 0:1], mhalf[:, 0:1], ACT.Square)
            act.dma_start(sink_row[:], swa_sinks).then_inc(small_in, 16)
            act.dma_start(br[:, 0:NG], router_group_b).then_inc(small_in, 16)
            act.dma_start(br[:, NG:NG + NE], router_expert_b).then_inc(small_in, 16)

            def squares(n, src, t, half, junk=xn):
                cols = slice(half * 512, (half + 1) * 512)
                act.activation(junk[:, t, cols], src, ACT.Square, scale=float(D) ** -0.5,
                               accum_out=mean_sq[:, n, t, half:half + 1]).then_inc(sq_done, 1)

            def whole_squares(n, rows, t):
                act.activation(xn[:, t], rows[:, t], ACT.Square, scale=float(D) ** -0.5,
                               accum_out=mean_sq[:, n, t, 0:1]).then_inc(sq_done, 1)

            def row_squares(n, rows, t, half):
                squares(n, rows[:, t, half * 512:(half + 1) * 512], t, half)

            def unit_hi(n, hi, u):
                act.wait_ge(nt_ps, 4 * n + u + 1)
                for i in range(2):
                    k = 2 * u + i
                    op = act.activation(hi[:, k], NT_BANKS[u][:, i * T:(i + 1) * T], ACT.Copy,
                                        scale=gains[:, n, k:k + 1])
                op.then_inc(nt_hi, 1)

            def split_hi(g):
                if g >= NH:
                    return
                act.wait_ge(w_in_sem[g % NW], 16 * (g // NW + 1))
                if g >= NS:
                    act.wait_ge(half_done, g - NS + 1)
                act.activation(w_hi[:, g % NS], w_raw[:, g % NW], ACT.Copy).then_inc(hi_done, 1)

            def evacuate(c):
                k, i, src = kinds[c], kinds[:c].count(kinds[c]), PJ[c % 2]
                two = src[:].rearrange("p (a n) -> p a n", a=2)
                act.wait_ge(half_done, 2 * c + 2)
                if k == "qa":
                    op = act.activation(qa[:, 2 * i:2 * i + 2], two, ACT.Copy, scale=float(HD) ** -0.5)
                elif k == "qb":
                    op = act.activation(qb[:, 2 * i:2 * i + 2], two, ACT.Copy, scale=float(HD) ** -0.5)
                elif k == "ka":
                    op = act.activation(ka[:, 2 * i:2 * i + 2], two, ACT.Copy)
                elif k == "va":
                    op = act.activation(va[:, :, i * CW:(i + 1) * CW], two, ACT.Copy)
                elif k == "kvb":
                    for g in range(2):
                        for half in range(2):
                            act.activation(kb2[half * HD:(half + 1) * HD, g], src[g * HD:(g + 1) * HD, 0:T], ACT.Copy)
                    op = act.activation(vb[:], src[:, T:2 * T].rearrange("p (t d) -> p t d", t=TT), ACT.Copy)
                elif k == "gate":
                    if i == 0:
                        act.wait_ge(c_misc, 15)
                    op = act.activation(gates[:, 2 * i:2 * i + 2], two, ACT.Copy)
                elif k == "kx":
                    op = act.activation(kx[:, 2 * i:2 * i + 2], two, ACT.Copy)
                elif k == "qx":
                    op = act.activation(qx[:, 2 * i:2 * i + 2], two, ACT.Copy)
                else:
                    op = act.activation(vx[:, :, i * CW:(i + 1) * CW], two, ACT.Copy)
                op.then_inc(ev_act, 1)

            def exponentials(j):
                b = j % 2
                act.wait_ge(s_max, s_max_count(j))
                for tt in range(TT):
                    cols = slice(0, P) if tt == 0 else slice(P, SK)
                    for hh in range(2):
                        i = 2 * tt + hh
                        act.activation(scores[:, b, hh, cols], scores[:, b, hh, cols], ACT.Exp,
                                       bias=nmax[:, b, tt, hh:hh + 1], accum_out=rsum[:, b, i:i + 1]).then_inc(s_exp, 1)
                if j >= PAIRS:
                    act.activation(sink_exp[:, b], sink_arg[:, b], ACT.Exp).then_inc(s_exp, 1)

            def prob_out(j):
                act.wait_ge(pt_ps, j + 1)
                if j:
                    act.wait_ge(pv_ps, j)
                for hh in range(2):
                    act.activation(probT[:, hh], PT[hh][:, 0:SK], ACT.Copy).then_inc(pt_sb, 1)

            def mix_out_hi(j):
                act.wait_ge(pv_ps, j + 1)
                act.activation(mixT_hi[:, j], PO[j % 2][:, 0:T], ACT.Copy).then_inc(mix_hi, 1)

            for t in range(TT):
                act.wait_ge(x_in[t], 16)
                whole_squares(0, xres, t)
            act.wait_ge(rs_done, 1)
            act.activation(xn[:, 0], xres[:, 0], ACT.Copy, scale=rnorm[:, 0, 0:1]).then_inc(x0n_done, 1)
            split_hi(0)
            act.wait_ge(c_gain, 1)
            unit_hi(0, hT_hi, 0)
            unit_hi(0, hT_hi, 1)
            split_hi(1)
            unit_hi(0, hT_hi, 2)
            unit_hi(0, hT_hi, 3)
            for c in range(FIRST_UNDER):
                split_hi(2 * c + 2)
                split_hi(2 * c + 3)
                evacuate(c)
                if c == 0:
                    act.wait_ge(mem_in, 16)
                    for t in range(TT):
                        whole_squares(MEM_NORM, mem_raw, t)
            for i in range(STEPS):
                c = FIRST_UNDER + i
                split_hi(2 * c + 2)
                if i < UNITS:
                    exponentials(i)
                split_hi(2 * c + 3)
                evacuate(c)
                if 1 <= i <= UNITS:
                    prob_out(i - 1)
                if 2 <= i <= UNITS + 1:
                    mix_out_hi(i - 2)
            def sigmoids(m):
                for g in (0, KD):
                    act.activation(gates[:, g + 2 * m:g + 2 * m + 2], gates[:, g + 2 * m:g + 2 * m + 2],
                                   ACT.Sigmoid).then_inc(sig_done, 1)

            for u in range(4):
                unit_hi(MEM_NORM, memT_hi, u)
            split_hi(2 * at["merge"] + 2)
            act.wait_ge(ev_act, evac_count(last["gate"]))
            sigmoids(0)

            def merged_hi(m):
                act.wait_ge(mg_sum, m + 1)
                act.activation(mgT_hi[:, 2 * m:2 * m + 2], gates[:, 2 * m:2 * m + 2], ACT.Copy).then_inc(mg_hi, 1)

            for m in range(4):
                c = at["merge"] + m
                if m:
                    split_hi(2 * c + 2)
                    merged_hi(m - 1)
                split_hi(2 * c + 3)
                if m < 3:
                    sigmoids(m + 1)

            def step(c):
                split_hi(2 * c + 2)
                split_hi(2 * c + 3)
                if kinds[c] not in ON_DVE:
                    evacuate(c)

            split_hi(2 * at["kx"] + 2)
            merged_hi(3)
            split_hi(2 * at["kx"] + 3)
            evacuate(at["kx"])
            for m in range(4):
                step(at["mix"] + m)
                if m:
                    unit_hi(X2_NORM, h2T_hi, m - 1)
            step(last["kx"])
            unit_hi(X2_NORM, h2T_hi, 3)
            split_hi(2 * at["vx"] + 2)
            split_hi(2 * at["vx"] + 3)
            act.wait_ge(ev_dve, evac_count(last["mix"]))
            for half in range(2):
                for t in range(TT):
                    row_squares(X2_NORM, xres, t, half)
            evacuate(at["vx"])
            step(at["qx"])
            step(last["qx"])

            def xexponentials(h):
                act.wait_ge(xs_max, 2 * h + 2)
                for tt in range(TT):
                    act.activation(xprob[:, h, tt], XS_BANKS[h][:, tt * T:(tt + 1) * T], ACT.Exp,
                                   scale=xscale[:, tt:tt + 1], bias=xnmax[:, h, tt:tt + 1],
                                   accum_out=xsum[:, h, tt:tt + 1]).then_inc(xs_exp, 1)

            xexponentials(0)
            split_hi(2 * V1 + 2)
            xexponentials(1)
            split_hi(2 * V1 + 3)
            xexponentials(2)
            xexponentials(3)
            evacuate(V1)

            def ox_out_hi(h):
                act.wait_ge(xpv_ps, h + 1)
                act.activation(oxT_hi[:, h], PO[h % 2][:, 0:T], ACT.Copy).then_inc(ox_hi, 1)

            for h in range(XH):
                if h % 2 == 0:
                    act.wait_ge(xpt_ps, h + 1)
                    if h:
                        act.wait_ge(xpv_ps, h - 1)
                    act.activation(xpT[:, 0], PT[0][:], ACT.Copy).then_inc(xpt_act, 1)
                if h:
                    ox_out_hi(h - 1)
            ox_out_hi(XH - 1)
            split_hi(2 * V1 + 4)
            split_hi(2 * V1 + 5)

            def h3_out(u):
                act.wait_ge(nt_ps, 4 * X3_NORM + u + 1)
                act.activation(h3T[:, 2 * u:2 * u + 2], NT_BANKS3[u][:].rearrange("p (k q) -> p k q", k=2),
                               ACT.Copy).then_inc(h3_act, 1)

            h3_out(0)
            act.wait_ge(ev_dve, evac_count(NC - 1) - 2)
            for t in range(TT):
                row_squares(X3_NORM, xres, t, 0)
            h3_out(2)
            act.wait_ge(ev_dve, evac_count(NC - 1))
            for t in range(TT):
                row_squares(X3_NORM, xres, t, 1)

            for t in range(TT):
                act.wait_ge(r_top, t + 1)
                act.activation(g_exp[:, t], g_log[:, t, 0:NG], ACT.Exp, bias=g_neg[:, t:t + 1],
                               accum_out=g_sum[:, t:t + 1]).then_inc(r_exp, 1)
            for t in range(TT):
                act.wait_ge(r_top, TT + t + 1)
                act.activation(e2[:, t:t + 1], e_top[:, t, 1:2], ACT.Exp, bias=e_neg[:, t:t + 1]).then_inc(r_exp, 1)
            act.wait_ge(trips_set, 1)
            total = act.value_load(trips[0:1, 0:1], min_val=BODIES, max_val=BODIES * ROUNDS)
            with act.Fori(0, total) as body:
                for q in range(BODY_QUADS):
                    n = body * BODY_QUADS + q
                    act.wait_ge(chunk_used, n * MOE_CHUNKS + GU_CHUNKS)
                    act.activation(silu_g[:], PJ[0][:, 0:FE], ACT.Silu).then_inc(silu_done, 1)
                    act.wait_ge(hidT_ps, n + 1)
                    act.activation(hidT[:], HID_T.rearrange("p (k s) -> p k s", k=KF), ACT.Copy)\
                        .then_inc(hidT_sb, 1)
                    act.wait_ge(chunk_used, n * MOE_CHUNKS + GU_CHUNKS + KF)
                    act.activation(y_sb[:, 0:512], SC[0][:], ACT.Copy).then_inc(y_act, 1)
            for half in range(2):
                for t in range(TT):
                    act.wait_ge(back_ps[t][half], total * BODY_QUADS)
                    squares(4, ACC[t][half][:], t, half, xres)
            for t in range(TT):
                act.wait_ge(fin_xg, t + 1)
                act.wait_ge(rs_done, 2 * 4 + t + 1)
                act.activation(xres[:, t, 0:512], moe_x[:, 4 * t:4 * t + 4].rearrange("p k s -> p (k s)"), ACT.Copy,
                               scale=rnorm[:, 4, t:t + 1]).then_inc(fin_act, 1)

        @block.vector
        def _(dve):
            def means(n, t):
                dve.wait_ge(sq_done, sq_count(n, t))
                dve.tensor_scalar(mean_eps[:, n, t:t + 1], mean_sq[:, n, t, 0:1], mean_sq[:, n, t, 1:2], EPS,
                                  ALU.add, ALU.add).then_inc(ms_done, 1)

            def normalise(n, src, tiles=range(TT)):
                for t in range(TT):
                    means(n, t)
                for t in tiles:
                    dve.wait_ge(rs_done, 2 * n + t + 1)
                    dve.tensor_scalar(xn[:, t], src[:, t], rnorm[:, n, t:t + 1], None, ALU.mult).then_inc(xn_done, 1)

            def unit_lo(n, hi, lo, u):
                dve.wait_ge(nt_hi, 4 * n + u + 1)
                for i in range(2):
                    k = 2 * u + i
                    op = dve.scalar_tensor_tensor(out=lo[:, k], in0=NT_BANKS[u][:, i * T:(i + 1) * T],
                                                  scalar=gains[:, n, k:k + 1], in1=hi[:, k].bitcast(F32),
                                                  op0=ALU.mult, op1=ALU.subtract)
                op.then_inc(nt_lo, 1)

            def split_lo(g):
                if g >= NH:
                    return
                dve.wait_ge(hi_done, g + 1)
                dve.tensor_tensor(w_lo[:, g % NS], w_raw[:, g % NW], w_hi[:, g % NS].bitcast(F32), ALU.subtract)\
                    .then_inc(lo_done, 1)

            def bias_and_max(j):
                b, swa = j % 2, j >= PAIRS
                dve.wait_ge(s_ps, j + 1)
                if j >= 2:
                    dve.wait_ge(pt_ps, j - 1)
                for hh in range(2):
                    h = 2 * (j % PAIRS) + hh
                    dve.scalar_tensor_tensor(out=scores[:, b, hh], in0=dist[:, int(swa)], scalar=2.0 ** -(h + 1),
                                             in1=SC[hh][:, 0:SK], op0=ALU.mult, op1=ALU.add).then_inc(s_bias, 1)
                dve.wait_ge(s_bias, 2 * j + 2)
                for tt in range(TT):
                    cols = slice(0, P) if tt == 0 else slice(P, SK)
                    dve.tensor_reduce(nmax[:, b, tt], scores[:, b, :, cols], axis=AX.X, op=ALU.max,
                                      negate=True).then_inc(s_max, 1)
                if swa:
                    h = 2 * (j % PAIRS)
                    count = s_max_count(j)
                    dve.wait_ge(s_max, count - 2)
                    dve.tensor_tensor(nmax[:, b], nmax[:, b], nsinks[:, h:h + 2].unsqueeze(1).broadcast_to([P, 2, 2]),
                                      ALU.min).then_inc(s_max, 1)
                    dve.wait_ge(s_max, count - 1)
                    dve.tensor_tensor(sink_arg[:, b].rearrange("p (t h) -> p t h", t=2), nmax[:, b],
                                      sinks[:, h:h + 2].unsqueeze(1).broadcast_to([P, 2, 2]), ALU.add)\
                        .then_inc(s_max, 1)

            sunk = [0]

            def inverse_sums(j):
                b = j % 2
                dve.wait_ge(s_exp, s_exp_count(j))
                if j >= PAIRS:
                    dve.tensor_tensor(rsum[:, b], rsum[:, b], sink_exp[:, b], ALU.add).then_inc(c_sink, 1)
                    sunk[0] += 1
                    dve.wait_ge(c_sink, 1 + sunk[0])
                dve.reciprocal(rinv[:, b], rsum[:, b]).then_inc(s_inv, 1)

            def mix_out_lo(j):
                dve.wait_ge(mix_hi, j + 1)
                dve.tensor_tensor(mixT_lo[:, j], PO[j % 2][:, 0:T], mixT_hi[:, j].bitcast(F32), ALU.subtract)\
                    .then_inc(mix_lo, 1)

            normalise(0, xres, [1])
            dve.wait_ge(c_gain_ps, 1)
            dve.tensor_copy(gains[:], PO[0][:, 0:4 * KD].rearrange("p (n k) -> p n k", n=4)).then_inc(c_gain, 1)
            split_lo(0)
            dve.wait_ge(c_gain, 1)
            unit_lo(0, hT_hi, hT_lo, 0)
            unit_lo(0, hT_hi, hT_lo, 1)
            split_lo(1)
            unit_lo(0, hT_hi, hT_lo, 2)
            unit_lo(0, hT_hi, hT_lo, 3)
            dve.wait_ge(c_sink_ps, 1)
            dve.tensor_copy(sinks[:], PO[1][:, 0:HEADS]).then_inc(c_sink, 1)
            dve.tensor_scalar(nsinks[:], PO[1][:, 0:HEADS], -1.0, None, ALU.mult).then_inc(c_gain, 1)
            dve.tensor_copy(br_all[:], PO[1][:, HEADS:HEADS + NG + NE]).then_inc(c_gain, 1)
            dve.wait_ge(c_sink, 1)
            dve.wait_ge(c_gain, 3)
            for c in range(FIRST_UNDER):
                split_lo(2 * c + 2)
                split_lo(2 * c + 3)
                if c == 1:
                    normalise(MEM_NORM, mem_raw)
            dve.wait_ge(c_misc, 15)
            for i in range(STEPS):
                c = FIRST_UNDER + i
                if i < UNITS:
                    bias_and_max(i)
                split_lo(2 * c + 2)
                if i < UNITS:
                    inverse_sums(i)
                split_lo(2 * c + 3)
                if 2 <= i <= UNITS + 1:
                    mix_out_lo(i - 2)
            for u in range(4):
                unit_lo(MEM_NORM, memT_hi, memT_lo, u)
            def merged_lo(m):
                dve.wait_ge(mg_hi, m + 1)
                dve.tensor_tensor(mgT_lo[:, 2 * m:2 * m + 2], gates[:, 2 * m:2 * m + 2],
                                  mgT_hi[:, 2 * m:2 * m + 2].bitcast(F32), ALU.subtract).then_inc(mg_lo, 1)

            for m in range(4):
                c = at["merge"] + m
                split_lo(2 * c + 2)
                ga, gb = gates[:, 2 * m:2 * m + 2], gates[:, KD + 2 * m:KD + 2 * m + 2]
                dve.wait_ge(half_done, 2 * c + 1)
                dve.wait_ge(sig_done, 2 * m + 2)
                dve.tensor_tensor(ga, ga, PJ[c % 2][:].rearrange("p (a n) -> p a n", a=2), ALU.mult)\
                    .then_inc(mg_part, 1)
                if m:
                    merged_lo(m - 1)
                split_lo(2 * c + 3)
                dve.wait_ge(half_done, 2 * c + 2)
                dve.tensor_tensor(gb, gb, PT[c % 2][:].rearrange("p (a n) -> p a n", a=2), ALU.mult)\
                    .then_inc(ev_dve, 1)
                dve.wait_ge(mg_part, m + 1)
                dve.wait_ge(ev_dve, evac_count(c))
                dve.tensor_tensor(ga, ga, gb, ALU.add).then_inc(mg_sum, 1)
            def add_residual(src, col):
                dst = xres[:, :, col:col + CW]
                dve.tensor_tensor(dst, dst, src[:].rearrange("p (t n) -> p t n", t=TT), ALU.add).then_inc(ev_dve, 1)

            def step(c):
                split_lo(2 * c + 2)
                split_lo(2 * c + 3)

            split_lo(2 * at["kx"] + 2)
            merged_lo(3)
            split_lo(2 * at["kx"] + 3)
            for c in range(at["mix"], last["mix"] + 1):
                step(c)
                dve.wait_ge(half_done, 2 * c + 2)
                add_residual(PJ[c % 2], (c - at["mix"]) * CW)
                if c > at["mix"]:
                    unit_lo(X2_NORM, h2T_hi, h2T_lo, c - at["mix"] - 1)
            step(last["kx"])
            unit_lo(X2_NORM, h2T_hi, h2T_lo, 3)
            step(at["vx"])
            for t in range(TT):
                means(X2_NORM, t)
            step(at["qx"])
            dve.wait_ge(rs_done, 2 * (X2_NORM + 1))
            dve.tensor_scalar(xscale[:], rnorm[:, X2_NORM], XSCALE, None, ALU.mult).then_inc(xscale_set, 1)
            step(last["qx"])
            dve.wait_ge(xscale_set, 1)

            def x_maxima(h):
                dve.wait_ge(xs_ps, h + 1)
                dve.tensor_reduce(xmax[:, h], XS_BANKS[h][:].rearrange("p (t m) -> p t m", t=TT), axis=AX.X,
                                  op=ALU.max).then_inc(xs_max, 1)
                dve.wait_ge(xs_max, 2 * h + 1)
                dve.scalar_tensor_tensor(out=xnmax[:, h], in0=xmax[:, h], scalar=-1.0, in1=xscale[:], op0=ALU.mult,
                                         op1=ALU.mult).then_inc(xs_max, 1)

            def x_inverse_sums(h):
                dve.wait_ge(xs_exp, 2 * h + 2)
                dve.reciprocal(xinv[:, h], xsum[:, h]).then_inc(xs_inv, 1)

            x_maxima(0)
            x_maxima(1)
            split_lo(2 * V1 + 2)
            x_maxima(2)
            x_inverse_sums(0)
            x_maxima(3)
            x_inverse_sums(1)
            split_lo(2 * V1 + 3)
            x_inverse_sums(2)
            x_inverse_sums(3)

            def ox_out_lo(h):
                dve.wait_ge(ox_hi, h + 1)
                dve.tensor_tensor(oxT_lo[:, h], PO[h % 2][:, 0:T], oxT_hi[:, h].bitcast(F32), ALU.subtract)\
                    .then_inc(ox_lo, 1)

            for h in range(XH):
                if h % 2:
                    dve.wait_ge(xpt_ps, h + 1)
                    if h > 1:
                        dve.wait_ge(xpv_ps, h - 1)
                    dve.tensor_copy(xpT[:, 1], PT[1][:]).then_inc(xpt_dve, 1)
                    ox_out_lo(h - 1)
                elif h:
                    ox_out_lo(h - 1)
            ox_out_lo(XH - 1)
            split_lo(2 * V1 + 4)
            split_lo(2 * V1 + 5)

            def h3_out(u):
                dve.wait_ge(nt_ps, 4 * X3_NORM + u + 1)
                dve.tensor_copy(h3T[:, 2 * u:2 * u + 2], NT_BANKS3[u][:].rearrange("p (k q) -> p k q", k=2))\
                    .then_inc(h3_dve, 1)

            for m in range(4):
                c, half = at["xo"] + m // 2, m % 2
                dve.wait_ge(half_done, 2 * c + half + 1)
                add_residual((PT if half else PJ)[c % 2], m * CW)
                if m == 2:
                    h3_out(1)
            h3_out(3)
            for t in range(TT):
                means(X3_NORM, t)

            steps, done = [0], [0] * TT

            def mark(ts, op):
                op.then_inc(r_step, 1)
                steps[0] += 1
                for t in ts:
                    done[t] = steps[0]

            def after(ts):
                dve.wait_ge(r_step, max(done[t] for t in ts))

            both_tiles = range(TT)
            mark(both_tiles, dve.memset(g_log[:], BIG))
            after(both_tiles)
            dve.wait_ge(rs_done, 2 * (X3_NORM + 1))
            dve.wait_ge(logits_ps, 1)
            for t in range(TT):
                mark([t], dve.scalar_tensor_tensor(out=g_log[:, t, 0:NG], in0=LOGIT[:, t * 64:t * 64 + NG],
                                                   scalar=rnorm[:, X3_NORM, t:t + 1], in1=br_all[:, 0:NG],
                                                   op0=ALU.mult, op1=ALU.add))
            for t in range(TT):
                after([t])
                mark([t], dve.max(g_top[:, t], g_log[:, t]))
            for t in range(TT):
                dve.scalar_tensor_tensor(out=logit[:, t], in0=LOGIT[:, t * 64 + NG:t * 64 + NG + NE],
                                         scalar=rnorm[:, X3_NORM, t:t + 1], in1=br_all[:, NG:NG + NE],
                                         op0=ALU.mult, op1=ALU.add)
            for t in range(TT):
                after([t])
                mark([t], dve.max_index(g_idx[:, t], g_top[:, t], g_log[:, t]))
            for t in range(TT):
                dve.tensor_scalar(g_neg[:, t:t + 1], g_top[:, t, 0:1], -1.0, None, ALU.mult).then_inc(r_top, 1)
            after(both_tiles)
            mark(both_tiles, dve.tensor_copy(g_idf[:], g_idx[:]))
            after(both_tiles)
            for t in range(TT):
                mark(both_tiles, dve.tensor_scalar(pen[:, t], iota_e[:, 0:NG], g_idf[:, t, 0:1], BIG,
                                                   ALU.not_equal, ALU.mult))
            after(both_tiles)
            mark(both_tiles, dve.tensor_tensor(e_log[:], logit[:].rearrange("p t (g e) -> p t g e", g=NG),
                                               pen[:].unsqueeze(3).broadcast_to([P, TT, NG, EPG]), ALU.add))
            after(both_tiles)
            for t in range(TT):
                mark([t], dve.max(e_top[:, t], e_log[:, t].rearrange("p g e -> p (g e)")))
            for t in range(TT):
                after([t])
                mark([t], dve.max_index(e_idx[:, t], e_top[:, t], e_log[:, t].rearrange("p g e -> p (g e)")))
            for t in range(TT):
                dve.tensor_scalar(e_neg[:, t:t + 1], e_top[:, t, 0:1], -1.0, None, ALU.mult).then_inc(r_top, 1)
            after(both_tiles)
            mark(both_tiles, dve.tensor_copy(e_idf[:], e_idx[:]))
            after(both_tiles)
            for t in range(TT):
                mark([t], dve.tensor_scalar(first[:, t], iota_e[:], e_idf[:, t, 0:1], None, ALU.is_equal))
            for t in range(TT):
                after([t])
                dve.scalar_tensor_tensor(out=both[:, t], in0=iota_e[:], scalar=e_idf[:, t, 1:2], in1=first[:, t],
                                         op0=ALU.is_equal, op1=ALU.add).then_inc(r_mask, 1)
            dve.wait_ge(r_exp, 2 * TT)
            mark(both_tiles, dve.scalar_tensor_tensor(out=den[:], in0=e2[:], scalar=1.0, in1=g_sum[:], op0=ALU.add,
                                                      op1=ALU.mult))
            after(both_tiles)
            mark(both_tiles, dve.reciprocal(ew[:, 0], den[:]))
            after(both_tiles)
            dve.tensor_tensor(ew[:, 1], ew[:, 0], e2[:], ALU.mult).then_inc(r_ew, 1)
            dve.wait_ge(pos_ps, 1)
            dve.scalar_tensor_tensor(out=posm[:], in0=LISTED[:, 0:TT * NE].rearrange("p (t e) -> p t e", t=TT),
                                     scalar=float(UNLISTED), in1=both[:].bitcast(F32), op0=ALU.add, op1=ALU.mult)\
                .then_inc(r_posm, 1)
            dve.wait_ge(pos_ps, 2)
            mark(both_tiles, dve.tensor_reduce(cmax[:], COUNTS[:, 0:NE], axis=AX.X, op=ALU.max))
            dve.wait_ge(r_posm, 1)
            dve.tensor_scalar(slot_of[:], posm[:], -float(UNLISTED), None, ALU.add).then_inc(r_slots, 1)
            after(both_tiles)
            mark(both_tiles, dve.tensor_scalar(over[:, 0:ROUNDS - 1], iota_rw[:, 1:ROUNDS], cmax[:], float(UNLISTED),
                                               ALU.subtract, ALU.is_lt))
            after(both_tiles)
            mark(both_tiles, dve.tensor_reduce(nover[:], over[:, 0:ROUNDS - 1], axis=AX.X, op=ALU.add))
            after(both_tiles)
            dve.tensor_scalar(trips[:], nover[:], float(BODIES), float(BODIES), ALU.mult, ALU.add).then_inc(trips_set, 1)
            dve.wait_ge(r_slots, 1)

            rnorm_bc = rnorm[:, X3_NORM].unsqueeze(2).unsqueeze(3).broadcast_to([P, TT, QE, WIN])
            iota_s = iota_e[:, 0:WIN].unsqueeze(1).unsqueeze(1).broadcast_to([P, TT, QE, WIN])
            dve.wait_ge(c_gain, 3)

            def one_hots(experts, made):
                dve.tensor_tensor(sel[:], slot_of[:, :, experts].unsqueeze(3).broadcast_to([P, TT, QE, WIN]),
                                  iota_s, ALU.is_equal).then_inc(sel_made, 1)
                dve.wait_ge(sel_made, made + 1)
                dve.tensor_tensor(sel_norm[:], sel[:], rnorm_bc, ALU.mult).then_inc(sel_made, 1)

            one_hots(slice(0, QE), 0)
            dve.wait_ge(trips_set, 1)
            total = dve.value_load(trips[0:1, 0:1], min_val=BODIES, max_val=BODIES * ROUNDS)
            with dve.Fori(0, total) as body:
                for q in range(BODY_QUADS):
                    n = body * BODY_QUADS + q
                    experts = bass.ds((body % BODIES) * (BODY_QUADS * QE) + q * QE, QE)
                    for half in range(2):
                        dve.wait_ge(gather_ps, n * 2 + half + 1)
                        dve.tensor_tensor(moe_x[:, half * 4:half * 4 + 4],
                                          SC[half][:].rearrange("p (k s) -> p k s", k=4),
                                          gains[:, X3_NORM, half * 4:half * 4 + 4].unsqueeze(2)
                                          .broadcast_to([P, 4, P]), ALU.mult).then_inc(moe_x_sb, 1)
                    dve.wait_ge(r_weight, TT)
                    dve.tensor_tensor(selw[:], sel[:], wboth[:, :, experts].unsqueeze(3)
                                      .broadcast_to([P, TT, QE, WIN]), ALU.mult).then_inc(sel_made, 1)
                    dve.tensor_scalar(slot_of[:, :, experts], slot_of[:, :, experts], -float(WIN), None, ALU.add)\
                        .then_inc(slots_moved, 1)
                    dve.wait_ge(slots_moved, n + 1)
                    dve.wait_ge(silu_done, n + 1)
                    dve.tensor_tensor(hid[:], silu_g[:], PJ[0][:, FE:2 * FE], ALU.mult).then_inc(hid_done, 1)
                    dve.wait_ge(selT_ps, n + 1)
                    dve.tensor_copy(selwT[:], SEL_T).then_inc(selT_sb, 1)
                    next_body = (body + (q + 1) // BODY_QUADS) % BODIES
                    one_hots(bass.ds(next_body * (BODY_QUADS * QE) + (q + 1) % BODY_QUADS * QE, QE), n * 3 + 3)
                    dve.wait_ge(chunk_used, n * MOE_CHUNKS + MOE_CHUNKS)
                    dve.tensor_copy(y_sb[:, 512:], SC[1][:]).then_inc(y_dve, 1)

            dve.wait_ge(fin_in, 16)
            for t in range(TT):
                dve.wait_ge(sq_done, sq_count(X3_NORM, TT - 1) + t + 1)
                dve.tensor_tensor(moe_x[:, 4 * t:4 * t + 4].rearrange("p k s -> p (k s)"), ACC[t][0][:],
                                  fin_g[:, 0:512], ALU.mult).then_inc(fin_xg, 1)
            for t in range(TT):
                means(4, t)
            for t in range(TT):
                dve.wait_ge(rs_done, 2 * 4 + t + 1)
                dve.scalar_tensor_tensor(out=xres[:, t, 512:], in0=ACC[t][1][:], scalar=rnorm[:, 4, t:t + 1],
                                         in1=fin_g[:, 512:], op0=ALU.mult, op1=ALU.mult).then_inc(fin_dve, 1)

        @block.tensor
        def _(pe):
            def transpose_unit(banks, src, u, t):
                for i in range(2):
                    k = 2 * u + i
                    op = pe.transpose(banks[u][:, i * T + t * P:i * T + (t + 1) * P], src[:, t, k * P:(k + 1) * P],
                                      ident[:])
                return op

            def transpose_normalised(ready):
                for units in ((0, 1), (2, 3)):
                    for t in range(TT):
                        pe.wait_ge(*ready[t])
                        for u in units:
                            op = transpose_unit(NT_BANKS, xn, u, t)
                            if t == TT - 1:
                                op.then_inc(nt_ps, 1)

            def transpose_residual(banks, u, added_count):
                pe.wait_ge(ev_dve, added_count)
                for t in range(TT):
                    op = transpose_unit(banks, xres, u, t)
                op.then_inc(nt_ps, 1)

            def product(ps, a, b, start, stop):
                pe.matmul(ps, a[0], b[0], start=start, stop=False, skip_group_check=True)
                pe.matmul(ps, a[0], b[1], start=False, stop=False, skip_group_check=True)
                return pe.matmul(ps, a[1], b[0], start=False, stop=stop, skip_group_check=True)

            def half_chunk(g, hi, lo, ready=None, before=0, tiles=1):
                c, h = divmod(g, 2)
                kind, b = kinds[c], g % NS
                own = kind in ("merge", "xo")
                ps = PT[c % 2] if own and h else PJ[c % 2]
                if h == 0 and c >= 2:
                    pe.wait_ge(ev_dve if kinds[c - 2] in ON_DVE else ev_act, evac_count(c - 2))
                if g == 2 * at["merge"] + 1:
                    pe.wait_ge(nt_lo, 4 * MEM_NORM + 2)
                pe.wait_ge(lo_done, g + 1)
                k0 = {"merge": h * HK, "xo": 0}.get(kind, h * HK)
                opens, closes = own or h == 0, own or h == 1
                for k in range(HK):
                    if ready is not None and k % tiles == 0:
                        pe.wait_ge(ready, before + (k0 + k) // tiles + 1)
                    for j in range(2):
                        W = (w_hi[:, b, k], w_lo[:, b, k])
                        wcol = [w[:, j * P:(j + 1) * P] for w in W]
                        X = (hi[:, k0 + k], lo[:, k0 + k])
                        xcol = [v[:, j * P:(j + 1) * P] for v in X]
                        start, stop = opens and k == 0 and j == 0, closes and k == HK - 1
                        if kind in ("va", "vx", "mix", "xo"):
                            op = product(ps[:, j * T:(j + 1) * T], xcol, W, start, stop)
                        elif kind == "kvb" and j == 1:
                            for t in range(TT):
                                op = product(ps[:, T + t * P:T + (t + 1) * P], [v[:, t * P:(t + 1) * P] for v in X],
                                             wcol, start, stop)
                        else:
                            op = product(ps[:, j * T:(j + 1) * T], wcol, X, start, stop)
                op.then_inc(half_done, 1)

            def pair_scores(j):
                swa, i = divmod(j, PAIRS)
                pe.wait_ge(ev_act, evac_count(at["kvb"] if swa else at["ka"] + i // 2))
                if j:
                    pe.wait_ge(s_bias, 2 * j)
                q = qb if swa else qa
                for tt in range(TT):
                    for hh in range(2):
                        rows = slice(hh * HD, (hh + 1) * HD)
                        keys = kb2[rows, (2 * i + hh) // 4] if swa else ka[rows, i]
                        if tt == 0:
                            op = pe.matmul(SC[hh][:, 0:P], q[rows, i, 0:P], keys[:, 0:P], start=True, stop=True)
                        else:
                            op = pe.matmul(SC[hh][:, P:SK], q[rows, i, P:T], keys, start=True, stop=True)
                op.then_inc(s_ps, 1)

            def pair_transposes(j):
                pe.wait_ge(s_norm, 4 * (j + 1))
                if j:
                    pe.wait_ge(pt_sb, 2 * j)
                for hh in range(2):
                    for i in range(3):
                        cols = slice(i * P, (i + 1) * P)
                        op = pe.transpose(PT[hh][:, cols], scores[:, j % 2, hh, cols], ident[:])
                op.then_inc(pt_ps, 1)

            def pair_values(j):
                swa, i = divmod(j, PAIRS)
                pe.wait_ge(ev_act, evac_count(at["kvb"] if swa else at["va"] + i // 2))
                pe.wait_ge(pt_sb, 2 * j + 2)
                if j >= 2:
                    pe.wait_ge(mix_lo, j - 1)
                for tt, kt, cols in ((0, 0, slice(0, P)), (1, 0, slice(P, 2 * P)), (1, 1, slice(2 * P, SK))):
                    for hh in range(2):
                        h = 2 * i + hh
                        v = vb[:, kt, (h // 4) * HD:(h // 4 + 1) * HD] if swa else va[:, kt, h * HD:(h + 1) * HD]
                        op = pe.matmul(PO[j % 2][hh * HD:(hh + 1) * HD, tt * P:(tt + 1) * P], v, probT[:, hh, cols],
                                       start=kt == 0, stop=kt == tt)
                op.then_inc(pv_ps, 1)

            pe.wait_ge(c_ident, 1)
            pe.wait_ge(gain_in, 64)
            pe.transpose(PO[0][:, 0:4 * KD], g_rows[:], ident[0:4 * KD, 0:4 * KD]).then_inc(c_gain_ps, 1)
            transpose_normalised(((x0n_done, 1), (xn_done, 1)))
            pe.wait_ge(c_ones, 1)
            pe.wait_ge(small_in, 48)
            pe.matmul(PO[1][:, 0:HEADS], ones[0:1, :], sink_row[:], start=True, stop=True)
            pe.matmul(PO[1][:, HEADS:HEADS + NG + NE], ones[0:1, :], br[:], start=True, stop=True)\
                .then_inc(c_sink_ps, 1)
            for g in range(2 * FIRST_UNDER):
                if g < 2:
                    half_chunk(g, hT_hi, hT_lo, nt_lo, 0, 2)
                else:
                    half_chunk(g, hT_hi, hT_lo)
            pe.wait_ge(c_gain, 3)
            pe.wait_ge(c_sink, 1)
            for i in range(STEPS):
                c = FIRST_UNDER + i
                if i < UNITS:
                    pair_scores(i)
                half_chunk(2 * c, hT_hi, hT_lo)
                half_chunk(2 * c + 1, hT_hi, hT_lo)
                if 1 <= i <= UNITS:
                    pair_transposes(i - 1)
                if 2 <= i <= UNITS + 1:
                    pair_values(i - 2)
            transpose_normalised(((xn_done, 2), (xn_done, 3)))

            def chunk(c, hi, lo, *ready):
                half_chunk(2 * c, hi, lo, *ready)
                half_chunk(2 * c + 1, hi, lo, *ready)

            chunk(at["merge"], mixT_hi, mixT_lo, mix_lo, 0, 1)
            for c in range(at["merge"] + 1, last["merge"] + 1):
                chunk(c, mixT_hi, mixT_lo)
            chunk(at["kx"], memT_hi, memT_lo)
            for m in range(4):
                chunk(at["mix"] + m, mgT_hi, mgT_lo, mg_lo, 0, 2)
                if m:
                    transpose_residual(NT_BANKS, m - 1, evac_count(at["mix"] + m - 1))
            chunk(last["kx"], memT_hi, memT_lo)
            transpose_residual(NT_BANKS, 3, evac_count(last["mix"]))
            chunk(at["vx"], memT_hi, memT_lo)
            chunk(at["qx"], h2T_hi, h2T_lo, nt_lo, 4 * X2_NORM, 2)
            chunk(last["qx"], h2T_hi, h2T_lo)

            def x_scores(h):
                pe.wait_ge(ev_act, evac_count((at["qx"], last["qx"])[h // 2]))
                for tt in range(TT):
                    op = pe.matmul(XS_BANKS[h][:, tt * T:(tt + 1) * T], qx[:, h, tt * P:(tt + 1) * P], kx[:, h],
                                   start=True, stop=True)
                op.then_inc(xs_ps, 1)

            x_scores(0)
            x_scores(1)
            half_chunk(2 * V1, memT_hi, memT_lo)
            x_scores(2)
            x_scores(3)
            half_chunk(2 * V1 + 1, memT_hi, memT_lo)

            def x_transposes(h):
                pe.wait_ge(xs_norm, 2 * h + 2)
                for mt in range(2):
                    for tt in range(TT):
                        op = pe.transpose(PT[h % 2][:, mt * T + tt * P:mt * T + (tt + 1) * P],
                                          xprob[:, h, tt, mt * P:(mt + 1) * P], ident[:])
                op.then_inc(xpt_ps, 1)

            def x_values(h):
                pe.wait_ge((xpt_act, xpt_dve)[h % 2], h // 2 + 1)
                if h >= 2:
                    pe.wait_ge(ox_lo, h - 1)
                for mt in range(2):
                    op = pe.matmul(PO[h % 2][:, 0:T], vx[:, mt, h * P:(h + 1) * P], xpT[:, h % 2, mt * T:(mt + 1) * T],
                                   start=mt == 0, stop=mt == 1)
                op.then_inc(xpv_ps, 1)

            x_transposes(0)
            for h in range(XH):
                if h + 1 < XH:
                    x_transposes(h + 1)
                if h == 0:
                    pe.wait_ge(ev_act, evac_count(last["vx"]))
                x_values(h)
            X = 2 * at["xo"]
            half_chunk(X, oxT_hi, oxT_lo, ox_lo, 0, 1)
            half_chunk(X + 1, oxT_hi, oxT_lo)
            half_chunk(X + 2, oxT_hi, oxT_lo)
            transpose_residual(NT_BANKS3, 0, evac_count(NC - 1) - 3)
            transpose_residual(NT_BANKS3, 1, evac_count(NC - 1) - 2)
            half_chunk(X + 3, oxT_hi, oxT_lo)
            transpose_residual(NT_BANKS3, 2, evac_count(NC - 1) - 1)

            def logits(ks):
                for k in ks:
                    for t in range(TT):
                        op = pe.matmul(LOGIT[:, t * 64:t * 64 + NG + NE], h3T[:, k, t * P:(t + 1) * P], wrg[:, k],
                                       start=k == 0 and t == 0, stop=k == KD - 1, skip_group_check=True)
                return op

            pe.wait_ge(h3_act, 1)
            logits((0, 1))
            transpose_residual(NT_BANKS3, 3, evac_count(NC - 1))
            pe.wait_ge(h3_dve, 1)
            logits((2, 3))
            pe.wait_ge(h3_act, 2)
            logits((4, 5))
            pe.wait_ge(h3_dve, 2)
            logits((6, 7)).then_inc(logits_ps, 1)
            def copy_residual(half):
                for t in range(TT):
                    pe.matmul(ACC[t][half][:], ident[:], xres[:, t, half * 512:(half + 1) * 512], start=True,
                              stop=True)

            copy_residual(0)
            pe.wait_ge(c_misc, 17)
            pe.wait_ge(r_mask, 2)
            flat = both[:].rearrange("p t e -> p (t e)")
            pe.matmul(LISTED[:, 0:2 * NE], below_r[:], flat, start=True, stop=False, skip_group_check=True)
            pe.matmul(LISTED[:, NE:2 * NE], ones_r[:], both[:, 0], start=False, stop=True, skip_group_check=True)\
                .then_inc(pos_ps, 1)
            pe.matmul(COUNTS[:, 0:NE], ones_r[:], both[:, 0], start=True, stop=False)
            pe.matmul(COUNTS[:, 0:NE], ones_r[:], both[:, 1], start=False, stop=True).then_inc(pos_ps, 1)
            copy_residual(1)

            pe.wait_ge(trips_set, 1)
            total = pe.value_load(trips[0:1, 0:1], min_val=BODIES, max_val=BODIES * ROUNDS)
            with pe.Fori(0, total) as body:
                for q in range(BODY_QUADS):
                    n = body * BODY_QUADS + q
                    pe.wait_ge(sel_made, n * 3 + 2)
                    for k in range(KD):
                        for t in range(TT):
                            op = pe.matmul(SC[k // 4][:, (k % 4) * P:(k % 4 + 1) * P], xres[:, t, k * P:(k + 1) * P],
                                           sel_norm[:, t].rearrange("p e s -> p (e s)"), start=t == 0, stop=t == TT - 1)
                        if k % 4 == 3:
                            op.then_inc(gather_ps, 1)
                    for k in range(KD):
                        i = q * MOE_CHUNKS + k
                        if k % 4 == 0:
                            pe.wait_ge(moe_x_sb, n * 2 + k // 4 + 1)
                        pe.wait_ge(moe_in[slot_of_chunk(i)], landed(i, body))
                        for e in range(QE):
                            op = pe.matmul(PJ[0][e * WIN:(e + 1) * WIN, :], moe_x[:, k, e * WIN:(e + 1) * WIN],
                                           slots[slot_of_chunk(i)][:, e * 512:(e + 1) * 512],
                                           start=k == 0, stop=k == KD - 1)
                        op.then_inc(chunk_used, 1)
                    pe.wait_ge(sel_made, n * 3 + 3)
                    for t in range(TT):
                        op = pe.transpose(SEL_T[:, t * P:(t + 1) * P], selw[:, t].rearrange("p e s -> p (e s)"),
                                          ident[:])
                    op.then_inc(selT_ps, 1)
                    pe.wait_ge(hid_done, n + 1)
                    for k in range(KF):
                        op = pe.transpose(HID_T[:, k * P:(k + 1) * P], hid[:, k * P:(k + 1) * P], ident[:])
                    op.then_inc(hidT_ps, 1)

                    def down(half, kt):
                        i = q * MOE_CHUNKS + GU_CHUNKS + 2 * half + kt
                        pe.wait_ge(moe_in[slot_of_chunk(i)], landed(i, body))
                        for e in range(QE):
                            op = pe.matmul(SC[half][e * WIN:(e + 1) * WIN, :], hidT[:, kt, e * WIN:(e + 1) * WIN],
                                           slots[slot_of_chunk(i)][:, e * 512:(e + 1) * 512],
                                           start=kt == 0, stop=kt == KF - 1)
                        op.then_inc(chunk_used, 1)

                    def back_to_tokens(t, half):
                        pe.matmul(ACC[t][half][:], selwT[:, t * P:(t + 1) * P],
                                  y_sb[:, half * 512:(half + 1) * 512], start=False, stop=True,
                                  skip_group_check=True).then_inc(back_ps[t][half], 1)

                    pe.wait_ge(hidT_sb, n + 1)
                    down(0, 0)
                    down(0, 1)
                    pe.wait_ge(selT_sb, n + 1)
                    down(1, 0)
                    pe.wait_ge(y_act, n + 1)
                    back_to_tokens(0, 0)
                    down(1, 1)
                    back_to_tokens(1, 0)
                    pe.wait_ge(y_dve, n + 1)
                    for t in range(TT):
                        back_to_tokens(t, 1)


_INS = ["x", "mem", "mix_norm_g", "w_in", "moba_out_w", "swa_out_w", "swa_sinks", "mix_out_w", "xattn_norm_g",
        "mem_norm_g", "xattn_wq", "xattn_wkv", "xattn_wo", "ffn_norm_g", "router_group_w", "router_group_b",
        "router_expert_w", "router_expert_b", "expert_w_gate", "expert_w_up", "expert_w_down", "final_norm_g"]
_OUTS = [((1, 256, 1024), "float32")]


def kernel(**inputs):
    import numpy as _np
    import concourse.bacc as _bacc
    from concourse import mybir as _mybir
    from concourse.bass_utils import run_bass_kernel_spmd as _run

    nc = _bacc.Bacc("TRN2", target_bir_lowering=False, num_devices=1)
    arrays, args = {}, []
    for name in _INS:
        a = _np.ascontiguousarray(inputs[name])
        arrays[f"in_{name}_dram"] = a
        args.append(nc.dram_tensor(f"in_{name}_dram", a.shape, _mybir.dt.from_np(a.dtype), kind="ExternalInput").ap())
    for i, (shape, dtype) in enumerate(_OUTS):
        dt = _mybir.dt.from_np(_np.dtype(dtype))
        args.append(nc.dram_tensor(f"out_{i}_dram", shape, dt, kind="ExternalOutput").ap())
    hybrid_layer(nc, *args)
    r = _run(nc, [arrays], core_ids=[0])
    got = tuple(r.results[0][f"out_{i}_dram"] for i in range(len(_OUTS)))
    return got[0]
```
